# Optimizing a Trainium2 kernel written in Bass

```python
import jax
import jax.numpy as jnp
from jax import lax
import numpy as np

D_MODEL = 1024
BATCH = 1
SEQ = 512
DEPTH = 1

DSA_PATTERNS = ((128, 1), (512, 4), (2048, 16))
DSA_GROUPS = 3
DSA_HEADS = 8
DSA_HEAD_DIM = 64
DSA_WIDTH = DSA_HEADS * DSA_HEAD_DIM
DSA_BLOCK = 128
ROPE_THETA = 10000.0

GDN_HEADS = 8
GDN_KEY_DIM = 64
GDN_VAL_DIM = 64
GDN_K_WIDTH = GDN_HEADS * GDN_KEY_DIM
GDN_V_WIDTH = GDN_HEADS * GDN_VAL_DIM
GDN_CONV = 4
GDN_CHUNK = 64

NORM_EPS = 1e-6

IN_SIZES = (
    DSA_GROUPS * 3 * DSA_WIDTH,
    DSA_WIDTH,
    2 * GDN_K_WIDTH + GDN_V_WIDTH,
    GDN_V_WIDTH,
    GDN_HEADS,
    GDN_HEADS,
    D_MODEL,
    D_MODEL,
)
IN_WIDTH = sum(IN_SIZES)


def _rmsnorm(x, w):
    xf = x.astype(jnp.float32)
    y = xf * lax.rsqrt(jnp.mean(xf * xf, axis=-1, keepdims=True) + NORM_EPS)
    return (y * w.astype(jnp.float32)).astype(x.dtype)

def _l2norm(t):
    return t * lax.rsqrt(jnp.sum(t * t, axis=-1, keepdims=True) + NORM_EPS)

def _split_columns(h):
    parts, start = [], 0
    for size in IN_SIZES:
        parts.append(h[..., start:start + size])
        start += size
    return parts

def _rope_tables(seq, dim):
    inv_freq = ROPE_THETA ** (-jnp.arange(0, dim, 2, dtype=jnp.float32) / dim)
    ang = jnp.arange(seq, dtype=jnp.float32)[:, None] * inv_freq[None, :]
    ang = jnp.concatenate([ang, ang], axis=-1)
    return jnp.cos(ang), jnp.sin(ang)

def _apply_rope(t, cos, sin):
    half = t.shape[-1] // 2
    rot = jnp.concatenate([-t[..., half:], t[..., :half]], axis=-1)
    return t * cos[:, None, None, :] + rot * sin[:, None, None, :]

def _dilated_window_attention(q, k, v, window, dilation):
    b, s, h, dh = q.shape
    n_back = window // dilation
    sub_len = s // dilation
    n_blk = -(-sub_len // DSA_BLOCK)
    pad = n_blk * DSA_BLOCK - sub_len

    def to_blocks(t):
        t = t.reshape(b, sub_len, dilation, h, dh).transpose(0, 2, 1, 3, 4)
        t = jnp.pad(t, ((0, 0), (0, 0), (0, pad), (0, 0), (0, 0)))
        return t.reshape(b, dilation, n_blk, DSA_BLOCK, h, dh)

    def with_previous_block(t):
        prev = jnp.pad(t, ((0, 0), (0, 0), (1, 0), (0, 0), (0, 0), (0, 0)))[:, :, :-1]
        return jnp.concatenate([prev, t], axis=3)

    qb = to_blocks(q)
    kb = with_previous_block(to_blocks(k))
    vb = with_previous_block(to_blocks(v))
    scores = jnp.einsum('brnqhd,brnkhd->brnhqk', qb, kb) * (dh ** -0.5)
    qi = jnp.arange(DSA_BLOCK)[:, None]
    kj = jnp.arange(2 * DSA_BLOCK)[None, :]
    dist = qi + DSA_BLOCK - kj
    key_idx = jnp.arange(n_blk)[:, None, None] * DSA_BLOCK + kj - DSA_BLOCK
    valid = (dist >= 0) & (dist <= n_back) & (key_idx >= 0)
    scores = jnp.where(valid[:, None], scores, -jnp.inf)
    m = jnp.max(scores, axis=-1, keepdims=True)
    p = jnp.exp(scores - m)
    den = jnp.sum(p, axis=-1, keepdims=True)
    o = jnp.einsum('brnhqk,brnkhd->brnqhd', p / den, vb)
    lse = (m + jnp.log(den))[..., 0].transpose(0, 1, 2, 4, 3)

    def from_blocks(t):
        t = t.reshape(b, dilation, n_blk * DSA_BLOCK, *t.shape[4:])[:, :, :sub_len]
        t = jnp.moveaxis(t, 1, 2)
        return t.reshape(b, s, *t.shape[3:])

    return from_blocks(o), from_blocks(lse)

def _dilated_mixture(q, k, v):
    outs, lses = [], []
    for g, (window, dilation) in enumerate(DSA_PATTERNS):
        o, lse = _dilated_window_attention(q[:, :, g], k[:, :, g], v[:, :, g], window, dilation)
        outs.append(o)
        lses.append(lse)
    wts = jax.nn.softmax(jnp.stack(lses), axis=0)
    o = jnp.einsum('gbsh,gbshd->bshd', wts, jnp.stack(outs))
    return o.reshape(o.shape[0], o.shape[1], -1)

def _causal_depthwise_conv(x, w):
    k, c = w.shape
    return lax.conv_general_dilated(
        x, w[:, None, :].astype(x.dtype), window_strides=(1,), padding=((k - 1, 0),),
        dimension_numbers=('NWC', 'WIO', 'NWC'), feature_group_count=c)

def _gated_delta_rule(q, k, v, g, beta):
    b, s, h, dk = q.shape
    dv = v.shape[-1]
    c = GDN_CHUNK
    n = s // c

    def chunk(t):
        return t.reshape(b, n, c, h, -1).transpose(0, 3, 1, 2, 4)

    qc, kc, vc = chunk(q), chunk(k), chunk(v)
    gc = g.reshape(b, n, c, h).transpose(0, 3, 1, 2)
    bc = beta.reshape(b, n, c, h).transpose(0, 3, 1, 2)
    G = jnp.cumsum(gc, axis=-1)
    causal = jnp.tril(jnp.ones((c, c), dtype=bool))
    strict = jnp.tril(jnp.ones((c, c), dtype=bool), k=-1)
    decay_incl = jnp.exp(jnp.where(causal, G[..., :, None] - G[..., None, :], -jnp.inf))
    decay_strict = jnp.where(strict, decay_incl, 0.0)
    k_beta = kc * bc[..., None]
    a = jnp.einsum('bhnid,bhnjd->bhnij', k_beta, kc) * decay_strict
    eye = jnp.eye(c, dtype=a.dtype)
    t_inv = lax.linalg.triangular_solve(eye + a, jnp.broadcast_to(eye, a.shape),
                                        left_side=True, lower=True, unit_diagonal=True)
    u = t_inv @ (vc * bc[..., None])
    w = t_inv @ (k_beta * jnp.exp(G)[..., None])
    attn = jnp.einsum('bhnid,bhnjd->bhnij', qc, kc) * decay_incl
    q_dec = qc * jnp.exp(G)[..., None]
    g_last = G[..., -1:]
    k_dec = kc * jnp.exp(g_last - G)[..., None]
    chunk_decay = jnp.exp(g_last[..., 0])
    xs = tuple(jnp.moveaxis(t, 2, 0) for t in (q_dec, attn, u, w, k_dec, chunk_decay))

    def step(state, inp):
        q_e, at, u_c, w_c, k_d, dec = inp
        v_new = u_c - jnp.einsum('bhck,bhkv->bhcv', w_c, state)
        o = jnp.einsum('bhck,bhkv->bhcv', q_e, state) + jnp.einsum('bhij,bhjv->bhiv', at, v_new)
        state = state * dec[..., None, None] + jnp.einsum('bhck,bhcv->bhkv', k_d, v_new)
        return state, o

    state0 = jnp.zeros((b, h, dk, dv), dtype=q.dtype)
    _, o = lax.scan(step, state0, xs)
    return o.transpose(1, 0, 3, 2, 4).reshape(b, s, h, dv)

def first_inputs(seed: int = 0) -> dict:
    key = jax.random.key(seed)
    ks = jax.random.split(key, 12)
    f32 = jnp.float32
    x = jax.random.normal(ks[0], (BATCH, SEQ, D_MODEL), f32)
    norm_w = 1.0 + 0.05 * jax.random.normal(ks[1], (DEPTH, D_MODEL), f32)
    w_in = jax.random.normal(ks[2], (DEPTH, D_MODEL, IN_WIDTH), f32) * D_MODEL ** -0.5
    conv_w = jax.random.normal(ks[3], (DEPTH, GDN_CONV, 2 * GDN_K_WIDTH + GDN_V_WIDTH), f32) * GDN_CONV ** -0.5
    a_log = jnp.log(jax.random.uniform(ks[4], (DEPTH, GDN_HEADS), f32, 1.0, 16.0))
    dt_bias = 0.5 * jax.random.normal(ks[5], (DEPTH, GDN_HEADS), f32)
    gdn_norm_w = 1.0 + 0.05 * jax.random.normal(ks[6], (DEPTH, GDN_VAL_DIM), f32)
    w_up_a = jax.random.normal(ks[7], (DEPTH, DSA_WIDTH, D_MODEL), f32) * DSA_WIDTH ** -0.5
    w_up_b = jax.random.normal(ks[8], (DEPTH, GDN_V_WIDTH, D_MODEL), f32) * GDN_V_WIDTH ** -0.5
    w_out = jax.random.normal(ks[9], (DEPTH, D_MODEL, D_MODEL), f32) * D_MODEL ** -0.5
    final_norm_w = 1.0 + 0.05 * jax.random.normal(ks[10], (D_MODEL,), f32)
    return {'x': x, 'norm_w': norm_w, 'w_in': w_in, 'conv_w': conv_w, 'a_log': a_log,
            'dt_bias': dt_bias, 'gdn_norm_w': gdn_norm_w, 'w_up_a': w_up_a, 'w_up_b': w_up_b,
            'w_out': w_out, 'final_norm_w': final_norm_w}

def first_block(x, norm_w, w_in, conv_w, a_log, dt_bias, gdn_norm_w, w_up_a, w_up_b, w_out, final_norm_w):
    f32 = jnp.float32
    b, s, _ = x.shape
    cos, sin = _rope_tables(s, DSA_HEAD_DIM)
    for layer in range(DEPTH):
        h = _rmsnorm(x, norm_w[layer])
        proj = h @ w_in[layer]
        dsa_qkv, dsa_z, gdn_qkv, gdn_z, gdn_b, gdn_a, gate_a, gate_b = _split_columns(proj)

        qkv = dsa_qkv.astype(f32).reshape(b, s, DSA_GROUPS, 3, DSA_HEADS, DSA_HEAD_DIM)
        q_a = _apply_rope(qkv[:, :, :, 0], cos, sin)
        k_a = _apply_rope(qkv[:, :, :, 1], cos, sin)
        v_a = qkv[:, :, :, 2]
        o_a = _dilated_mixture(q_a, k_a, v_a).astype(x.dtype)
        y_a = (o_a * jax.nn.silu(dsa_z)) @ w_up_a[layer]

        cqkv = jax.nn.silu(_causal_depthwise_conv(gdn_qkv, conv_w[layer])).astype(f32)
        gq, gk, gv = jnp.split(cqkv, [GDN_K_WIDTH, 2 * GDN_K_WIDTH], axis=-1)
        gq = _l2norm(gq.reshape(b, s, GDN_HEADS, GDN_KEY_DIM)) * GDN_KEY_DIM ** -0.5
        gk = _l2norm(gk.reshape(b, s, GDN_HEADS, GDN_KEY_DIM))
        gv = gv.reshape(b, s, GDN_HEADS, GDN_VAL_DIM)
        beta = jax.nn.sigmoid(gdn_b.astype(f32))
        g = -jnp.exp(a_log[layer].astype(f32)) * jax.nn.softplus(gdn_a.astype(f32) + dt_bias[layer].astype(f32))
        o_b = _gated_delta_rule(gq, gk, gv, g, beta)
        o_b = _rmsnorm(o_b, gdn_norm_w[layer]).reshape(b, s, GDN_V_WIDTH).astype(x.dtype)
        y_b = (o_b * jax.nn.silu(gdn_z)) @ w_up_b[layer]

        merged = jax.nn.sigmoid(gate_a) * y_a + jax.nn.sigmoid(gate_b) * y_b
        x = x + merged @ w_out[layer]
    return _rmsnorm(x, final_norm_w)


GRID_W = 64
CTX_LEN = 256
HEAD_DIM = D_MODEL // 16
A_HEADS = 4
B_HEADS = 4
C_HEADS = 8
A_WIDTH = A_HEADS * HEAD_DIM
B_WIDTH = B_HEADS * HEAD_DIM
C_WIDTH = C_HEADS * HEAD_DIM
MIX_WIDTH = A_WIDTH + B_WIDTH + C_WIDTH
HGRN_CHUNK = 16
HGRN_F_FLOOR = 1e-20
RWKV_W_RANK = 64
RWKV_A_RANK = 64
RWKV_G_RANK = 128
RWKV_LN_EPS = 64e-5
NA_WIN_ROWS = 8
NA_WIN_COLS = 16
NA_COL_BLOCK = 16
NA_KEY_COLS = NA_COL_BLOCK + NA_WIN_COLS
N_GROUPS = 4
EXPERTS_PER_GROUP = 8
TOP_K_IN_GROUP = 2
D_EXPERT = 512
EPS = 1e-6
NEG_INF = -1e30
A_PROJ = 5 * A_WIDTH
B_PROJ = 3 * B_WIDTH + 2 * RWKV_W_RANK + 2 * RWKV_A_RANK + RWKV_G_RANK
C_PROJ = 3 * C_WIDTH
P_TOTAL = A_PROJ + B_PROJ + C_PROJ
RWKV_SPLITS = (B_WIDTH, 2 * B_WIDTH, 3 * B_WIDTH, 3 * B_WIDTH + RWKV_W_RANK, 3 * B_WIDTH + 2 * RWKV_W_RANK,
               3 * B_WIDTH + 2 * RWKV_W_RANK + RWKV_A_RANK, 3 * B_WIDTH + 2 * RWKV_W_RANK + 2 * RWKV_A_RANK)


def rms_norm(x, gain):
    xf = x.astype(jnp.float32)
    return xf * lax.rsqrt(jnp.mean(xf * xf, axis=-1, keepdims=True) + EPS) * gain.astype(jnp.float32)

def to_heads(t, n_heads):
    b, t_len, _ = t.shape
    return t.reshape(b, t_len, n_heads, HEAD_DIM).transpose(0, 2, 1, 3)

def chunk_gla(q, k, v, log_f, s0):
    b, h, t_len, _ = q.shape
    n = t_len // HGRN_CHUNK

    def blocks(u):
        return u.reshape(b, h, n, HGRN_CHUNK, u.shape[-1])

    q, k, v, log_f = blocks(q), blocks(k), blocks(v), blocks(log_f)
    cum = jnp.cumsum(log_f, axis=3)
    tri = jnp.tril(jnp.ones((HGRN_CHUNK, HGRN_CHUNK), dtype=bool))[:, :, None]
    diff = cum[:, :, :, :, None, :] - cum[:, :, :, None, :, :]
    decay = jnp.where(tri, jnp.exp(jnp.where(tri, diff, 0.0)), 0.0)
    scores = jnp.einsum('bhntd,bhnsd,bhntsd->bhnts', q, k, decay)
    o_intra = jnp.einsum('bhnts,bhnsv->bhntv', scores, v)
    q_in = q * jnp.exp(cum)
    k_out = k * jnp.exp(cum[:, :, :, -1:, :] - cum)
    kv = jnp.einsum('bhnsd,bhnsv->bhndv', k_out, v)
    chunk_decay = jnp.exp(cum[:, :, :, -1, :])

    def step(s, inp):
        q_c, dec_c, kv_c = inp
        o_c = jnp.einsum('bhtd,bhdv->bhtv', q_c, s)
        return s * dec_c[..., None] + kv_c, o_c

    s_fin, o_inter = lax.scan(step, s0, (jnp.moveaxis(q_in, 2, 0), jnp.moveaxis(chunk_decay, 2, 0),
                                         jnp.moveaxis(kv, 2, 0)))
    o = o_intra + jnp.moveaxis(o_inter, 0, 2)
    return o.reshape(b, h, t_len, v.shape[-1]), s_fin

def hgrn2_forget(f_pre, lb):
    f = lb + (1.0 - lb) * jax.nn.sigmoid(f_pre)
    log_f = jnp.log(jnp.maximum(f, HGRN_F_FLOOR))
    k = (1.0 - lb) * jax.nn.sigmoid(-f_pre)
    return to_heads(log_f, A_HEADS), to_heads(k, A_HEADS)

def hgrn2_mixer(p_ctx, p_lat, lb_fwd, lb_bwd, gn_gain):
    qc, ffc, fbc, ic, gc = jnp.split(p_ctx, 5, axis=-1)
    ql, ffl, fbl, il, gl = jnp.split(p_lat, 5, axis=-1)
    qc, ic, ql, il = (to_heads(t, A_HEADS) for t in (qc, ic, ql, il))
    s0 = jnp.zeros((p_lat.shape[0], A_HEADS, HEAD_DIM, HEAD_DIM), jnp.float32)

    def flip(t):
        return t[:, :, ::-1]

    lf, kf = hgrn2_forget(ffc, lb_fwd)
    oc_f, s_f = chunk_gla(qc, kf, ic, lf, s0)
    lf, kf = hgrn2_forget(ffl, lb_fwd)
    ol_f, _ = chunk_gla(ql, kf, il, lf, s_f)
    lbk, kb = hgrn2_forget(fbc, lb_bwd)
    oc_b, s_b = chunk_gla(flip(qc), flip(kb), flip(ic), flip(lbk), s0)
    lbk, kb = hgrn2_forget(fbl, lb_bwd)
    ol_b, _ = chunk_gla(flip(ql), flip(kb), flip(il), flip(lbk), s_b)

    def readout(o, g):
        o = rms_norm(o.transpose(0, 2, 1, 3), gn_gain)
        return o.reshape(g.shape) * jax.nn.silu(g)

    return readout(ol_f + flip(ol_b), gl), readout(oc_f + flip(oc_b), gc)

def centred_shift(u):
    pad = jnp.pad(u, ((0, 0), (1, 1), (0, 0)))
    return 0.5 * (pad[:, :-2] + pad[:, 2:])

def rwkv7_scan(r, w, k, v, kk, ak, s0):
    def step(s, inp):
        r_t, w_t, k_t, v_t, kk_t, ak_t = inp
        sa = jnp.einsum('bhvk,bhk->bhv', s, kk_t)
        s = s * w_t[:, :, None, :] - sa[..., None] * ak_t[:, :, None, :] + v_t[..., None] * k_t[:, :, None, :]
        return s, jnp.einsum('bhvk,bhk->bhv', s, r_t)

    xs = tuple(jnp.moveaxis(u, 1, 0) for u in (r, w, k, v, kk, ak))
    s_fin, ys = lax.scan(step, s0, xs)
    return jnp.moveaxis(ys, 0, 1), s_fin

def rwkv7_mixer(p_ctx, p_lat, mu, w0, w_up, a0, a_up, g_up, kk_scale, k_a, r_k, ln_gain, ln_bias):
    def hd(t):
        return t.reshape(t.shape[0], t.shape[1], B_HEADS, HEAD_DIM)

    def prep(p):
        p = p + (centred_shift(p) - p) * mu
        r, k, v, wdf, wdb, adf, adb, gd = jnp.split(p, list(RWKV_SPLITS), axis=-1)
        kk = hd(k * kk_scale)
        kk = kk / jnp.maximum(jnp.sqrt(jnp.sum(kk * kk, axis=-1, keepdims=True)), 1e-12)
        dirs = []
        for d, (wd, ad) in enumerate(((wdf, adf), (wdb, adb))):
            w = -jax.nn.softplus(-(w0[d] + jnp.tanh(wd) @ w_up[d])) - 0.5
            decay = jnp.exp(-jnp.exp(w))
            a = jax.nn.sigmoid(a0[d] + ad @ a_up[d])
            k_d = k * (1.0 + (a - 1.0) * k_a)
            dirs.append((hd(decay), hd(k_d), hd(a) * kk))
        g = jax.nn.sigmoid(gd) @ g_up
        return hd(r), hd(v), kk, dirs, g

    rc, vc, kkc, dc, gc = prep(p_ctx)
    rl, vl, kkl, dl, gl = prep(p_lat)
    s0 = jnp.zeros((p_lat.shape[0], B_HEADS, HEAD_DIM, HEAD_DIM), jnp.float32)

    def flip(t):
        return t[:, ::-1]

    (wcf, kcf, akcf), (wcb, kcb, akcb) = dc
    (wlf, klf, aklf), (wlb, klb, aklb) = dl
    yc_f, s_f = rwkv7_scan(rc, wcf, kcf, vc, kkc, akcf, s0)
    yl_f, _ = rwkv7_scan(rl, wlf, klf, vl, kkl, aklf, s_f)
    yc_b, s_b = rwkv7_scan(flip(rc), flip(wcb), flip(kcb), flip(vc), flip(kkc), flip(akcb), s0)
    yl_b, _ = rwkv7_scan(flip(rl), flip(wlb), flip(klb), flip(vl), flip(kkl), flip(aklb), s_b)

    def readout(y, r, v, k_f, k_b, g):
        mean = jnp.mean(y, axis=-1, keepdims=True)
        var = jnp.mean(jnp.square(y - mean), axis=-1, keepdims=True)
        y = ((y - mean) * lax.rsqrt(var + RWKV_LN_EPS)).reshape(g.shape) * ln_gain + ln_bias
        bonus = (jnp.sum(r * (k_f + k_b) * r_k, axis=-1, keepdims=True) * v).reshape(g.shape)
        return (y + bonus) * g

    out_lat = readout(yl_f + flip(yl_b), rl, vl, klf, klb, gl)
    out_ctx = readout(yc_f + flip(yc_b), rc, vc, kcf, kcb, gc)
    return out_lat, out_ctx

def axial_rope(t, pos_r, pos_c):
    quarter = HEAD_DIM // 4
    inv = ROPE_THETA ** (-jnp.arange(quarter, dtype=jnp.float32) / quarter)
    ang = jnp.concatenate([pos_r[:, None] * inv, pos_c[:, None] * inv], axis=-1)
    cos = jnp.cos(ang)[None, :, None, :]
    sin = jnp.sin(ang)[None, :, None, :]
    t1, t2 = jnp.split(t, 2, axis=-1)
    return jnp.concatenate([t1 * cos - t2 * sin, t2 * cos + t1 * sin], axis=-1)

def neighbourhood_attention(p_ctx, p_lat, q_gain, k_gain, rpb, pos_r, pos_c, need_ctx):
    bsz, t_lat, _ = p_lat.shape
    n_ctx = p_ctx.shape[1]
    rows = t_lat // GRID_W
    win_r = min(NA_WIN_ROWS, rows)
    scale = HEAD_DIM ** -0.5

    def qkv(p):
        q, k, v = jnp.split(p, 3, axis=-1)
        hd = lambda t: t.reshape(t.shape[0], t.shape[1], C_HEADS, HEAD_DIM)
        return rms_norm(hd(q), q_gain), rms_norm(hd(k), k_gain), hd(v)

    qc, kc, vc = qkv(p_ctx)
    ql, kl, vl = qkv(p_lat)
    ql, kl = axial_rope(ql, pos_r, pos_c), axial_rope(kl, pos_r, pos_c)
    kc_h, vc_h = kc.transpose(0, 2, 1, 3), vc.transpose(0, 2, 1, 3)

    def grid(t):
        return t.transpose(0, 2, 1, 3).reshape(bsz, C_HEADS, rows, GRID_W, HEAD_DIM)

    qg, kg, vg = grid(ql), grid(kl), grid(vl)
    n_cb = GRID_W // NA_COL_BLOCK
    q_col = jnp.arange(GRID_W).reshape(n_cb, NA_COL_BLOCK)
    k_start = jnp.clip(jnp.arange(n_cb) * NA_COL_BLOCK - NA_WIN_COLS // 2, 0, GRID_W - NA_KEY_COLS)
    k_col = k_start[:, None] + jnp.arange(NA_KEY_COLS)
    w_start = jnp.clip(q_col - NA_WIN_COLS // 2, 0, GRID_W - NA_WIN_COLS)
    kc3 = k_col[:, None, :]
    in_win = (kc3 >= w_start[..., None]) & (kc3 < w_start[..., None] + NA_WIN_COLS)
    col_idx = jnp.clip(kc3 - q_col[..., None] + NA_WIN_COLS - 1, 0, 2 * NA_WIN_COLS - 2)
    n_win = win_r * NA_KEY_COLS

    def one_row(r):
        r_start = jnp.clip(r - win_r // 2, 0, rows - win_r)
        k_blk = lax.dynamic_slice_in_dim(kg, r_start, win_r, axis=2)[:, :, :, k_col]
        v_blk = lax.dynamic_slice_in_dim(vg, r_start, win_r, axis=2)[:, :, :, k_col]
        q_row = lax.dynamic_index_in_dim(qg, r, axis=2, keepdims=False).reshape(
            bsz, C_HEADS, n_cb, NA_COL_BLOCK, HEAD_DIM)
        s_win = jnp.einsum('bhjqd,bhrjkd->bhjqrk', q_row, k_blk) * scale
        row_idx = r_start + jnp.arange(win_r) - r + NA_WIN_ROWS - 1
        bias = rpb[:, row_idx[None, None, :, None], col_idx[:, :, None, :]]
        s_win = jnp.where(in_win[:, :, None, :], s_win + bias, NEG_INF)
        s_ctx = jnp.einsum('bhjqd,bhld->bhjql', q_row, kc_h) * scale
        s_all = jnp.concatenate([s_win.reshape(s_win.shape[:4] + (n_win,)), s_ctx], axis=-1)
        prob = jax.nn.softmax(s_all, axis=-1)
        p_win = prob[..., :n_win].reshape(s_win.shape)
        p_ctx = prob[..., n_win:]
        o = (jnp.einsum('bhjqrk,bhrjkd->bhjqd', p_win, v_blk)
             + jnp.einsum('bhjql,bhld->bhjqd', p_ctx, vc_h))
        return o.reshape(bsz, C_HEADS, GRID_W, HEAD_DIM)

    o = lax.map(one_row, jnp.arange(rows))
    out_lat = o.transpose(1, 0, 3, 2, 4).reshape(bsz, t_lat, C_WIDTH)
    out_ctx = None
    if need_ctx:
        qc_h = qc.transpose(0, 2, 1, 3)
        pc = jax.nn.softmax(jnp.einsum('bhqd,bhkd->bhqk', qc_h, kc_h) * scale, axis=-1)
        out_ctx = jnp.einsum('bhqk,bhkd->bhqd', pc, vc_h).transpose(0, 2, 1, 3).reshape(bsz, n_ctx, C_WIDTH)
    return out_lat, out_ctx

def hierarchical_moe(h, w_rg, b_rg, w_re, b_re, w_gate, w_up, w_down):
    g_logits = h @ w_rg + b_rg
    g_prob = jax.nn.softmax(g_logits, axis=-1)
    g_sel = jnp.argmax(g_logits, axis=-1)
    g_w = jnp.take_along_axis(g_prob, g_sel[:, None], axis=-1)
    e_logits = (h @ w_re + b_re).reshape(-1, N_GROUPS, EXPERTS_PER_GROUP)
    e_logits = jnp.take_along_axis(e_logits, g_sel[:, None, None], axis=1)[:, 0]
    e_prob = jax.nn.softmax(e_logits, axis=-1)
    top_w, top_i = lax.top_k(e_prob, TOP_K_IN_GROUP)
    top_w = top_w / jnp.sum(top_w, axis=-1, keepdims=True) * g_w
    e_w = jnp.sum(jax.nn.one_hot(top_i, EXPERTS_PER_GROUP, dtype=jnp.float32) * top_w[..., None], axis=1)
    comb = jax.nn.one_hot(g_sel, N_GROUPS, dtype=jnp.float32)[:, :, None] * e_w[:, None, :]
    y = jnp.zeros(h.shape, jnp.float32)
    for gi in range(N_GROUPS):
        hid = jax.nn.silu(jnp.einsum('nd,edf->nef', h, w_gate[gi])) * jnp.einsum('nd,edf->nef', h, w_up[gi])
        y = y + jnp.einsum('nef,efd->nd', hid * comb[:, gi, :, None], w_down[gi])
    return y

def second_inputs(seed: int = 0) -> dict:
    key = jax.random.key(seed)
    ks = iter(jax.random.split(key, 40))
    D, G, E, F = D_MODEL, N_GROUPS, EXPERTS_PER_GROUP, D_EXPERT

    def nrm(shape, s):
        return s * jax.random.normal(next(ks), shape, jnp.float32)

    return {
        'x': nrm((BATCH, SEQ, D), 1.0),
        'c': nrm((BATCH, D), 1.0),
        'ctx': nrm((BATCH, CTX_LEN, D), 1.0),
        'c_ctx': nrm((D,), 1.0),
        'norm1_gain': 1.0 + nrm((DEPTH, D), 0.02),
        'norm2_gain': 1.0 + nrm((DEPTH, D), 0.02),
        'w_ada': nrm((DEPTH, D, 6 * D), 0.5 * D ** -0.5),
        'b_ada': nrm((DEPTH, 6 * D), 0.02),
        'w_in': nrm((DEPTH, D, P_TOTAL), D ** -0.5),
        'w_out': nrm((DEPTH, MIX_WIDTH, D), MIX_WIDTH ** -0.5),
        'hgrn_lb_logits': nrm((2, DEPTH, A_WIDTH), 0.5),
        'hgrn_gn_gain': 1.0 + nrm((DEPTH, A_HEADS, HEAD_DIM), 0.02),
        'rwkv_mu': jax.random.uniform(next(ks), (DEPTH, B_PROJ), jnp.float32, 0.0, 1.0),
        'rwkv_w0': -1.5 + nrm((DEPTH, 2, B_WIDTH), 0.5),
        'rwkv_w_up': nrm((DEPTH, 2, RWKV_W_RANK, B_WIDTH), RWKV_W_RANK ** -0.5),
        'rwkv_a0': nrm((DEPTH, 2, B_WIDTH), 0.1),
        'rwkv_a_up': nrm((DEPTH, 2, RWKV_A_RANK, B_WIDTH), RWKV_A_RANK ** -0.5),
        'rwkv_g_up': nrm((DEPTH, RWKV_G_RANK, B_WIDTH), RWKV_G_RANK ** -0.5),
        'rwkv_kk_scale': 0.85 + nrm((DEPTH, B_WIDTH), 0.02),
        'rwkv_k_a': 1.0 + nrm((DEPTH, B_WIDTH), 0.02),
        'rwkv_r_k': nrm((DEPTH, B_HEADS, HEAD_DIM), 0.1),
        'rwkv_ln_gain': 1.0 + nrm((DEPTH, B_WIDTH), 0.02),
        'rwkv_ln_bias': nrm((DEPTH, B_WIDTH), 0.02),
        'na_q_gain': 1.0 + nrm((DEPTH, HEAD_DIM), 0.02),
        'na_k_gain': 1.0 + nrm((DEPTH, HEAD_DIM), 0.02),
        'na_rpb': nrm((DEPTH, C_HEADS, 2 * NA_WIN_ROWS - 1, 2 * NA_WIN_COLS - 1), 0.1),
        'w_router_group': nrm((DEPTH, D, G), D ** -0.5),
        'b_router_group': nrm((DEPTH, G), 0.01),
        'w_router_expert': nrm((DEPTH, D, G * E), D ** -0.5),
        'b_router_expert': nrm((DEPTH, G * E), 0.01),
        'w_exp_gate': nrm((DEPTH, G, E, D, F), D ** -0.5),
        'w_exp_up': nrm((DEPTH, G, E, D, F), D ** -0.5),
        'w_exp_down': nrm((DEPTH, G, E, F, D), F ** -0.5),
    }

def second_block(x, c, ctx, c_ctx, norm1_gain, norm2_gain, w_ada, b_ada, w_in, w_out,
              hgrn_lb_logits, hgrn_gn_gain, rwkv_mu, rwkv_w0, rwkv_w_up, rwkv_a0, rwkv_a_up,
              rwkv_g_up, rwkv_kk_scale, rwkv_k_a, rwkv_r_k, rwkv_ln_gain, rwkv_ln_bias,
              na_q_gain, na_k_gain, na_rpb, w_router_group, b_router_group,
              w_router_expert, b_router_expert, w_exp_gate, w_exp_up, w_exp_down):
    f32 = jnp.float32
    bsz, t_lat, _ = x.shape
    n_ctx = ctx.shape[1]
    pos = jnp.arange(t_lat)
    pos_r = (pos // GRID_W).astype(f32)
    pos_c = (pos % GRID_W).astype(f32)
    lb_p = jax.nn.softmax(hgrn_lb_logits.astype(f32), axis=1)
    lower_bounds = jnp.cumsum(lb_p, axis=1) - lb_p[:, :1]
    silu_c = jax.nn.silu(c.astype(f32))
    silu_cc = jax.nn.silu(c_ctx.astype(f32))
    xl = x.astype(f32)
    xc = ctx.astype(f32)
    for layer in range(DEPTH):
        last = layer == DEPTH - 1
        mod_l = (silu_c @ w_ada[layer] + b_ada[layer])[:, None, :]
        mod_c = (silu_cc @ w_ada[layer] + b_ada[layer])[None, None, :]
        sh1l, sc1l, g1l, sh2l, sc2l, g2l = jnp.split(mod_l, 6, axis=-1)
        sh1c, sc1c, g1c, sh2c, sc2c, g2c = jnp.split(mod_c, 6, axis=-1)
        hl = rms_norm(xl, norm1_gain[layer]) * (1.0 + sc1l) + sh1l
        hc = rms_norm(xc, norm1_gain[layer]) * (1.0 + sc1c) + sh1c
        pl = hl @ w_in[layer]
        pc = hc @ w_in[layer]
        al, bl, cl = jnp.split(pl, [A_PROJ, A_PROJ + B_PROJ], axis=-1)
        ac, bc, cc = jnp.split(pc, [A_PROJ, A_PROJ + B_PROJ], axis=-1)
        a_lat, a_ctx = hgrn2_mixer(ac, al, lower_bounds[0, layer], lower_bounds[1, layer], hgrn_gn_gain[layer])
        b_lat, b_ctx = rwkv7_mixer(bc, bl, rwkv_mu[layer], rwkv_w0[layer], rwkv_w_up[layer], rwkv_a0[layer],
                                   rwkv_a_up[layer], rwkv_g_up[layer], rwkv_kk_scale[layer], rwkv_k_a[layer],
                                   rwkv_r_k[layer], rwkv_ln_gain[layer], rwkv_ln_bias[layer])
        c_lat, c_ctxo = neighbourhood_attention(cc, cl, na_q_gain[layer], na_k_gain[layer], na_rpb[layer],
                                                pos_r, pos_c, not last)
        xl = xl + g1l * (jnp.concatenate([a_lat, b_lat, c_lat], axis=-1) @ w_out[layer])
        h2l = (rms_norm(xl, norm2_gain[layer]) * (1.0 + sc2l) + sh2l).reshape(-1, D_MODEL)
        moe_w = (w_router_group[layer], b_router_group[layer], w_router_expert[layer], b_router_expert[layer],
                 w_exp_gate[layer], w_exp_up[layer], w_exp_down[layer])
        if last:
            xl = xl + g2l * hierarchical_moe(h2l, *moe_w).reshape(xl.shape)
        else:
            xc = xc + g1c * (jnp.concatenate([a_ctx, b_ctx, c_ctxo], axis=-1) @ w_out[layer])
            h2c = (rms_norm(xc, norm2_gain[layer]) * (1.0 + sc2c) + sh2c).reshape(-1, D_MODEL)
            y = hierarchical_moe(jnp.concatenate([h2c, h2l], axis=0), *moe_w)
            xc = xc + g2c * y[:bsz * n_ctx].reshape(xc.shape)
            xl = xl + g2l * y[bsz * n_ctx:].reshape(xl.shape)
    return xl.astype(x.dtype)


def setup_inputs(seed=0):
    out = dict(first_inputs(seed))
    for name, value in second_inputs(seed + 1).items():
        if name != "x":
            out[name + "_2"] = value
    return out


def reference(
    x, norm_w, w_in, conv_w, a_log, dt_bias, gdn_norm_w, w_up_a, w_up_b, w_out, final_norm_w,
    c_2, ctx_2, c_ctx_2, norm1_gain_2, norm2_gain_2, w_ada_2, b_ada_2, w_in_2, w_out_2,
    hgrn_lb_logits_2, hgrn_gn_gain_2, rwkv_mu_2, rwkv_w0_2, rwkv_w_up_2, rwkv_a0_2, rwkv_a_up_2,
    rwkv_g_up_2, rwkv_kk_scale_2, rwkv_k_a_2, rwkv_r_k_2, rwkv_ln_gain_2, rwkv_ln_bias_2,
    na_q_gain_2, na_k_gain_2, na_rpb_2, w_router_group_2, b_router_group_2, w_router_expert_2,
    b_router_expert_2, w_exp_gate_2, w_exp_up_2, w_exp_down_2,
):
    x = first_block(
        x, norm_w, w_in, conv_w, a_log, dt_bias, gdn_norm_w, w_up_a, w_up_b, w_out,
        final_norm_w,
    )
    return second_block(
        x, c_2, ctx_2, c_ctx_2, norm1_gain_2, norm2_gain_2, w_ada_2, b_ada_2, w_in_2, w_out_2,
        hgrn_lb_logits_2, hgrn_gn_gain_2, rwkv_mu_2, rwkv_w0_2, rwkv_w_up_2, rwkv_a0_2,
        rwkv_a_up_2, rwkv_g_up_2, rwkv_kk_scale_2, rwkv_k_a_2, rwkv_r_k_2, rwkv_ln_gain_2,
        rwkv_ln_bias_2, na_q_gain_2, na_k_gain_2, na_rpb_2, w_router_group_2, b_router_group_2,
        w_router_expert_2, b_router_expert_2, w_exp_gate_2, w_exp_up_2, w_exp_down_2,
    )


_drawn_inputs = setup_inputs


def setup_inputs(seed=0):
    import zlib

    import numpy as np

    out = dict(_drawn_inputs(seed))
    spreads = {}
    factors = {'gdn_norm_w': 3.034,
     'ctx_2': 13.748,
     'norm1_gain_2': 8.0,
     'norm2_gain_2': 37.808,
     'b_ada_2': 2.973,
     'hgrn_gn_gain_2': 64.0,
     'rwkv_w_up_2': 30.384,
     'rwkv_a0_2': 8.0,
     'rwkv_kk_scale_2': 200.0,
     'rwkv_k_a_2': 8.0,
     'rwkv_ln_gain_2': 200.0,
     'rwkv_ln_bias_2': 200.0,
     'na_q_gain_2': 64.0,
     'na_k_gain_2': 64.0,
     'na_rpb_2': 200.0,
     'b_router_group_2': 64.0,
     'b_router_expert_2': 64.0,
     'c_ctx_2': 6.438,
     'rwkv_w0_2': 8.0}
    for name, (base, spread) in spreads.items():
        noise = np.random.default_rng([zlib.crc32(name.encode()), seed]).standard_normal(out[name].shape)
        drawn = base * np.exp(spread * noise) if base else spread * noise
        out[name] = jnp.asarray(drawn.astype(out[name].dtype))
    for name, factor in factors.items():
        out[name] = (out[name] * factor).astype(out[name].dtype)
    return out
```

```python
import math
from contextlib import ExitStack

import numpy as np

import concourse.bass as bass
from concourse import mybir

F32 = mybir.dt.float32
ALU = mybir.AluOpType
ACT = mybir.ActivationFunctionType
AX = mybir.AxisListType

P = 128
S = 512
CTX = 256
T2 = CTX + S
D = 1024
KD = D // P
TT = S // P
TC = T2 // P
CT = CTX // P
HD = 64
N_EXP = 32
N_GRP = 4
EPG = N_EXP // N_GRP
D_EXP = 512
FT = D_EXP // P
EPS = 1e-6
NEG = -1e30
LEVELS = 7


class Kept:
    pass


class Item:

    def __init__(self, segs, values, out):
        self.segs, self.values, self.out = segs, values, out


class Chain:

    def __init__(self, eng, sem):
        self.eng, self.sem, self.n = eng, sem, 0

    def __call__(self, ins):
        self.n += 1
        ins.then_inc(self.sem, 1)
        self.eng.wait_ge(self.sem, self.n)


class Stage:

    FIRST, SET = 150, 24
    turn = 0

    def __init__(self, nc, name, *sems):
        self.nc, self.name, self.sems, self.ctx = nc, name, sems, ExitStack()

    def __enter__(self):
        nc, s = self.nc, Kept()
        assert len(self.sems) <= self.SET
        mine = self.FIRST + self.SET * (Stage.turn % 2)
        other = self.FIRST + self.SET * ((Stage.turn + 1) % 2)
        if Stage.turn:
            nc.sync.sem_clear(range(other, other + self.SET))
        Stage.turn += 1
        names = [n for n in self.sems if not n.startswith("soft")]
        self.handles = [nc.alloc_semaphore(f"{self.name}_{n}", num=mine + i) for i, n in enumerate(names)]
        s.sem = dict(zip(names, self.handles))
        for n in self.sems:
            if n.startswith("soft"):
                s.sem[n] = nc.alloc_semaphore(f"{self.name}_{n}")
        s.block = self.ctx.enter_context(self.nc.Block())
        return s

    def __exit__(self, *exc):
        self.ctx.__exit__(*exc)
        for h in self.handles:
            self.nc.release_semaphore(h)


def load_stage(nc, name, pairs):
    with Stage(nc, name, "loaded") as st:
        @st.block.sync
        def _(sync):
            for to, of in pairs:
                sync.dma_start(to, of).then_inc(st.sem["loaded"], 16)
            sync.wait_ge(st.sem["loaded"], 16 * len(pairs))


def norm_stage(nc, K, name, x_tiles, n_tok, out, gain, shift=None, square=None):
    with Stage(nc, name, "squared", "rooted", "v", "used") as st:
        sem = st.sem

        @st.block.scalar
        def _(act):
            for k in range(KD):
                if k >= 2:
                    act.wait_ge(sem["used"], k - 1)
                nc.scalar.activation(square[:, k % 2, :n_tok], x_tiles(k), ACT.Square).then_inc(sem["squared"], 1)
            rstd = K.rstd[:, 0, :n_tok]
            act.wait_ge(sem["used"], KD)
            nc.scalar.activation(rstd, K.psum[:, 0, :n_tok], ACT.Ln, scale=1.0 / D, bias=K.eps).then_inc(sem["rooted"], 1)
            act.wait_ge(sem["rooted"], 1)
            nc.scalar.activation(rstd, rstd, ACT.Exp, scale=-0.5).then_inc(sem["rooted"], 1)

        @st.block.tensor
        def _(pe):
            for k in range(KD):
                pe.wait_ge(sem["squared"], k + 1)
                m = nc.tensor.matmul(K.psum[:, 0, :n_tok], K.ones[:], square[:, k % 2, :n_tok],
                                     start=(k == 0), stop=(k == KD - 1))
                m.then_inc(sem["used"], 1)

        @st.block.vector
        def _(dve):
            link = Chain(dve, sem["v"])
            dve.wait_ge(sem["rooted"], 2)
            for k in range(KD):
                m = nc.vector.scalar_tensor_tensor(out(k), x_tiles(k), gain[:, k:k + 1], K.rstd[:, 0, :n_tok],
                                                   ALU.mult, ALU.mult)
                if shift is not None:
                    link(m)
                    nc.vector.tensor_scalar(out(k), out(k), shift[:, k:k + 1], None, ALU.add)


def project_feature(nc, K, name, weights, n_tiles, src, segs, evac, kd=KD, dve_post=None,
                    extra_sems=(), gpsimd=None, base=0):
    nseg = len(segs)
    per = 4 // nseg if nseg > 1 else 4
    wring = K.wring[:, :, :kd * P].rearrange("p s (k n) -> p s k n", k=kd)
    ns = K.nring
    with Stage(nc, name, *[f"w{j}" for j in range(ns)], "done", "emptied", "posted", "v", "a") as st:
        sem = st.sem

        @st.block.sync
        def _(sync):
            for t in range(n_tiles):
                if t >= ns:
                    sync.wait_ge(sem["done"], t - ns + 1)
                sync.dma_start(wring[:, t % ns], weights[base + t]).then_inc(sem[f"w{t % ns}"], 16)

        @st.block.tensor
        def _(pe):
            for t in range(n_tiles):
                pe.wait_ge(sem[f"w{t % ns}"], 16 * (t // ns + 1))
                if t >= per:
                    pe.wait_ge(sem["emptied"], t - per + 1)
                for g, (at, n) in enumerate(segs):
                    for k in range(kd):
                        m = nc.tensor.matmul(K.psum[:, (t % per) * nseg + g, :n], wring[:, t % ns, k],
                                             src(k)[:, at:at + n], start=(k == 0), stop=(k == kd - 1))
                m.then_inc(sem["done"], 1)

        @st.block.scalar
        def _(act):
            link = Chain(act, sem["a"])
            for t in range(n_tiles):
                act.wait_ge(sem["done"], t + 1)
                for g, (at, n) in enumerate(segs):
                    m = evac(t, g, at, n, K.psum[:, (t % per) * nseg + g, :n], link)
                m.then_inc(sem["emptied"], 1)

        if dve_post is not None:
            @st.block.vector
            def _(dve):
                link = Chain(dve, sem["v"])
                for t in range(n_tiles):
                    dve.wait_ge(sem["emptied"], t + 1)
                    dve_post(t, link)


def project_token(nc, K, name, weights, n_w, src, tiles, evac, width=512, kd=KD):
    ring = K.vring[:, :, :kd * width].rearrange("p s (k n) -> p s k n", k=kd)
    nt = len(tiles)
    with Stage(nc, name, "w0", "w1", "done", "emptied", "a") as st:
        sem = st.sem

        @st.block.sync
        def _(sync):
            for w in range(n_w):
                if w >= 2:
                    sync.wait_ge(sem["done"], (w - 1) * nt)
                sync.dma_start(ring[:, w % 2], weights(w)).then_inc(sem[f"w{w % 2}"], 16)

        @st.block.tensor
        def _(pe):
            for w in range(n_w):
                pe.wait_ge(sem[f"w{w % 2}"], 16 * (w // 2 + 1))
                for j, t in enumerate(tiles):
                    n = w * nt + j
                    if n >= 4:
                        pe.wait_ge(sem["emptied"], n - 3)
                    for k in range(kd):
                        m = nc.tensor.matmul(K.psum[:, n % 4, :width], src(k)[:, t * P:(t + 1) * P],
                                             ring[:, w % 2, k], start=(k == 0), stop=(k == kd - 1))
                    m.then_inc(sem["done"], 1)

        @st.block.scalar
        def _(act):
            for n in range(n_w * nt):
                act.wait_ge(sem["done"], n + 1)
                evac(n // nt, n % nt, K.psum[:, n % 4, :width]).then_inc(sem["emptied"], 1)


def rope_stage(nc, K, name, tiles, n, cos, sin):
    with Stage(nc, name, "rotated", "read", "v") as st:
        sem = st.sem

        @st.block.tensor
        def _(pe):
            for t, x in enumerate(tiles):
                if t >= 4:
                    pe.wait_ge(sem["read"], t - 3)
                nc.tensor.matmul(K.psum[:, t % 4, :n], K.rot[:], x, start=True, stop=True).then_inc(sem["rotated"], 1)

        @st.block.vector
        def _(dve):
            link = Chain(dve, sem["v"])
            for t, x in enumerate(tiles):
                dve.wait_ge(sem["rotated"], t + 1)
                nc.vector.tensor_tensor(K.tmp[:, t % 2, :n], K.psum[:, t % 4, :n], sin, ALU.mult).then_inc(sem["read"], 1)
                link(nc.vector.tensor_tensor(x, x, cos, ALU.mult))
                dve.wait_ge(sem["read"], t + 1)
                link(nc.vector.tensor_tensor(x, x, K.tmp[:, t % 2, :n], ALU.add))


def attention_stage(nc, K, name, items, s_sb, pt_sb, width):
    with Stage(nc, name, "scored", "masked", "maxed", "exped", "turned", "copied", "mixed", "normed", "v",
               "r") as st:
        sem = st.sem

        @st.block.tensor
        def _(pe):
            def mix(i):
                it = items[i]
                nk = len(it.values)
                pe.wait_ge(sem["exped"], i + 1)
                if i >= 1:
                    pe.wait_ge(sem["copied"], i)
                for j in range(nk):
                    m = nc.tensor.transpose(K.psum[:, 3 + j // 4, (j % 4) * P:(j % 4 + 1) * P],
                                            s_sb[:, i % 2, j * P:(j + 1) * P], K.ident[:])
                m.then_inc(sem["turned"], 1)
                pe.wait_ge(sem["copied"], i + 1)
                if i >= 1:
                    pe.wait_ge(sem["normed"], i)
                for j in range(nk):
                    m = nc.tensor.matmul(K.psum[:, 6, :HD], pt_sb[:, j * P:(j + 1) * P], it.values[j],
                                         start=(j == 0), stop=(j == nk - 1))
                m.then_inc(sem["mixed"], 1)

            for i, it in enumerate(items):
                if i >= 1:
                    pe.wait_ge(sem["masked"], i)
                for b, (q, k, n, col, mask) in enumerate(it.segs):
                    m = nc.tensor.matmul(K.psum[:, b, :n], q, k, start=True, stop=True)
                m.then_inc(sem["scored"], 1)
                if i >= 1:
                    mix(i - 1)
            mix(len(items) - 1)

        @st.block.vector
        def _(dve):
            link = Chain(dve, sem["v"])

            def norm(i):
                dve.wait_ge(sem["mixed"], i + 1)
                dve.wait_ge(sem["exped"], i + 1)
                link(nc.vector.reciprocal(K.stat[:, 4 + i % 2:5 + i % 2], K.stat[:, 2 + i % 2:3 + i % 2]))
                nc.vector.tensor_scalar(items[i].out, K.psum[:, 6, :HD], K.stat[:, 4 + i % 2:5 + i % 2], None,
                                        ALU.mult).then_inc(sem["normed"], 1)

            for i, it in enumerate(items):
                dve.wait_ge(sem["scored"], i + 1)
                if i >= 2:
                    dve.wait_ge(sem["turned"], i - 1)
                for b, (q, k, n, col, mask) in enumerate(it.segs):
                    to = s_sb[:, i % 2, col:col + n]
                    if mask is None:
                        m = nc.vector.tensor_scalar(to, K.psum[:, b, :n], HD ** -0.5, None, ALU.mult)
                    else:
                        m = nc.vector.scalar_tensor_tensor(to, K.psum[:, b, :n], HD ** -0.5, mask, ALU.mult, ALU.add)
                m.then_inc(sem["masked"], 1)
                dve.wait_ge(sem["masked"], i + 1)
                n_all = len(it.values) * P
                nc.vector.tensor_reduce(K.stat[:, i % 2:i % 2 + 1], s_sb[:, i % 2, :n_all], AX.X, ALU.max,
                                        negate=True).then_inc(sem["maxed"], 1)
                if i >= 1:
                    norm(i - 1)
            norm(len(items) - 1)

        @st.block.scalar
        def _(act):
            for i, it in enumerate(items):
                n_all = len(it.values) * P
                act.wait_ge(sem["maxed"], i + 1)
                if i >= 2:
                    act.wait_ge(sem["normed"], i - 1)
                nc.scalar.activation(s_sb[:, i % 2, :n_all], s_sb[:, i % 2, :n_all], ACT.Exp,
                                     bias=K.stat[:, i % 2:i % 2 + 1],
                                     accum_out=K.stat[:, 2 + i % 2:3 + i % 2]).then_inc(sem["exped"], 1)
                act.wait_ge(sem["turned"], i + 1)
                if i >= 1:
                    act.wait_ge(sem["mixed"], i)
                for b in range(0, len(it.values), 4):
                    n = min(4, len(it.values) - b) * P
                    m = nc.scalar.activation(pt_sb[:, b * P:b * P + n], K.psum[:, 3 + b // 4, :n], ACT.Copy)
                m.then_inc(sem["copied"], 1)


def turn_stage(nc, K, name, jobs, emit):
    groups = [jobs[i:i + 4] for i in range(0, len(jobs), 4)]
    with Stage(nc, name, "turned", "taken") as st:
        sem = st.sem

        @st.block.tensor
        def _(pe):
            for g, group in enumerate(groups):
                if g >= 4:
                    pe.wait_ge(sem["taken"], g - 3)
                for j, x in enumerate(group):
                    m = nc.tensor.transpose(K.psum[:, g % 4, j * P:(j + 1) * P], x, K.ident[:])
                m.then_inc(sem["turned"], 1)

        @st.block.vector
        def _(dve):
            for g, group in enumerate(groups):
                dve.wait_ge(sem["turned"], g + 1)
                emit(g, K.psum[:, g % 4, :len(group) * P]).then_inc(sem["taken"], 1)


def first_block(nc, K, a, x1):
    top = ExitStack()

    def sb(name, shape, stack=top):
        return stack.enter_context(nc.sbuf_tensor(name, shape, F32))

    h = sb("h1", [P, KD, S])
    K.gdn_gain = sb("gdn_gain", [P, S])
    load_stage(nc, "lx", [(x1[:], a["xT"]), (K.gdn_gain[:], a["gdn_gain"])])
    norm_stage(nc, K, "n1", lambda k: x1[:, k], S, lambda k: h[:, k], K.vec_norm, square=K.tmp)
    gatedA = sb("gatedA", [P, 4, S])
    gatedB = sb("gatedB", [P, 4, S])
    with ExitStack() as ph:
        qk = sb("qk", [P, 24, S], ph)
        v = sb("v", [P, 3, TT, S], ph)
        with ExitStack() as ph2:
            rings(nc, K, ph2, "a", vring=True)
            project_feature(nc, K, "pqk", a["w1f"], 24, lambda k: h[:, k], [(0, S)],
                            lambda t, g, at, n, ps, link: nc.scalar.activation(qk[:, t], ps, ACT.Copy))
            project_token(nc, K, "pv", lambda w: a["w1v"][w], 3, lambda k: h[:, k], range(TT),
                          lambda w, t, ps: nc.scalar.activation(v[:, w, t], ps, ACT.Copy))
        with ExitStack() as ph2:
            mask0 = sb("mask0", [P, 2 * P], ph2)
            mask1 = sb("mask1", [P, 4 * P], ph2)
            mask2 = sb("mask2", [P, 4 * P], ph2)
            cos, sin = sb("cos1", [P, S], ph2), sb("sin1", [P, S], ph2)
            load_stage(nc, "lm", [(mask0[:], a["mask0"]), (mask1[:], a["mask1"]), (mask2[:], a["mask2"]),
                                  (cos[:], a["cos1"]), (sin[:], a["sin1"])])
            rope_stage(nc, K, "r1", [qk[:, t] for t in range(24)], S, cos[:], sin[:])
            o = sb("o_dsa", [P, TT, S], ph2)
            s_sb = sb("s_sb", [P, 2, 10 * P], ph2)
            pt_sb = sb("pt_sb", [P, 10 * P], ph2)
            items = []
            for hh in range(8):
                m, r = hh // 2, (hh % 2) * HD
                for t in range(TT):
                    lo = max(0, t - 1)
                    n0, n1 = (t + 1 - lo) * P, (t + 1) * P
                    segs, vals, col = [], [], 0
                    for g, (k0, n, mask) in enumerate([(lo, n0, mask0[:, 2 * P - n0:]),
                                                       (0, n1, mask1[:, 4 * P - n1:]),
                                                       (0, n1, mask2[:, 4 * P - n1:])]):
                        segs.append((qk[r:r + HD, 8 * g + m, t * P:(t + 1) * P],
                                     qk[r:r + HD, 8 * g + 4 + m, k0 * P:k0 * P + n], n, col, mask))
                        vals += [v[:, g, k0 + j, hh * HD:(hh + 1) * HD] for j in range(n // P)]
                        col += n
                    items.append(Item(segs=segs, values=vals, out=o[:, t, hh * HD:(hh + 1) * HD]))
            attention_stage(nc, K, "dsa", items, s_sb, pt_sb, 10 * P)
            rings(nc, K, ph2, "z")
            z = sb("z_dsa", [P, 4, S], ph2)
            project_feature(nc, K, "pz", a["w1f"], 4, lambda k: h[:, k], [(0, S)],
                            lambda t, g, at, n, ps, link: nc.scalar.activation(z[:, t], ps, ACT.Silu), base=24)
            turn_stage(nc, K, "to1", [o[:, t, m * P:(m + 1) * P] for m in range(4) for t in range(TT)],
                       lambda g, ps: nc.vector.tensor_tensor(gatedA[:, g], ps, z[:, g], ALU.mult))
    gated_delta(nc, K, a, h, gatedB)
    with ExitStack() as ph:
        rings(nc, K, ph, "u")
        merged = sb("merged", [P, KD, S], ph)
        gate = sb("gate", [P, 2, S], ph)
        merge_stage(nc, K, a, h, gatedA, gatedB, merged)
        out_stage(nc, K, "po1", a["wo1"], lambda k: merged[:, k], x1, None)
    norm_stage(nc, K, "n2", lambda k: x1[:, k], S, lambda k: x1[:, k], K.vec_fnorm, square=K.tmp)
    top.close()


def rings(nc, K, stack, name, vring=False, n=4):
    K.nring = n
    K.wring = stack.enter_context(nc.sbuf_tensor(f"wring_{name}", [P, n, KD * P], F32))
    if vring:
        K.vring = stack.enter_context(nc.sbuf_tensor(f"vring_{name}", [P, 2, KD * 512], F32))


def merge_stage(nc, K, a, h, gatedA, gatedB, merged):
    def src(j, k):
        return h[:, k] if j % 2 == 0 else (gatedA, gatedB)[j // 2][:, k]

    with Stage(nc, "merge", "w0", "w1", "w2", "w3", "done", "gated", "taken", "v") as st:
        sem = st.sem

        def slot(j, k):
            return K.wring[:, j, k * P:(k + 1) * P]

        @st.block.sync
        def _(sync):
            for n in range(KD):
                for j in range(4):
                    i = 4 * n + j
                    if i >= 4:
                        sync.wait_ge(sem["done"], i - 3)
                    if j % 2 == 0:
                        sync.dma_start(K.wring[:, j], a["w1f"][44 + 8 * (j // 2) + n].rearrange("p k n -> p (k n)")).then_inc(sem[f"w{j}"], 16)
                    else:
                        sync.dma_start(K.wring[:, j, :4 * P], (a["upa"], a["upb"])[j // 2][n].rearrange("p k n -> p (k n)")).then_inc(sem[f"w{j}"], 16)

        @st.block.tensor
        def _(pe):
            for i in range(4 * KD):
                j = i % 4
                pe.wait_ge(sem[f"w{j}"], 16 * (i // 4 + 1))
                if i >= 8:
                    pe.wait_ge(sem["taken"], i // 4 - 1)
                nk = KD if j % 2 == 0 else 4
                for k in range(nk):
                    m = nc.tensor.matmul(K.psum[:, i % 8], slot(j, k), src(j, k), start=(k == 0), stop=(k == nk - 1))
                m.then_inc(sem["done"], 1)

        @st.block.scalar
        def _(act):
            for n in range(KD):
                for g in range(2):
                    act.wait_ge(sem["done"], 4 * n + 2 * g + 1)
                    if n >= 1:
                        act.wait_ge(sem["taken"], n)
                    nc.scalar.activation(K.tmp[:, g], K.psum[:, (4 * n + 2 * g) % 8], ACT.Sigmoid).then_inc(sem["gated"], 1)

        @st.block.vector
        def _(dve):
            link = Chain(dve, sem["v"])
            for n in range(KD):
                dve.wait_ge(sem["done"], 4 * n + 4)
                dve.wait_ge(sem["gated"], 2 * n + 2)
                b = (4 * n) % 8
                nc.vector.tensor_tensor(merged[:, n], K.tmp[:, 0], K.psum[:, b + 1], ALU.mult)
                link(nc.vector.tensor_tensor(K.rstd[:, 0], K.tmp[:, 1], K.psum[:, b + 3], ALU.mult))
                nc.vector.tensor_tensor(merged[:, n], merged[:, n], K.rstd[:, 0], ALU.add).then_inc(sem["taken"], 1)
                dve.wait_ge(sem["taken"], n + 1)


def out_stage(nc, K, name, weights, src, x, gain):
    ns = K.nring
    wring = K.wring[:].rearrange("p s (k n) -> p s k n", k=KD)
    with Stage(nc, name, *[f"w{j}" for j in range(ns)], "done", "taken") as st:
        sem = st.sem

        @st.block.sync
        def _(sync):
            for t in range(KD):
                if t >= ns:
                    sync.wait_ge(sem["done"], t - ns + 1)
                sync.dma_start(wring[:, t % ns], weights[t]).then_inc(sem[f"w{t % ns}"], 16)

        @st.block.tensor
        def _(pe):
            for t in range(KD):
                pe.wait_ge(sem[f"w{t % ns}"], 16 * (t // ns + 1))
                if t >= 4:
                    pe.wait_ge(sem["taken"], t - 3)
                for k in range(KD):
                    m = nc.tensor.matmul(K.psum[:, t % 4], wring[:, t % ns, k], src(k), start=(k == 0), stop=(k == KD - 1))
                m.then_inc(sem["done"], 1)

        @st.block.vector
        def _(dve):
            for t in range(KD):
                dve.wait_ge(sem["done"], t + 1)
                if gain is None:
                    m = nc.vector.tensor_tensor(x[:, t], K.psum[:, t % 4], x[:, t], ALU.add)
                else:
                    m = nc.vector.scalar_tensor_tensor(x[:, t], K.psum[:, t % 4], gain[:, t:t + 1], x[:, t], ALU.mult, ALU.add)
                m.then_inc(sem["taken"], 1)


def over_heads(ap, n=HD):
    shape = list(ap.shape) + [n]
    return ap.unsqueeze(len(ap.shape)).broadcast_to(shape)


def over_rows(ap, n):
    return ap.unsqueeze(1).broadcast_to([ap.shape[0], n] + list(ap.shape[1:]))


def invert_stage(nc, K, name, at, xt, n_batch, upper, work, lanes=4):
    bt, xs, ys = work[:, 0], work[:, 1], work[:, 2]
    steps = [(lanes * g + lane, lv, lane) for g in range(n_batch // lanes) for lv in range(LEVELS) for lane in range(lanes)]
    with Stage(nc, name, "between", "y", "ycopied", "xy", "updated") as st:
        sem = st.sem

        @st.block.gpsimd
        def _(pool):
            for s, (b, lv, lane) in enumerate(steps):
                if s >= lanes:
                    pool.wait_ge(sem["y"], s - lanes + 1)
                mask = K.level[:, (LEVELS if upper(b) else 0) + lv]
                nc.gpsimd.tensor_tensor(bt[:, lane], at[:, b], over_rows(mask, 4), ALU.mult).then_inc(sem["between"], 1)

        @st.block.tensor
        def _(pe):
            def products(s):
                b, lv, lane = steps[s]
                pe.wait_ge(sem["ycopied"], s + 1)
                if s >= 2:
                    pe.wait_ge(sem["updated"], s - 1)
                for i in range(4):
                    x_t = K.ident[:] if lv == 0 else xt[:, b, i]
                    nc.tensor.matmul(K.psum[:, 2 + 2 * (s % 2), i * P:(i + 1) * P], x_t, ys[:, lane, i], start=True, stop=True)
                    m = nc.tensor.matmul(K.psum[:, 3 + 2 * (s % 2), i * P:(i + 1) * P], ys[:, lane, i], x_t, start=True, stop=True)
                m.then_inc(sem["xy"], 1)

            for s, (b, lv, lane) in enumerate(steps):
                pe.wait_ge(sem["between"], s + 1)
                if s >= lanes:
                    pe.wait_ge(sem["updated"], s - lanes + 1)
                if s >= 2:
                    pe.wait_ge(sem["ycopied"], s - 1)
                for i in range(4):
                    x = K.ident[:] if lv == 0 else xs[:, lane, i]
                    m = nc.tensor.matmul(K.psum[:, s % 2, i * P:(i + 1) * P], bt[:, lane, i], x, start=True, stop=True)
                m.then_inc(sem["y"], 1)
                if s >= 1:
                    products(s - 1)
            products(len(steps) - 1)

        @st.block.scalar
        def _(act):
            for s, (b, lv, lane) in enumerate(steps):
                act.wait_ge(sem["y"], s + 1)
                if s >= lanes:
                    act.wait_ge(sem["xy"], s - lanes + 1)
                nc.scalar.activation(ys[:, lane], K.psum[:, s % 2].rearrange("p (i n) -> p i n", i=4), ACT.Copy).then_inc(sem["ycopied"], 1)

        @st.block.vector
        def _(dve):
            for s, (b, lv, lane) in enumerate(steps):
                dve.wait_ge(sem["xy"], s + 1)
                eye = over_rows(K.ident[:], 4)
                xy = K.psum[:, 2 + 2 * (s % 2)].rearrange("p (i n) -> p i n", i=4)
                yx = K.psum[:, 3 + 2 * (s % 2)].rearrange("p (i n) -> p i n", i=4)
                nc.vector.tensor_tensor(xs[:, lane], eye if lv == 0 else xs[:, lane], xy, ALU.subtract)
                nc.vector.tensor_tensor(xt[:, b], eye if lv == 0 else xt[:, b], yx, ALU.subtract).then_inc(sem["updated"], 1)


def head_norm_stage(nc, K, name, x, nt, nh, gain, square, stat, bias=None, eps=None):
    with Stage(nc, name, "squared", "summed", "rooted", "v") as st:
        sem = st.sem

        @st.block.scalar
        def _(act):
            for t in range(nt):
                nc.scalar.activation(square[:, t], x[:, t], ACT.Square).then_inc(sem["squared"], 1)
            act.wait_ge(sem["summed"], 1)
            nc.scalar.activation(stat, stat, ACT.Ln, scale=1.0 / HD, bias=K.eps if eps is None else eps).then_inc(sem["rooted"], 1)
            act.wait_ge(sem["rooted"], 1)
            nc.scalar.activation(stat, stat, ACT.Exp, scale=-0.5).then_inc(sem["rooted"], 1)

        @st.block.vector
        def _(dve):
            link = Chain(dve, sem["v"])
            dve.wait_ge(sem["squared"], nt)
            nc.vector.tensor_reduce(stat, square.rearrange("p t (h d) -> p (t h) d", d=HD), AX.X, ALU.add).then_inc(sem["summed"], 1)
            dve.wait_ge(sem["rooted"], 2)
            for t in range(nt):
                xh = x[:, t].rearrange("p (h d) -> p h d", d=HD)
                link(nc.vector.tensor_tensor(xh, xh, over_heads(stat[:, t * nh:(t + 1) * nh]), ALU.mult))
                link(nc.vector.tensor_tensor(x[:, t], x[:, t], gain, ALU.mult))
                if bias is not None:
                    link(nc.vector.tensor_tensor(x[:, t], x[:, t], bias, ALU.add))


def l2_stage(nc, K, name, tiles, n, gains, mean=1.0, floor=None):
    with Stage(nc, name, "squared", "summed", "logged", "rooted", "inverse", "v") as st:
        sem = st.sem

        @st.block.scalar
        def _(act):
            def root(t):
                r = K.rstd[:, t % 2, :n(t)]
                if t >= 2:
                    act.wait_ge(sem["v"], t - 1)
                if floor is not None:
                    act.wait_ge(sem["logged"], t + 1)
                    nc.scalar.activation(r, r, ACT.Sqrt).then_inc(sem["rooted"], 1)
                    return
                act.wait_ge(sem["summed"], t + 1)
                nc.scalar.activation(r, K.psum[:, t % 4, :n(t)], ACT.Ln, scale=mean, bias=K.eps).then_inc(sem["logged"], 1)
                act.wait_ge(sem["logged"], t + 1)
                nc.scalar.activation(r, r, ACT.Exp, scale=-0.5).then_inc(sem["rooted"], 1)

            for t, x in enumerate(tiles):
                if t >= 2:
                    act.wait_ge(sem["summed"], t - 1)
                nc.scalar.activation(K.tmp[:, t % 2, :n(t)], x, ACT.Square).then_inc(sem["squared"], 1)
                if t >= 1:
                    root(t - 1)
            root(len(tiles) - 1)

        @st.block.tensor
        def _(pe):
            for t, x in enumerate(tiles):
                pe.wait_ge(sem["squared"], t + 1)
                if t >= 4:
                    pe.wait_ge(sem["logged"], t - 3)
                nc.tensor.matmul(K.psum[:, t % 4, :n(t)], K.head_ones[:], K.tmp[:, t % 2, :n(t)], start=True, stop=True).then_inc(sem["summed"], 1)

        @st.block.vector
        def _(dve):
            for t, x in enumerate(tiles):
                r = K.rstd[:, t % 2, :n(t)]
                if floor is not None:
                    dve.wait_ge(sem["summed"], t + 1)
                    nc.vector.tensor_scalar(r, K.psum[:, t % 4, :n(t)], floor, None, ALU.max).then_inc(sem["logged"], 1)
                dve.wait_ge(sem["rooted"], t + 1)
                if floor is not None:
                    nc.vector.reciprocal(r, r).then_inc(sem["inverse"], 1)
                    dve.wait_ge(sem["inverse"], t + 1)
                nc.vector.scalar_tensor_tensor(x, r, gains[t], x, ALU.mult, ALU.mult).then_inc(sem["v"], 1)


def gated_delta(nc, K, a, h, gatedB):
    ph = ExitStack()

    def sb(name, shape, stack=ph):
        return stack.enter_context(nc.sbuf_tensor(name, shape, F32))

    at, xt, attn = sb("g_at", [P, 8, 4, P]), sb("g_xt", [P, 8, 4, P]), sb("g_attn", [P, 8, 4, P])
    k_decay, v_beta = sb("g_kdecay", [P, TT, S]), sb("g_vbeta", [P, TT, S])
    q_e, kb_e, row_e = sb("g_qe", [P, 4, S]), sb("g_kbe", [P, 4, S]), sb("g_rowe", [P, 4, S])
    z = sb("g_z", [P, 4, S])
    ba = sb("g_ba", [P, TT, 16])
    g, beta, Gt, g_scr = sb("g_g", [P, TT, 8]), sb("g_beta", [P, TT, 8]), sb("g_G", [P, TT * 8]), sb("g_scr", [P, 2, TT * 8])
    with ExitStack() as p2:
        qkv = sb("g_qkv", [P, 12, S], p2)
        with ExitStack() as p3:
            rings(nc, K, p3, "g", n=3)
            K.vring = p3.enter_context(nc.sbuf_tensor("vring_g", [P, 2, KD * 16], F32))
            x_c = sb("g_xc", [P, 2, S + 3], p3)
            with Stage(nc, "gz", "m") as st:
                @st.block.vector
                def _(dve):
                    nc.vector.memset(x_c[:, :, 0:3], 0.0)

            conv_stage(nc, K, a, h, x_c, qkv)
            project_feature(nc, K, "gpz", a["w1f"], 4, lambda k: h[:, k], [(0, S)],
                            lambda t, g_, at_, n, ps, link: nc.scalar.activation(z[:, t], ps, ACT.Silu), base=40)
            project_token(nc, K, "gba", lambda w: a["w1ba"], 1, lambda k: h[:, k], range(TT),
                          lambda w, t, ps: nc.scalar.activation(ba[:, t], ps, ACT.Copy), width=16)
        l2_stage(nc, K, "gl2", [qkv[:, t] for t in range(8)], lambda t: S, [HD ** -0.5] * 4 + [1.0] * 4)

        with Stage(nc, "gg", "v", "x0", "x", "e") as st:
            sem = st.sem
            x, y = g_scr[:, 0].rearrange("p (t h) -> p t h", h=8), g_scr[:, 1].rearrange("p (t h) -> p t h", h=8)

            @st.block.vector
            def _(dve):
                link = Chain(dve, sem["v"])
                link(nc.vector.tensor_tensor(x, ba[:, :, 8:16], over_rows(K.dt_bias[:], TT), ALU.add))
                nc.vector.tensor_tensor(y, ba[:, :, 8:16], over_rows(K.dt_bias[:], TT), ALU.add).then_inc(sem["x0"], 1)
                nc.vector.tensor_scalar(x, x, 0.0, None, ALU.max).then_inc(sem["x"], 1)
                dve.wait_ge(sem["x"], 1)
                dve.wait_ge(sem["e"], 5)
                link(nc.vector.tensor_tensor(x, x, y, ALU.add))
                link(nc.vector.tensor_tensor(g[:], x, over_rows(K.a_log[:], TT), ALU.mult))
                link(nc.vector.tensor_scalar(g[:], g[:], -1.0, None, ALU.mult))

            @st.block.scalar
            def _(act):
                nc.scalar.activation(beta[:], ba[:, :, 0:8], ACT.Sigmoid).then_inc(sem["e"], 1)
                act.wait_ge(sem["x0"], 1)
                nc.scalar.activation(K.a_log[:], K.a_log[:], ACT.Exp).then_inc(sem["e"], 1)
                nc.scalar.activation(y, y, ACT.Abs).then_inc(sem["e"], 1)
                act.wait_ge(sem["e"], 3)
                nc.scalar.activation(y, y, ACT.Exp, scale=-1.0).then_inc(sem["e"], 1)
                act.wait_ge(sem["e"], 4)
                nc.scalar.activation(y, y, ACT.Ln, bias=1.0).then_inc(sem["e"], 1)

        p3 = ExitStack()
        wide = sb("g_wide", [P, 2, TT * 8, HD], p3)
        with Stage(nc, "gc", "wide", "sums", "rows", "betas", "v", "exped", "kb", "d") as st:
            sem = st.sem

            @st.block.gpsimd
            def _(pool):
                nc.gpsimd.tensor_copy(wide[:, 0], over_heads(g[:].rearrange("p t h -> p (t h)"))).then_inc(sem["wide"], 1)
                nc.gpsimd.tensor_copy(wide[:, 1], over_heads(beta[:].rearrange("p t h -> p (t h)"))).then_inc(sem["wide"], 1)

            def pair(which, c, m):
                return wide[:, which, 8 * c + 2 * m:8 * c + 2 * m + 2].rearrange("p a b -> p (a b)")

            @st.block.tensor
            def _(pe):
                pe.wait_ge(sem["wide"], 2)
                gf = g[:].rearrange("p t h -> p (t h)")
                nc.tensor.matmul(K.psum[:, 0, 0:32], K.upto[:], gf, start=True, stop=True)
                nc.tensor.matmul(K.psum[:, 0, 32:64], K.ones[:], gf, start=True, stop=True).then_inc(sem["sums"], 1)
                for m in range(4):
                    for c in range(TT):
                        ins = nc.tensor.matmul(K.psum[:, 1 + m % 3, c * P:(c + 1) * P], pair(0, c, m),
                                               K.upto[:], start=True, stop=True) if m < 3 else None
                    if m < 3:
                        ins.then_inc(sem["rows"], 1)
                for m in range(4):
                    for c in range(TT):
                        ins = nc.tensor.matmul(K.psum[:, 4 + m, c * P:(c + 1) * P], pair(1, c, m),
                                               K.ident[:], start=True, stop=True)
                    ins.then_inc(sem["betas"], 1)
                pe.wait_ge(sem["exped"], 1)
                for c in range(TT):
                    ins = nc.tensor.matmul(K.psum[:, 1, c * P:(c + 1) * P], pair(0, c, 3), K.upto[:], start=True, stop=True)
                ins.then_inc(sem["rows"], 1)

            @st.block.scalar
            def _(act):
                for m in range(4):
                    act.wait_ge(sem["rows"], m + 1)
                    nc.scalar.activation(row_e[:, m], K.psum[:, 1 + m % 3], ACT.Exp).then_inc(sem["exped"], 1)
                act.wait_ge(sem["d"], 1)
                nc.scalar.activation(g_scr[:, 0], g_scr[:, 0], ACT.Exp).then_inc(sem["exped"], 1)

            @st.block.vector
            def _(dve):
                link = Chain(dve, sem["v"])
                dve.wait_ge(sem["sums"], 1)
                link(nc.vector.tensor_copy(Gt[:], K.psum[:, 0, 0:32]))
                nc.vector.tensor_tensor(g_scr[:, 0], K.psum[:, 0, 32:64], Gt[:], ALU.subtract).then_inc(sem["d"], 1)
                for m in range(4):
                    dve.wait_ge(sem["betas"], m + 1)
                    link(nc.vector.tensor_tensor(kb_e[:, m], qkv[:, 4 + m], K.psum[:, 4 + m], ALU.mult))
                    dve.wait_ge(sem["exped"], m + 1)
                    link(nc.vector.tensor_tensor(q_e[:, m], qkv[:, m], row_e[:, m], ALU.mult))

        p3.close()

        kd = g_scr[:, 0].rearrange("p (t h) -> p t h", h=8)
        turn_stage(nc, K, "gtk", [qkv[:, 4 + m, c * P:(c + 1) * P] for c in range(TT) for m in range(4)],
                   lambda c, ps: nc.vector.tensor_tensor(k_decay[:, c].rearrange("p (h d) -> p h d", d=HD),
                                                         ps.rearrange("p (h d) -> p h d", d=HD), over_heads(kd[:, c]), ALU.mult))
        turn_stage(nc, K, "gtv", [qkv[:, 8 + m, c * P:(c + 1) * P] for c in range(TT) for m in range(4)],
                   lambda c, ps: nc.vector.tensor_tensor(v_beta[:, c].rearrange("p (h d) -> p h d", d=HD),
                                                         ps.rearrange("p (h d) -> p h d", d=HD), over_heads(beta[:, c]), ALU.mult))

        dec = sb("g_dec", [P, 2, 4, P], p2)
        dec2 = sb("g_dec2", [P, 2, 2, 4, P], p2)
        with Stage(nc, "gm", "rowed", "prods", "diffed", "exped", "masked", "used", "v") as st:
            sem = st.sem
            batches = [(c, half) for c in range(TT) for half in range(2)]

            @st.block.tensor
            def _(pe):
                for b, (c, half) in enumerate(batches):
                    if b >= 1:
                        pe.wait_ge(sem["diffed"], b)
                    for i in range(4):
                        hh = 2 * i + half
                        ins = nc.tensor.matmul(K.psum[:, 0, i * P:(i + 1) * P], g[:, c, hh:hh + 1].broadcast_to([P, P]),
                                               K.upto[:], start=True, stop=True)
                    ins.then_inc(sem["rowed"], 1)
                    if b >= 2:
                        pe.wait_ge(sem["used"], b - 1)
                    for i in range(4):
                        hh = 2 * i + half
                        m, r = hh // 2, (hh % 2) * HD
                        kk = qkv[r:r + HD, 4 + m, c * P:(c + 1) * P]
                        nc.tensor.matmul(K.psum[:, 1 + 2 * (b % 2), i * P:(i + 1) * P], kk, kb_e[r:r + HD, m, c * P:(c + 1) * P], start=True, stop=True)
                        ins = nc.tensor.matmul(K.psum[:, 2 + 2 * (b % 2), i * P:(i + 1) * P], kk, qkv[r:r + HD, m, c * P:(c + 1) * P], start=True, stop=True)
                    ins.then_inc(sem["prods"], 1)

            @st.block.vector
            def _(dve):
                def use(b):
                    dve.wait_ge(sem["prods"], b + 1)
                    dve.wait_ge(sem["masked"], b + 1)
                    nc.vector.tensor_tensor(at[:, b], K.psum[:, 1 + 2 * (b % 2)].rearrange("p (i n) -> p i n", i=4), dec2[:, b % 2, 0], ALU.mult)
                    nc.vector.tensor_tensor(attn[:, b], K.psum[:, 2 + 2 * (b % 2)].rearrange("p (i n) -> p i n", i=4), dec2[:, b % 2, 1], ALU.mult).then_inc(sem["used"], 1)

                for b, (c, half) in enumerate(batches):
                    dve.wait_ge(sem["rowed"], b + 1)
                    if b >= 2:
                        dve.wait_ge(sem["masked"], b - 1)
                    for i in range(4):
                        hh = 8 * c + 2 * i + half
                        ins = nc.vector.tensor_scalar(dec[:, b % 2, i], K.psum[:, 0, i * P:(i + 1) * P], Gt[:, hh:hh + 1], 0.0, ALU.subtract, ALU.min)
                    ins.then_inc(sem["diffed"], 1)
                    if b >= 1:
                        use(b - 1)
                use(len(batches) - 1)

            @st.block.scalar
            def _(act):
                for b in range(len(batches)):
                    act.wait_ge(sem["diffed"], b + 1)
                    nc.scalar.activation(dec[:, b % 2], dec[:, b % 2], ACT.Exp).then_inc(sem["exped"], 1)

            @st.block.gpsimd
            def _(pool):
                for b in range(len(batches)):
                    pool.wait_ge(sem["exped"], b + 1)
                    if b >= 2:
                        pool.wait_ge(sem["used"], b - 1)
                    nc.gpsimd.tensor_tensor(dec2[:, b % 2, 0], dec[:, b % 2], over_rows(K.before[:], 4), ALU.mult)
                    nc.gpsimd.tensor_tensor(dec2[:, b % 2, 1], dec[:, b % 2], over_rows(K.upto[:], 4), ALU.mult).then_inc(sem["masked"], 1)

        with Stage(nc, "gk", "v") as st:
            @st.block.vector
            def _(dve):
                for m in range(4):
                    nc.vector.tensor_tensor(kb_e[:, m], kb_e[:, m], row_e[:, m], ALU.mult)
    with ExitStack() as p2:
        work = sb("g_work", [P, 3, 4, 4, P], p2)
        invert_stage(nc, K, "gi", at, xt, 8, lambda b: False, work)
    o = sb("g_o", [P, TT, S])
    with ExitStack() as p2:
        state = sb("g_state", [P, 4, P], p2)
        zz, vn, upd = sb("g_zz", [P, S], p2), sb("g_vn", [P, S], p2), sb("g_upd", [P, 4, P], p2)
        with Stage(nc, "gs", "ks", "z", "vn", "vcopied", "out", "state", "v", "ocopied") as st:
            sem = st.sem

            @st.block.tensor
            def _(pe):
                for c in range(TT):
                    pe.wait_ge(sem["state"], c + 1)
                    for m in range(4):
                        ins = nc.tensor.matmul(K.psum[:, 0, m * P:(m + 1) * P], kb_e[:, m, c * P:(c + 1) * P], state[:, m], start=True, stop=True)
                    ins.then_inc(sem["ks"], 1)
                    pe.wait_ge(sem["z"], c + 1)
                    for hh in range(8):
                        ins = nc.tensor.matmul(K.psum[:, 1, hh * HD:(hh + 1) * HD], xt[:, 2 * c + hh % 2, hh // 2], zz[:, hh * HD:(hh + 1) * HD], start=True, stop=True)
                    ins.then_inc(sem["vn"], 1)
                    pe.wait_ge(sem["vcopied"], c + 1)
                    for m in range(4):
                        nc.tensor.matmul(K.psum[:, 3, m * P:(m + 1) * P], k_decay[:, c, m * P:(m + 1) * P], vn[:, m * P:(m + 1) * P], start=True, stop=True)
                    if c >= 1:
                        pe.wait_ge(sem["ocopied"], c)
                    for m in range(4):
                        nc.tensor.matmul(K.psum[:, 2, m * P:(m + 1) * P], q_e[:, m, c * P:(c + 1) * P], state[:, m], start=True, stop=False, skip_group_check=True)
                        for hh in (2 * m, 2 * m + 1):
                            ins = nc.tensor.matmul(K.psum[:, 2, hh * HD:(hh + 1) * HD], attn[:, 2 * c + hh % 2, hh // 2], vn[:, hh * HD:(hh + 1) * HD],
                                                   start=False, stop=(hh % 2 == 1), skip_group_check=True)
                    ins.then_inc(sem["out"], 1)

            @st.block.vector
            def _(dve):
                link = Chain(dve, sem["v"])
                nc.vector.memset(state[:], 0.0).then_inc(sem["state"], 1)
                for c in range(TT):
                    dve.wait_ge(sem["ks"], c + 1)
                    nc.vector.tensor_tensor(zz[:], v_beta[:, c], K.psum[:, 0], ALU.subtract).then_inc(sem["z"], 1)
                    dve.wait_ge(sem["out"], c + 1)
                    link(nc.vector.tensor_tensor(upd[:], K.psum[:, 3].rearrange("p (m n) -> p m n", m=4), over_rows(K.head_ones[:], 4), ALU.mult))
                    for m in range(4):
                        ins = nc.vector.scalar_tensor_tensor(state[:, m], state[:, m], row_e[:, m, c * P + P - 1:c * P + P], upd[:, m], ALU.mult, ALU.add)
                    ins.then_inc(sem["state"], 1)
                    dve.wait_ge(sem["state"], c + 2)

            @st.block.scalar
            def _(act):
                for c in range(TT):
                    act.wait_ge(sem["vn"], c + 1)
                    if c >= 1:
                        act.wait_ge(sem["out"], c)
                    nc.scalar.activation(vn[:], K.psum[:, 1], ACT.Copy).then_inc(sem["vcopied"], 1)
                    act.wait_ge(sem["out"], c + 1)
                    nc.scalar.activation(o[:, c], K.psum[:, 2], ACT.Copy).then_inc(sem["ocopied"], 1)
    with ExitStack() as p2:
        sq = sb("g_sq", [P, TT, S], p2)
        head_norm_stage(nc, K, "gn", o, TT, 8, K.gdn_gain[:], sq, g_scr[:, 1])
        turn_stage(nc, K, "gto", [o[:, c, m * P:(m + 1) * P] for m in range(4) for c in range(TT)],
                   lambda m, ps: nc.vector.tensor_tensor(gatedB[:, m], ps, z[:, m], ALU.mult))
    ph.close()


def conv_stage(nc, K, a, h, x_c, qkv):
    ns = K.nring
    wring = K.wring[:].rearrange("p s (k n) -> p s k n", k=KD)
    with Stage(nc, "gp", *[f"w{j}" for j in range(ns)], "done", "emptied", "convd", "silud", "v") as st:
        sem = st.sem

        @st.block.sync
        def _(sync):
            for t in range(12):
                if t >= ns:
                    sync.wait_ge(sem["done"], t - ns + 1)
                sync.dma_start(wring[:, t % ns], a["w1f"][28 + t]).then_inc(sem[f"w{t % ns}"], 16)

        @st.block.tensor
        def _(pe):
            for t in range(12):
                pe.wait_ge(sem[f"w{t % ns}"], 16 * (t // ns + 1))
                if t >= 4:
                    pe.wait_ge(sem["emptied"], t - 3)
                for k in range(KD):
                    m = nc.tensor.matmul(K.psum[:, t % 4], wring[:, t % ns, k], h[:, k], start=(k == 0), stop=(k == KD - 1))
                m.then_inc(sem["done"], 1)

        @st.block.scalar
        def _(act):
            def silu(t):
                act.wait_ge(sem["convd"], t + 1)
                nc.scalar.activation(qkv[:, t], qkv[:, t], ACT.Silu).then_inc(sem["silud"], 1)

            for t in range(12):
                act.wait_ge(sem["done"], t + 1)
                if t >= 2:
                    act.wait_ge(sem["convd"], t - 1)
                nc.scalar.activation(x_c[:, t % 2, 3:], K.psum[:, t % 4], ACT.Copy).then_inc(sem["emptied"], 1)
                if t >= 1:
                    silu(t - 1)
            silu(11)

        @st.block.vector
        def _(dve):
            link = Chain(dve, sem["v"])
            for t in range(12):
                dve.wait_ge(sem["emptied"], t + 1)
                link(nc.vector.tensor_scalar(qkv[:, t], x_c[:, t % 2, 0:S], K.conv[:, t, 0:1], None, ALU.mult))
                for j in range(1, 4):
                    m = nc.vector.scalar_tensor_tensor(qkv[:, t], x_c[:, t % 2, j:j + S], K.conv[:, t, j:j + 1], qkv[:, t], ALU.mult, ALU.add)
                    if j < 3:
                        link(m)
                m.then_inc(sem["convd"], 1)


NCH = TC
ORDER = (list(range(NCH)), list(range(CT))[::-1] + list(range(CT, NCH))[::-1])


def modulation_stage(nc, K, a, mod, gains):
    ns = K.nring
    wring = K.wring[:].rearrange("p s (k n) -> p s k n", k=KD)
    loops = 48 // ns
    with Stage(nc, "ada", *[f"w{j}" for j in range(ns)], "silud", "done", "v") as st:
        sem = st.sem

        @st.block.sync
        def _(sync):
            for j in range(ns):
                sync.dma_start(wring[:, j], a["w_ada"][j]).then_inc(sem[f"w{j}"], 16)
            with sync.Fori(0, loops - 1) as i:
                for j in range(ns):
                    sync.wait_ge(sem["done"], i * ns + (j + 1))
                    sync.dma_start(wring[:, j], a["w_ada"][bass.ds(i * ns + (ns + j), 1)].rearrange("o p k n -> (o p) k n")).then_inc(sem[f"w{j}"], 16)

        @st.block.scalar
        def _(act):
            nc.scalar.activation(K.cond, K.cond, ACT.Silu).then_inc(sem["silud"], 1)

        @st.block.tensor
        def _(pe):
            pe.wait_ge(sem["silud"], 1)
            with pe.Fori(0, loops) as i:
                for j in range(ns):
                    pe.wait_ge(sem[f"w{j}"], i * 16 + 16)
                    for k in range(KD):
                        m = nc.tensor.matmul(K.psum[:, 0, bass.ds(i * (2 * ns) + 2 * j, 2)], wring[:, j, k],
                                             K.cond[:, 2 * k:2 * k + 2], start=(k == 0), stop=(k == KD - 1))
                    m.then_inc(sem["done"], 1)

        @st.block.vector
        def _(dve):
            link = Chain(dve, sem["v"])
            dve.wait_ge(sem["done"], 48)
            link(nc.vector.tensor_tensor(mod[:], K.psum[:, 0, 0:96].rearrange("p (t c) -> p t c", c=2), over_heads(K.b_ada, 2), ALU.add))
            for j, (at, who, norm) in enumerate([(8, 0, K.norm1), (8, 1, K.norm1), (32, 0, K.norm2)]):
                nc.vector.scalar_tensor_tensor(gains[:, j], mod[:, at:at + 8, who], 1.0, norm, ALU.add, ALU.mult)


def running_sums(nc, K, dve, link, lw, cum, tiles):
    for t in tiles:
        link(nc.vector.tensor_tensor_scan(cum[:, t], K.reset[:], lw[:, t], 0.0, ALU.mult, ALU.add))


def chunks(ap):
    return ap.rearrange("p (c n) -> p c n", n=P)


def hgrn(nc, K, a, h2, mix):
    ph = ExitStack()

    def sb(name, shape, stack=ph):
        return stack.enter_context(nc.sbuf_tensor(name, shape, F32))

    def proj(w, t, ps):
        return nc.scalar.activation(ig[:, t], ps, ACT.Copy)

    ig = sb("h_ig", [P, NCH, 512])
    acc = sb("h_acc", [P, 2, 2, TT, P])
    q_in = sb("h_qin", [P, 4, S])
    k_outT = sb("h_koutT", [P, NCH, 4 * P])
    e_tot = sb("h_etot", [P, 4, NCH])
    with ExitStack() as p2:
        q = sb("h_q", [P, 2, T2], p2)
        f = sb("h_f", [P, 4, T2], p2)
        with ExitStack() as p3:
            rings(nc, K, p3, "h", vring=False, n=2)
            K.vring = p3.enter_context(nc.sbuf_tensor("vring_h", [P, 1, KD * 512], F32))

            def evac(t, g, at, n, ps, link):
                to = q[:, t] if t < 2 else f[:, t - 2]
                return nc.scalar.activation(to[:, at:at + n], ps, ACT.Copy)

            project_feature(nc, K, "hp", a["w2f"], 6, lambda k_: h2[:, k_], [(0, CTX), (CTX, S)], evac)
            project_token(nc, K, "ht", lambda w: a["w2t"][0], 1, lambda k_: h2[:, k_], range(NCH), proj)
        with ExitStack() as p3:
            k = sb("h_k", [P, 4, T2], p3)
            c = sb("h_c", [P, 4, T2], p3)
            e = sb("h_e", [P, 4, T2], p3)
            with Stage(nc, "hg", "l", "x", "v", "a", "b", "sig", "f", "logf") as st:
                sem = st.sem
                lb, oml = K.hlb[:, 0:4], K.hlb[:, 4:8]

                @st.block.scalar
                def _(act):
                    act.wait_ge(sem["l"], 1)
                    nc.scalar.activation(lb, lb, ACT.Exp).then_inc(sem["b"], 1)
                    for n in range(4):
                        nc.scalar.activation(e[:, n], f[:, n], ACT.Abs).then_inc(sem["a"], 1)
                    act.wait_ge(sem["a"], 4)
                    nc.scalar.activation(e[:], e[:], ACT.Exp, scale=-1.0).then_inc(sem["a"], 1)
                    act.wait_ge(sem["a"], 5)
                    nc.scalar.activation(e[:], e[:], ACT.Ln, bias=1.0).then_inc(sem["a"], 1)
                    act.wait_ge(sem["x"], 1)
                    nc.scalar.activation(k[:], k[:], ACT.Exp, scale=-1.0)
                    nc.scalar.activation(f[:], f[:], ACT.Exp).then_inc(sem["sig"], 1)
                    act.wait_ge(sem["f"], 1)
                    nc.scalar.activation(f[:], f[:], ACT.Ln, scale=8.0).then_inc(sem["logf"], 1)

                @st.block.vector
                def _(dve):
                    link = Chain(dve, sem["v"])
                    nc.vector.tensor_tensor(lb, lb, lb, ALU.subtract).then_inc(sem["l"], 1)
                    dve.wait_ge(sem["b"], 1)
                    link(nc.vector.reciprocal(oml, lb))
                    link(nc.vector.tensor_tensor(lb, lb, oml, ALU.mult))
                    link(nc.vector.tensor_tensor(lb, lb, lb, ALU.subtract))
                    link(nc.vector.tensor_scalar(oml, lb, -1.0, 1.0, ALU.mult, ALU.add))
                    dve.wait_ge(sem["a"], 6)
                    link(nc.vector.scalar_tensor_tensor(k[:], f[:], 0.0, e[:], ALU.max, ALU.add))
                    nc.vector.scalar_tensor_tensor(f[:], f[:], 0.0, e[:], ALU.min, ALU.subtract).then_inc(sem["x"], 1)
                    dve.wait_ge(sem["sig"], 1)
                    for n in range(4):
                        nc.vector.tensor_scalar(k[:, n], k[:, n], oml[:, n:n + 1], None, ALU.mult)
                        link(nc.vector.tensor_scalar(f[:, n], f[:, n], oml[:, n:n + 1], lb[:, n:n + 1], ALU.mult, ALU.add))
                    nc.vector.tensor_scalar(f[:], f[:], 1e-20, None, ALU.max).then_inc(sem["f"], 1)
                    dve.wait_ge(sem["logf"], 1)
                    link(nc.vector.tensor_scalar(f[:], f[:], -math.log(8.0), None, ALU.add))
                    running_sums(nc, K, dve, link, f, c, range(4))
                    for n in (2, 3):
                        link(nc.vector.tensor_copy(e_tot[:, n], chunks(c[:, n])[:, :, P - 1]))
                        nc.vector.tensor_copy(e_tot[:, n - 2], chunks(c[:, n - 2])[:, :, P - 1])
                        link(nc.vector.tensor_tensor(c[:, n], f[:, n], c[:, n], ALU.subtract))
                        link(nc.vector.tensor_tensor(chunks(c[:, n]), chunks(c[:, n]), over_heads(e_tot[:, n], P), ALU.add))

            with Stage(nc, "hd", "v", "d", "exped", "x") as st:
                sem = st.sem

                @st.block.vector
                def _(dve):
                    link = Chain(dve, sem["v"])
                    for n in range(4):
                        nc.vector.tensor_tensor(chunks(e[:, n]), over_heads(e_tot[:, n], P), chunks(c[:, n]), ALU.subtract).then_inc(sem["d"], 1)
                    for n in range(4):
                        dve.wait_ge(sem["exped"], 2 * n + 2)
                        nc.vector.tensor_tensor(e[:, n], k[:, n], e[:, n], ALU.mult)
                        nc.vector.tensor_tensor(q_in[:, n], q[:, n % 2, CTX:], q_in[:, n], ALU.mult)

                @st.block.scalar
                def _(act):
                    for n in range(4):
                        act.wait_ge(sem["d"], n + 1)
                        nc.scalar.activation(e[:, n], e[:, n], ACT.Exp).then_inc(sem["exped"], 1)
                        nc.scalar.activation(q_in[:, n], c[:, n, CTX:], ACT.Exp).then_inc(sem["exped"], 1)
                    act.wait_ge(sem["d"], 4)
                    nc.scalar.activation(e_tot[:], e_tot[:], ACT.Exp)

            turn_stage(nc, K, "hkt", [e[:, n, j * P:(j + 1) * P] for j in range(NCH) for n in range(4)],
                       lambda g, ps: nc.vector.tensor_copy(k_outT[:, g], ps))
            level_stage(nc, K, q, k, c, acc, e, f, sb, p3)
    o = sb("h_o", [P, TT, 256])
    with ExitStack() as p2:
        kv = sb("h_kv", [P, NCH, 4, P], p2)
        states = sb("h_states", [P, NCH, 4, P], p2)
        with Stage(nc, "hs", "kv", "masked", "state", "v", "out") as st:
            sem = st.sem

            @st.block.tensor
            def _(pe):
                for j in range(NCH):
                    if j >= 4:
                        pe.wait_ge(sem["masked"], j - 3)
                    for n in range(4):
                        ins = nc.tensor.matmul(K.psum[:, j % 4, n * P:(n + 1) * P], k_outT[:, j, n * P:(n + 1) * P],
                                               ig[:, j, (n % 2) * P:(n % 2 + 1) * P], start=True, stop=True)
                    ins.then_inc(sem["kv"], 1)
                pe.wait_ge(sem["state"], 1)
                for t in range(TT):
                    j = CT + t
                    for m in range(2):
                        for d in range(2):
                            nc.tensor.matmul(K.psum[:, 4 + t, m * P:(m + 1) * P], q_in[:, 2 * d + m, t * P:(t + 1) * P], states[:, j, 2 * d + m],
                                             start=(d == 0), stop=False, skip_group_check=True)
                        for par in range(2):
                            hh = 2 * m + par
                            ins = nc.tensor.matmul(K.psum[:, 4 + t, hh * HD:(hh + 1) * HD], acc[:, par, m, t], ig[:, j, hh * HD:(hh + 1) * HD],
                                                   start=False, stop=(par == 1), skip_group_check=True)
                    ins.then_inc(sem["out"], 1)

            @st.block.vector
            def _(dve):
                link = Chain(dve, sem["v"])
                for j in range(NCH):
                    dve.wait_ge(sem["kv"], j + 1)
                    nc.vector.tensor_tensor(kv[:, j], K.psum[:, j % 4].rearrange("p (n x) -> p n x", n=4), over_rows(K.head_ones[:], 4), ALU.mult).then_inc(sem["masked"], 1)
                dve.wait_ge(sem["masked"], NCH)
                for d in range(2):
                    link(nc.vector.memset(states[:, ORDER[d][0], 2 * d:2 * d + 2], 0.0))
                for i in range(NCH - 1):
                    for d in range(2):
                        j, nx = ORDER[d][i], ORDER[d][i + 1]
                        for m in range(2):
                            n = 2 * d + m
                            ins = nc.vector.scalar_tensor_tensor(states[:, nx, n], states[:, j, n], e_tot[:, n, j:j + 1], kv[:, j, n], ALU.mult, ALU.add)
                    if i < NCH - 2:
                        link(ins)
                ins.then_inc(sem["state"], 1)

            @st.block.scalar
            def _(act):
                for t in range(TT):
                    act.wait_ge(sem["out"], t + 1)
                    nc.scalar.activation(o[:, t], K.psum[:, 4 + t, 0:256], ACT.Copy)
        sq = sb("h_sq", [P, TT, 256], p2)
        stat = sb("h_stat", [P, 16], p2)
        head_norm_stage(nc, K, "hn", o, TT, 4, K.rows2[:, 0:256], sq, stat[:])
        gate_stage(nc, K, "hgt", o, lambda t: ig[:, CT + t, 256:512], ACT.Silu)
    turn_stage(nc, K, "hto", [o[:, t, m * P:(m + 1) * P] for m in range(2) for t in range(TT)],
               lambda m, ps: nc.vector.tensor_copy(mix[:, m], ps))
    ph.close()


def gate_stage(nc, K, name, o, gate, func):
    with Stage(nc, name, "g", "v") as st:
        @st.block.scalar
        def _(act):
            for t in range(TT):
                nc.scalar.activation(gate(t), gate(t), func).then_inc(st.sem["g"], 1)

        @st.block.vector
        def _(dve):
            for t in range(TT):
                dve.wait_ge(st.sem["g"], t + 1)
                nc.vector.tensor_tensor(o[:, t], o[:, t], gate(t), ALU.mult)


def level_stage(nc, K, q, k, c, acc, e, f, sb, stack):
    part = [x[:].rearrange("p n t -> p (n t)")[:, i * 2 * S:(i + 1) * 2 * S].rearrange("p (n t) -> p n t", n=2)
            for x in (e, f) for i in range(3)]
    E, Q, KK = part[0:2], part[2:4], part[4:6]
    items = [(0, -1)] + [(d, lv) for lv in range(LEVELS) for d in range(2)]

    def blocked(x, b):
        return x[:, :, :].rearrange("p n (g b) -> p (n g) b", b=b)

    with Stage(nc, "hl", "diff", "abs", "exped", "keys", "queries", "scored", "picked", "v") as st:
        sem = st.sem

        @st.block.vector
        def _(dve):
            def pick(i):
                d, lv = items[i]
                dve.wait_ge(sem["scored"], i + 1)
                mask = (K.ident if lv < 0 else K.level[:, d * LEVELS + lv]).bitcast(mybir.dt.uint32)
                for par in range(2):
                    for m in range(2):
                        ins = nc.vector.copy_predicated(acc[:, par, m], over_rows(mask, TT),
                                                        K.psum[:, (i % 2) * 4 + 2 * par + m].rearrange("p (c t) -> p c t", t=P))
                ins.then_inc(sem["picked"], 1)
                dve.wait_ge(sem["picked"], i + 1)

            for i, (d, lv) in enumerate(items):
                if i >= 2:
                    dve.wait_ge(sem["scored"], i - 1)
                if lv < 0:
                    nc.vector.tensor_tensor(KK[0][:], k[:, 0:2, CTX:], k[:, 2:4, CTX:], ALU.add).then_inc(sem["queries"], 1)
                    continue
                b = 2 << lv
                mid = b // 2 - 1 if d == 0 else b // 2
                for n in range(2):
                    cb = c[:, 2 * d + n, CTX:].rearrange("p (g b) -> p g b", b=b)
                    ins = nc.vector.tensor_tensor(E[i % 2][:, n].rearrange("p (g b) -> p g b", b=b), cb,
                                                  cb[:, :, mid:mid + 1].broadcast_to([P, S // b, b]), ALU.subtract)
                ins.then_inc(sem["diff"], 1)
                pick(i - 1)
                dve.wait_ge(sem["exped"], i)
                nc.vector.tensor_tensor(Q[i % 2][:], q[:, :, CTX:], E[i % 2][:], ALU.mult).then_inc(sem["queries"], 1)
            pick(len(items) - 1)

        @st.block.scalar
        def _(act):
            for i in range(1, len(items)):
                act.wait_ge(sem["diff"], i)
                nc.scalar.activation(E[i % 2][:], E[i % 2][:], ACT.Abs).then_inc(sem["abs"], 1)
                act.wait_ge(sem["abs"], i)
                nc.scalar.activation(E[i % 2][:], E[i % 2][:], ACT.Exp, scale=-1.0).then_inc(sem["exped"], 1)

        @st.block.gpsimd
        def _(pool):
            for i, (d, lv) in enumerate(items):
                if lv < 0:
                    continue
                pool.wait_ge(sem["exped"], i)
                if i >= 2:
                    pool.wait_ge(sem["scored"], i - 1)
                nc.gpsimd.tensor_tensor(KK[i % 2][:], k[:, 2 * d:2 * d + 2, CTX:], E[i % 2][:], ALU.mult).then_inc(sem["keys"], 1)

        @st.block.tensor
        def _(pe):
            for i, (d, lv) in enumerate(items):
                pe.wait_ge(sem["queries"], i + 1)
                if lv >= 0:
                    pe.wait_ge(sem["keys"], i)
                if i >= 2:
                    pe.wait_ge(sem["picked"], i - 1)
                for par in range(2):
                    r = par * HD
                    for m in range(2):
                        for t in range(TT):
                            at = slice(t * P, (t + 1) * P)
                            qq = q[r:r + HD, m, CTX + t * P:CTX + (t + 1) * P] if lv < 0 else Q[i % 2][r:r + HD, m, at]
                            ins = nc.tensor.matmul(K.psum[:, (i % 2) * 4 + 2 * par + m, at], KK[i % 2][r:r + HD, m, at], qq, start=True, stop=True)
                ins.then_inc(sem["scored"], 1)


def neighbourhood(nc, K, a, h2, mix):
    ph = ExitStack()

    def sb(name, shape, stack=ph):
        return stack.enter_context(nc.sbuf_tensor(name, shape, F32))

    o = sb("n_o", [P, TT, S])
    with ExitStack() as p2:
        q, k, v = sb("n_q", [P, 4, S], p2), sb("n_k", [P, 4, T2], p2), sb("n_v", [P, NCH, 512], p2)
        with ExitStack() as p3:
            rings(nc, K, p3, "n", vring=True)
            project_feature(nc, K, "nq", a["w2f"], 4, lambda k_: h2[:, k_, CTX:], [(0, S)],
                            lambda t, g, at, n, ps, link: nc.scalar.activation(q[:, t], ps, ACT.Copy), base=15)
            project_feature(nc, K, "nk", a["w2f"], 4, lambda k_: h2[:, k_], [(0, CTX), (CTX, S)],
                            lambda t, g, at, n, ps, link: nc.scalar.activation(k[:, t, at:at + n], ps, ACT.Copy), base=19)
            project_token(nc, K, "nv", lambda w: a["w2t"][1], 1, lambda k_: h2[:, k_], range(NCH),
                          lambda w, t, ps: nc.scalar.activation(v[:, t], ps, ACT.Copy))
        table = sb("n_table", [P, 8, 14 * HD], p2)
        window = sb("n_window", [P, HD], p2)
        cos, sin = sb("cos2", [P, S], p2), sb("sin2", [P, S], p2)
        load_stage(nc, "nl", [(table[:], a["na_table"]), (window[:], a["na_window"]), (cos[:], a["cos2"]), (sin[:], a["sin2"])])
        with Stage(nc, "nw", "m") as st:
            @st.block.gpsimd
            def _(pool):
                for hh in range(8):
                    tb = table[:, hh].rearrange("p (j n) -> p j n", n=HD)
                    nc.gpsimd.tensor_tensor(tb, tb, over_rows(window[:], 14), ALU.add)
        tiles = [q[:, m] for m in range(4)] + [k[:, m, CTX:] for m in range(4)] + [k[:, m, 0:CTX] for m in range(4)]
        l2_stage(nc, K, "nn", tiles, lambda t: S if t < 8 else CTX, [K.na_gain[:, 0:1]] * 4 + [K.na_gain[:, 1:2]] * 8, mean=1.0 / HD)
        rope_stage(nc, K, "nr", tiles[:8], S, cos[:], sin[:])
        s_sb, pt_sb = sb("n_s", [P, 2, 6 * P], p2), sb("n_pt", [P, 6 * P], p2)
        items = []
        for hh in range(8):
            m, r = hh // 2, (hh % 2) * HD
            for t in range(TT):
                qq = q[r:r + HD, m, t * P:(t + 1) * P]
                off = (6 - 2 * t) * HD
                segs = [(qq, k[r:r + HD, m, CTX:], S, 0, table[:, hh, off:off + S]), (qq, k[r:r + HD, m, 0:CTX], CTX, S, None)]
                vals = [v[:, j, hh * HD:(hh + 1) * HD] for j in list(range(CT, NCH)) + list(range(CT))]
                items.append(Item(segs=segs, values=vals, out=o[:, t, hh * HD:(hh + 1) * HD]))
        attention_stage(nc, K, "na", items, s_sb, pt_sb, 6 * P)
    turn_stage(nc, K, "nto", [o[:, t, m * P:(m + 1) * P] for m in range(4) for t in range(TT)],
               lambda m, ps: nc.vector.tensor_copy(mix[:, 4 + m], ps))
    ph.close()


def rwkv_projections(nc, K, a, h2, p_mix, px):
    ns = K.nring
    wring = K.wring[:].rearrange("p s (k n) -> p s k n", k=KD)
    segs = [(0, CTX, 1), (CTX, S, CTX + 2)]
    with Stage(nc, "rp", *[f"w{j}" for j in range(ns)], "zeroed", "done", "emptied", "shifted", "v") as st:
        sem = st.sem

        @st.block.gpsimd
        def _(pool):
            nc.gpsimd.memset(px[:], 0.0).then_inc(sem["zeroed"], 1)

        @st.block.sync
        def _(sync):
            for t in range(9):
                if t >= ns:
                    sync.wait_ge(sem["done"], t - ns + 1)
                sync.dma_start(wring[:, t % ns], a["w2f"][6 + t]).then_inc(sem[f"w{t % ns}"], 16)

        @st.block.tensor
        def _(pe):
            for t in range(9):
                pe.wait_ge(sem[f"w{t % ns}"], 16 * (t // ns + 1))
                if t >= 2:
                    pe.wait_ge(sem["emptied"], t - 1)
                for g, (at, n, col) in enumerate(segs):
                    for k in range(KD):
                        m = nc.tensor.matmul(K.psum[:, (t % 2) * 2 + g, :n], wring[:, t % ns, k], h2[:, k, at:at + n], start=(k == 0), stop=(k == KD - 1))
                m.then_inc(sem["done"], 1)

        @st.block.scalar
        def _(act):
            act.wait_ge(sem["zeroed"], 1)
            for t in range(9):
                act.wait_ge(sem["done"], t + 1)
                if t >= 2:
                    act.wait_ge(sem["shifted"], t - 1)
                for g, (at, n, col) in enumerate(segs):
                    m = nc.scalar.activation(px[:, t % 2, col:col + n], K.psum[:, (t % 2) * 2 + g, :n], ACT.Copy)
                m.then_inc(sem["emptied"], 1)

        @st.block.vector
        def _(dve):
            link = Chain(dve, sem["v"])
            for t in range(9):
                dve.wait_ge(sem["emptied"], t + 1)
                for at, n, col in segs:
                    m = nc.vector.tensor_tensor(p_mix[:, t, at:at + n], px[:, t % 2, col - 1:col - 1 + n], px[:, t % 2, col + 1:col + 1 + n], ALU.add)
                link(m)
                for at, n, col in segs:
                    m = nc.vector.scalar_tensor_tensor(p_mix[:, t, at:at + n], p_mix[:, t, at:at + n], 0.5, px[:, t % 2, col:col + n], ALU.mult, ALU.subtract)
                link(m)
                for at, n, col in segs:
                    m = nc.vector.scalar_tensor_tensor(p_mix[:, t, at:at + n], p_mix[:, t, at:at + n], K.mu[:, t:t + 1], px[:, t % 2, col:col + n], ALU.mult, ALU.add)
                m.then_inc(sem["shifted"], 1)


def rwkv(nc, K, a, p_mix, mix):
    ph = ExitStack()

    def sb(name, shape, stack=ph):
        return stack.enter_context(nc.sbuf_tensor(name, shape, F32))

    v_T, g_T = sb("r_vT", [P, NCH, 256]), sb("r_gT", [P, TT, 256])
    kk = sb("r_kk", [P, 2, T2])
    bonus, y = sb("r_bonus", [P, 2, S]), sb("r_y", [P, TT, 256])
    r_, k_, v_ = p_mix[:, 0:2], p_mix[:, 2:4], p_mix[:, 4:6]
    up_w = sb("r_up", [P, 3, 256])
    load_stage(nc, "rl", [(up_w[:], a["rw_up"])])
    with Stage(nc, "rt", "v", "a") as st:
        @st.block.scalar
        def _(act):
            nc.scalar.activation(p_mix[:, 6], p_mix[:, 6], ACT.Tanh)
            nc.scalar.activation(p_mix[:, 8], p_mix[:, 8], ACT.Sigmoid)

        @st.block.vector
        def _(dve):
            for m in range(2):
                nc.vector.tensor_scalar(kk[:, m], k_[:, m], K.rw[:, 4 + m:5 + m], None, ALU.mult)
    l2_stage(nc, K, "rk", [kk[:, m, at:at + n] for m in range(2) for at, n in ((0, S), (S, CTX))],
             lambda t: (S, CTX)[t % 2], [1.0] * 4, floor=1e-24)
    vjobs = [v_[:, m, j * P:(j + 1) * P] for j in range(NCH) for m in range(2)]
    turn_stage(nc, K, "rv", vjobs, lambda g, ps: nc.vector.tensor_copy(v_T[:, 2 * g:2 * g + 2], ps.rearrange("p (j n) -> p j n", j=2)))
    with Stage(nc, "rg", "done") as st:
        @st.block.tensor
        def _(pe):
            for t in range(TT):
                m = nc.tensor.matmul(K.psum[:, t, 0:256], p_mix[:, 8, CTX + t * P:CTX + (t + 1) * P], up_w[:, 2], start=True, stop=True)
                m.then_inc(st.sem["done"], 1)

        @st.block.scalar
        def _(act):
            for t in range(TT):
                act.wait_ge(st.sem["done"], t + 1)
                nc.scalar.activation(g_T[:, t], K.psum[:, t, 0:256], ACT.Copy)

    for d in range(2):
        rwkv_direction(nc, K, d, up_w, r_, k_, p_mix, kk, v_T, bonus, y)

    mean = sb("r_mean", [P, 32])
    with Stage(nc, "rb", "z", "done", "v", "b") as st:
        sem = st.sem

        @st.block.vector
        def _(dve):
            link = Chain(dve, sem["v"])
            for m in range(2):
                nc.vector.scalar_tensor_tensor(bonus[:, m], r_[:, m, CTX:], K.rw[:, 8 + m:9 + m], bonus[:, m], ALU.mult, ALU.mult).then_inc(sem["z"], 1)
            link(nc.vector.tensor_reduce(mean[:, 16:32], y[:].rearrange("p t (h d) -> p (t h) d", d=HD), AX.X, ALU.add))
            link(nc.vector.tensor_scalar(mean[:, 16:32], mean[:, 16:32], 1.0 / HD, None, ALU.mult))
            yh = y[:].rearrange("p t (h d) -> p (t h) d", d=HD)
            link(nc.vector.tensor_tensor(yh, yh, over_heads(mean[:, 16:32]), ALU.subtract))
            dve.wait_ge(sem["done"], 1)
            link(nc.vector.tensor_copy(mean[:, 0:16], K.psum[:, 0, 0:16]))

        @st.block.tensor
        def _(pe):
            pe.wait_ge(sem["z"], 2)
            for t in range(TT):
                for m in range(2):
                    ins = nc.tensor.matmul(K.psum[:, 0, 4 * t + 2 * m:4 * t + 2 * m + 2], bonus[:, m, t * P:(t + 1) * P], K.head_ones[:, 0:65:64], start=True, stop=True)
            ins.then_inc(sem["done"], 1)
    with ExitStack() as p2:
        sq = sb("r_sq", [P, TT, 256], p2)
        head_norm_stage(nc, K, "rn", y, TT, 4, K.rows2[:, 256:512], sq, mean[:, 16:32], bias=K.rows2[:, 512:768], eps=K.eps_ln)
        with Stage(nc, "ro", "v") as st:
            @st.block.vector
            def _(dve):
                link = Chain(dve, st.sem["v"])
                for t in range(TT):
                    nc.vector.tensor_tensor(sq[:, t].rearrange("p (h d) -> p h d", d=HD), v_T[:, CT + t].rearrange("p (h d) -> p h d", d=HD),
                                            over_heads(mean[:, 4 * t:4 * t + 4]), ALU.mult)
                    link(nc.vector.tensor_copy(K.stat[:, 0:1], mean[:, 0:1]))
                    link(nc.vector.tensor_tensor(y[:, t], y[:, t], sq[:, t], ALU.add))
                    link(nc.vector.tensor_tensor(y[:, t], y[:, t], g_T[:, t], ALU.mult))
    turn_stage(nc, K, "rto", [y[:, t, m * P:(m + 1) * P] for m in range(2) for t in range(TT)],
               lambda m, ps: nc.vector.tensor_copy(mix[:, 2 + m], ps))
    ph.close()


def rwkv_direction(nc, K, d, up_w, r_, k_, p_mix, kk, v_T, bonus, y):
    ph = ExitStack()

    def sb(name, shape, stack=ph):
        return stack.enter_context(nc.sbuf_tensor(f"r{d}_{name}", shape, F32))

    at, bt = sb("at", [P, NCH, 4, P]), sb("bt", [P, NCH, 4, P])
    cd = sb("cd", [P, TT, 2, 4, P])
    kke, re = sb("kke", [P, 2, T2]), sb("re", [P, 2, S])
    koT = sb("koT", [P, NCH, 4 * P])
    e_tot = sb("etot", [P, 2, NCH])
    half = HD
    with ExitStack() as p2:
        kd, ak, lw = sb("kd", [P, 2, T2], p2), sb("ak", [P, 2, T2], p2), sb("lw", [P, 2, T2], p2)
        ci, ce = sb("ci", [P, 2, T2], p2), sb("ce", [P, 2, T2], p2)
        rows = slice(d * HD, (d + 1) * HD)
        with Stage(nc, f"ru{d}", "up", "sig", "v") as st:
            sem = st.sem

            @st.block.tensor
            def _(pe):
                for j in range(4):
                    for s_, (at_, n) in enumerate(((0, S), (S, CTX))):
                        ins = nc.tensor.matmul(K.psum[:, 2 * j + s_, :n], up_w[rows, j // 2, (j % 2) * P:(j % 2 + 1) * P],
                                               p_mix[rows, 6 + j // 2, at_:at_ + n], start=True, stop=True)
                    ins.then_inc(sem["up"], 1)

            @st.block.scalar
            def _(act):
                for j in range(4):
                    act.wait_ge(sem["up"], j + 1)
                    for s_, (at_, n) in enumerate(((0, S), (S, CTX))):
                        to = (lw, ak)[j // 2][:, j % 2, at_:at_ + n]
                        ins = nc.scalar.activation(to, K.psum[:, 2 * j + s_, :n], ACT.Sigmoid, bias=K.rw[:, 10 + 4 * (j // 2) + 2 * d + j % 2:11 + 4 * (j // 2) + 2 * d + j % 2])
                    ins.then_inc(sem["sig"], 1)

            @st.block.vector
            def _(dve):
                link = Chain(dve, sem["v"])
                dve.wait_ge(sem["sig"], 2)
                link(nc.vector.tensor_scalar(lw[:], lw[:], -math.exp(-0.5), None, ALU.mult))
                running_sums(nc, K, dve, link, lw, ci, range(2))
                dve.wait_ge(sem["sig"], 4)
                for m in range(2):
                    link(nc.vector.tensor_scalar(kd[:, m], ak[:, m], -1.0, K.rw[:, 6 + m:7 + m], ALU.add, ALU.mult))
                    link(nc.vector.scalar_tensor_tensor(kd[:, m], kd[:, m], 1.0, k_[:, m], ALU.add, ALU.mult))
                link(nc.vector.tensor_tensor(ak[:], ak[:], kk[:], ALU.mult))
                if d == 0:
                    nc.vector.tensor_copy(bonus[:], kd[:, :, CTX:])
                else:
                    nc.vector.tensor_tensor(bonus[:], bonus[:], kd[:, :, CTX:], ALU.add)
                for m in range(2):
                    link(nc.vector.tensor_copy(e_tot[:, m], chunks(ci[:, m])[:, :, P - 1]))
                    if d == 0:
                        link(nc.vector.tensor_tensor(ce[:, m], ci[:, m], lw[:, m], ALU.subtract))
                    else:
                        link(nc.vector.tensor_tensor(chunks(ce[:, m]), over_heads(e_tot[:, m], P), chunks(ci[:, m]), ALU.subtract))
                        link(nc.vector.tensor_tensor(ci[:, m], ce[:, m], lw[:, m], ALU.add))
        tmp = lw
        with Stage(nc, f"re{d}", "diffed", "exped", "v", "used") as st:
            sem = st.sem

            @st.block.vector
            def _(dve):
                link = Chain(dve, sem["v"])
                for m in range(2):
                    ins = nc.vector.tensor_tensor(chunks(tmp[:, m]), over_heads(e_tot[:, m], P), chunks(ci[:, m]), ALU.subtract)
                ins.then_inc(sem["diffed"], 1)
                dve.wait_ge(sem["exped"], 3)
                nc.vector.tensor_tensor(kke[:], kk[:], kke[:], ALU.mult)
                link(nc.vector.tensor_tensor(re[:], r_[:, :, CTX:], re[:], ALU.mult))

            @st.block.scalar
            def _(act):
                nc.scalar.activation(kke[:], ce[:], ACT.Exp).then_inc(sem["exped"], 1)
                nc.scalar.activation(re[:], ci[:, :, CTX:], ACT.Exp).then_inc(sem["exped"], 1)
                act.wait_ge(sem["diffed"], 1)
                nc.scalar.activation(tmp[:], tmp[:], ACT.Exp).then_inc(sem["exped"], 1)
                nc.scalar.activation(e_tot[:], e_tot[:], ACT.Exp).then_inc(sem["exped"], 1)
        ko = at[:].rearrange("p c i t -> p (c i t)").rearrange("p (w m t) -> p w m t", w=2, m=2)
        with Stage(nc, f"rko{d}", "v") as st:
            @st.block.vector
            def _(dve):
                nc.vector.tensor_tensor(ko[:, 0], kd[:], tmp[:], ALU.mult)
                nc.vector.tensor_tensor(ko[:, 1], ak[:], tmp[:], ALU.mult)
        turn_stage(nc, K, f"rkt{d}", [ko[:, w, m, j * P:(j + 1) * P] for j in range(NCH) for w in range(2) for m in range(2)],
                   lambda g, ps: nc.vector.tensor_copy(koT[:, g], ps))
        rwkv_scores(nc, K, d, r_, kk, kd, ak, ci, ce, at, bt, cd, (lw[:], p_mix[:, 4:6]), sb, p2)
    xt = sb("xt", [P, NCH, 4, P])
    with ExitStack() as p2:
        work = sb("work", [P, 3, 3, 4, P], p2)
        invert_stage(nc, K, f"ri{d}", at, xt, NCH, lambda b: d == 1, work, lanes=3)
    with ExitStack() as p2:
        state, upd, zz, un = sb("state", [P, 2, P], p2), sb("upd", [P, 2, P], p2), sb("zz", [P, 256], p2), sb("un", [P, 256], p2)
        lat_seen = {}
        for i, j in enumerate(ORDER[d]):
            lat_seen[i] = sum(x >= CT for x in ORDER[d][:i])
        with Stage(nc, f"rs{d}", "state", "z", "zcopied", "u", "ucopied", "out", "kv", "ytaken", "v") as st:
            sem = st.sem

            @st.block.tensor
            def _(pe):
                for i, j in enumerate(ORDER[d]):
                    lat = j - CT
                    pe.wait_ge(sem["state"], i + 1)
                    for m in range(2):
                        nc.tensor.matmul(K.psum[:, 0, m * P:(m + 1) * P], kke[:, m, j * P:(j + 1) * P], state[:, m], start=True, stop=False, skip_group_check=True)
                        for par in range(2):
                            hh = 2 * m + par
                            ins = nc.tensor.matmul(K.psum[:, 0, hh * HD:(hh + 1) * HD], bt[:, j, 2 * par + m], v_T[:, j, hh * HD:(hh + 1) * HD],
                                                   start=False, stop=(par == 1), skip_group_check=True)
                    ins.then_inc(sem["z"], 1)
                    pe.wait_ge(sem["zcopied"], i + 1)
                    for hh in range(4):
                        ins = nc.tensor.matmul(K.psum[:, 1, hh * HD:(hh + 1) * HD], xt[:, j, 2 * (hh % 2) + hh // 2], zz[:, hh * HD:(hh + 1) * HD], start=True, stop=True)
                    ins.then_inc(sem["u"], 1)
                    pe.wait_ge(sem["ucopied"], i + 1)
                    for m in range(2):
                        nc.tensor.matmul(K.psum[:, 3, m * P:(m + 1) * P], koT[:, j, m * P:(m + 1) * P], v_T[:, j, m * P:(m + 1) * P], start=True, stop=False)
                        ins = nc.tensor.matmul(K.psum[:, 3, m * P:(m + 1) * P], koT[:, j, (2 + m) * P:(3 + m) * P], un[:, m * P:(m + 1) * P], start=False, stop=True)
                    if lat < 0:
                        ins.then_inc(sem["kv"], 1)
                        continue
                    if lat_seen[i] >= 1:
                        pe.wait_ge(sem["ytaken"], lat_seen[i])
                    for m in range(2):
                        nc.tensor.matmul(K.psum[:, 2, m * P:(m + 1) * P], re[:, m, lat * P:(lat + 1) * P], state[:, m], start=True, stop=False, skip_group_check=True)
                        for par in range(2):
                            hh = 2 * m + par
                            o = K.psum[:, 2, hh * HD:(hh + 1) * HD]
                            nc.tensor.matmul(o, cd[:, lat, 0, 2 * par + m], v_T[:, j, hh * HD:(hh + 1) * HD], start=False, stop=False, skip_group_check=True)
                            ins = nc.tensor.matmul(o, cd[:, lat, 1, 2 * par + m], un[:, hh * HD:(hh + 1) * HD], start=False, stop=(par == 1), skip_group_check=True)
                    ins.then_inc(sem["kv"], 1)

            @st.block.scalar
            def _(act):
                for i, j in enumerate(ORDER[d]):
                    act.wait_ge(sem["z"], i + 1)
                    nc.scalar.activation(zz[:], K.psum[:, 0, 0:256], ACT.Copy).then_inc(sem["zcopied"], 1)
                    act.wait_ge(sem["u"], i + 1)
                    nc.scalar.activation(un[:], K.psum[:, 1, 0:256], ACT.Copy, scale=-1.0).then_inc(sem["ucopied"], 1)
                    act.wait_ge(sem["kv"], i + 1)

            @st.block.vector
            def _(dve):
                link = Chain(dve, sem["v"])
                nc.vector.memset(state[:], 0.0).then_inc(sem["state"], 1)
                for i, j in enumerate(ORDER[d]):
                    lat = j - CT
                    dve.wait_ge(sem["kv"], i + 1)
                    link(nc.vector.tensor_tensor(upd[:], K.psum[:, 3, 0:256].rearrange("p (m n) -> p m n", m=2), over_rows(K.head_ones[:], 2), ALU.mult))
                    for m in range(2):
                        ins = nc.vector.scalar_tensor_tensor(state[:, m], state[:, m], e_tot[:, m, j:j + 1], upd[:, m], ALU.mult, ALU.add)
                    ins.then_inc(sem["state"], 1)
                    if lat >= 0:
                        if d == 0:
                            ins = nc.vector.tensor_copy(y[:, lat], K.psum[:, 2, 0:256])
                        else:
                            ins = nc.vector.tensor_tensor(y[:, lat], K.psum[:, 2, 0:256], y[:, lat], ALU.add)
                        ins.then_inc(sem["ytaken"], 1)
                    dve.wait_ge(sem["state"], i + 2)
    ph.close()


def rwkv_scores(nc, K, d, r_, kk, kd, ak, ci, ce, at, bt, cd, spare, sb, stack):
    half = HD
    s0, s1 = (x.rearrange("p m t -> p (m t)") for x in spare)
    kb, qb = (x[:, 0:8 * P].rearrange("p (s a b t) -> p s a b t", s=2, a=2, b=2) for x in (s0, s1))
    kc, qc = (x[:, 8 * P:12 * P].rearrange("p (s a b t) -> p s a b t", s=2, a=2, b=2) for x in (s0, s1))
    ek = sb("ek", [P, 2, 2, P], stack)
    ekc = sb("ekc", [P, 2, 2, half], stack)
    early, late = (0, half) if d == 0 else (half, 0)
    border = half - 1 if d == 0 else half
    with Stage(nc, f"rq{d}", "zero", "diffed", "exped", "q", "k", "scored", "taken", "v") as st:
        sem = st.sem

        def views(j):
            t = slice(j * P, (j + 1) * P)
            ts = slice(j * P + late, j * P + late + half)
            es = slice(j * P + early, j * P + early + half)
            return t, ts, es

        @st.block.gpsimd
        def _(pool):
            nc.gpsimd.memset(at[:], 0.0).then_inc(sem["zero"], 1)
            nc.gpsimd.memset(bt[:], 0.0).then_inc(sem["zero"], 1)
            nc.gpsimd.memset(cd[:], 0.0).then_inc(sem["zero"], 1)
            for j in range(NCH):
                t, ts, es = views(j)
                s = j % 2
                pool.wait_ge(sem["exped"], j + 1)
                if j >= 2:
                    pool.wait_ge(sem["scored"], j - 1)
                nc.gpsimd.tensor_tensor(kb[:, s, 0], ak[:, :, t], ek[:, s], ALU.mult)
                nc.gpsimd.tensor_tensor(kb[:, s, 1], kd[:, :, t], ek[:, s], ALU.mult)
                nc.gpsimd.tensor_tensor(kc[:, s, 0], ak[:, :, es], ekc[:, s], ALU.mult)
                nc.gpsimd.tensor_tensor(kc[:, s, 1], kd[:, :, es], ekc[:, s], ALU.mult).then_inc(sem["k"], 1)

        @st.block.scalar
        def _(act):
            for j in range(NCH):
                s = j % 2
                act.wait_ge(sem["diffed"], j + 1)
                nc.scalar.activation(qb[:, s], qb[:, s], ACT.Exp)
                nc.scalar.activation(qc[:, s], qc[:, s], ACT.Exp)
                nc.scalar.activation(ek[:, s], ek[:, s], ACT.Exp, scale=-1.0)
                nc.scalar.activation(ekc[:, s], ekc[:, s], ACT.Exp, scale=-1.0).then_inc(sem["exped"], 1)

        @st.block.vector
        def _(dve):
            def take(j):
                dve.wait_ge(sem["scored"], j + 1)
                b = 4 * (j % 2)
                for par in range(2):
                    for kt in range(2):
                        for qt in range(2 if j >= CT else 1):
                            mask = (K.before, K.upto)[qt] if d == 0 else (K.after, K.from_)[qt]
                            to = ((at, bt)[kt][:, j, 2 * par:2 * par + 2] if qt == 0 else cd[:, j - CT, 1 - kt, 2 * par:2 * par + 2])
                            ps = K.psum[:, b + 2 * par + kt].rearrange("p (m q t) -> p m q t", m=2, q=2)[:, :, qt]
                            for p0, c0 in ((0, 0), (half, half)):
                                c = slice(0, P) if p0 == early else slice(c0, c0 + half)
                                ins = nc.vector.tensor_tensor(to[p0:p0 + half, :, c], ps[p0:p0 + half, :, c],
                                                              over_rows(mask[p0:p0 + half, c], 2), ALU.mult)
                ins.then_inc(sem["taken"], 1)

            dve.wait_ge(sem["zero"], 3)
            for j in range(NCH):
                t, ts, es = views(j)
                s = j % 2
                if j >= 2:
                    dve.wait_ge(sem["scored"], j - 1)
                    dve.wait_ge(sem["k"], j - 1)
                for m in range(2):
                    mids = ci[:, m, t].rearrange("p (h n) -> p h n", h=2)[:, :, 31:32].broadcast_to([P, 2, half])
                    edge = ci[:, m, j * P + border:j * P + border + 1]
                    for qt, x in enumerate((ce, ci)):
                        nc.vector.tensor_tensor(qb[:, s, m, qt].rearrange("p (h n) -> p h n", h=2), x[:, m, t].rearrange("p (h n) -> p h n", h=2), mids, ALU.subtract)
                        nc.vector.tensor_scalar(qc[:, s, m, qt], x[:, m, ts], edge, None, ALU.subtract)
                    nc.vector.tensor_tensor(ek[:, s, m].rearrange("p (h n) -> p h n", h=2), ci[:, m, t].rearrange("p (h n) -> p h n", h=2), mids, ALU.subtract)
                    ins = nc.vector.tensor_scalar(ekc[:, s, m], ci[:, m, es], edge, None, ALU.subtract)
                ins.then_inc(sem["diffed"], 1)
                if j >= 1:
                    take(j - 1)
                dve.wait_ge(sem["exped"], j + 1)
                for m in range(2):
                    for qt, x in enumerate((kk, r_)):
                        nc.vector.tensor_tensor(qb[:, s, m, qt], x[:, m, t], qb[:, s, m, qt], ALU.mult)
                        ins = nc.vector.tensor_tensor(qc[:, s, m, qt], x[:, m, ts], qc[:, s, m, qt], ALU.mult)
                ins.then_inc(sem["q"], 1)
            take(NCH - 1)

        @st.block.tensor
        def _(pe):
            for j in range(NCH):
                s, b = j % 2, 4 * (j % 2)
                pe.wait_ge(sem["q"], j + 1)
                pe.wait_ge(sem["k"], j + 1)
                if j >= 2:
                    pe.wait_ge(sem["taken"], j - 1)
                for par in range(2):
                    r = slice(par * HD, (par + 1) * HD)
                    for kt in range(2):
                        bank = K.psum[:, b + 2 * par + kt].rearrange("p (m q t) -> p m q t", m=2, q=2)
                        for m in range(2):
                            for h0 in (0, half):
                                hs = slice(h0, h0 + half)
                                nc.tensor.matmul(bank[hs, m, :, hs], kb[r, s, kt, m, hs], qb[r, s, m, :, hs], start=True, stop=True)
                            ins = nc.tensor.matmul(bank[early:early + half, m, :, late:late + half], kc[r, s, kt, m], qc[r, s, m], start=True, stop=True)
                ins.then_inc(sem["scored"], 1)


def router_stage(nc, K, lg, first, second, weights, scr):
    with Stage(nc, "route", "v", "x", "e") as st:
        sem = st.sem
        gl, el = lg[:, :, 0:N_GRP], lg[:, :, N_GRP:]
        gx, ind, fg = scr[:, :, 0:4], scr[:, :, 4:8], scr[:, :, 8:12]
        es, e2, f1, f2, t8 = (scr[:, :, 16 + 8 * i:24 + 8 * i] for i in range(5))
        one = [scr[:, :, 56 + i] for i in range(8)]
        gmax, gsum, mx, m1, m2, ratio, w1, w2 = one

        @st.block.vector
        def _(dve):
            link = Chain(dve, sem["v"])

            def first_of(x, top, to, n):
                link(nc.vector.tensor_tensor(to, x, over_heads(top, n), ALU.is_equal))
                link(nc.vector.tensor_tensor(to, to, over_rows(K.desc[:, 8 - n:8], TT), ALU.mult))
                link(nc.vector.tensor_reduce(mx, to, AX.X, ALU.max))
                link(nc.vector.tensor_tensor(to, to, over_heads(mx, n), ALU.is_equal))

            link(nc.vector.tensor_reduce(gmax, gl, AX.X, ALU.max))
            nc.vector.tensor_tensor(gx, gl, over_heads(gmax, 4), ALU.subtract).then_inc(sem["x"], 1)
            first_of(gl, gmax, fg, 4)
            link(nc.vector.tensor_tensor(es, el[:, :, 0:8], over_heads(fg[:, :, 0], 8), ALU.mult))
            for g in range(1, N_GRP):
                link(nc.vector.tensor_tensor(t8, el[:, :, 8 * g:8 * g + 8], over_heads(fg[:, :, g], 8), ALU.mult))
                link(nc.vector.tensor_tensor(es, es, t8, ALU.add))
            link(nc.vector.tensor_reduce(m1, es, AX.X, ALU.max))
            first_of(es, m1, f1, 8)
            link(nc.vector.scalar_tensor_tensor(e2, f1, -3e38, es, ALU.mult, ALU.add))
            link(nc.vector.tensor_reduce(m2, e2, AX.X, ALU.max))
            first_of(e2, m2, f2, 8)
            nc.vector.tensor_tensor(ratio, m2, m1, ALU.subtract).then_inc(sem["x"], 1)
            dve.wait_ge(sem["e"], 2)
            link(nc.vector.tensor_reduce(gsum, gx, AX.X, ALU.add))
            link(nc.vector.scalar_tensor_tensor(w1, ratio, 1.0, gsum, ALU.add, ALU.mult))
            link(nc.vector.reciprocal(weights[:, 0], w1))
            link(nc.vector.tensor_tensor(weights[:, 1], weights[:, 0], ratio, ALU.mult))
            for g in range(N_GRP):
                for to, f in ((first, f1), (second, f2)):
                    nc.vector.tensor_tensor(to[:, 8 * g:8 * g + 8, :].rearrange("p e t -> p t e"), f, over_heads(fg[:, :, g], 8), ALU.mult)

        @st.block.scalar
        def _(act):
            act.wait_ge(sem["x"], 1)
            nc.scalar.activation(gx, gx, ACT.Exp).then_inc(sem["e"], 1)
            act.wait_ge(sem["x"], 2)
            nc.scalar.activation(ratio, ratio, ACT.Exp).then_inc(sem["e"], 1)


SLOTS = 64
N_EXTRA = 2 * S // SLOTS
LOTS = N_EXP + N_EXTRA


def place_stage(nc, K, first, second, rank, pos, lots, n_lots, scr):
    both = scr[:, 0]
    q, r, t1 = scr[:, 1], scr[:, 2], scr[:, 3]
    cnt, more, base, t32 = (scr[:, 4, :, i] for i in range(4))
    with Stage(nc, "place", "both", "ranked", "v") as st:
        sem = st.sem

        @st.block.tensor
        def _(pe):
            pe.wait_ge(sem["both"], 1)
            for t in range(TT):
                for u in range(t + 1):
                    nc.tensor.matmul(K.psum[:, t, 0:N_EXP], (K.before if u == t else K.ones)[:], both[:, :, u], start=(u == 0), stop=(u == t))
            for u in range(TT):
                ins = nc.tensor.matmul(K.psum[:, TT, 0:N_EXP], K.ones[:], both[:, :, u], start=(u == 0), stop=(u == TT - 1))
            ins.then_inc(sem["ranked"], 1)

        @st.block.vector
        def _(dve):
            link = Chain(dve, sem["v"])
            nc.vector.tensor_tensor(both, first, second, ALU.add).then_inc(sem["both"], 1)
            dve.wait_ge(sem["ranked"], 1)
            for t in range(TT):
                link(nc.vector.tensor_copy(r[:, :, t], K.psum[:, t, 0:N_EXP]))
            link(nc.vector.tensor_copy(cnt, K.psum[:, TT, 0:N_EXP]))
            link(nc.vector.scalar_tensor_tensor(rank, r, 1.0, both, ALU.add, ALU.mult))
            link(nc.vector.tensor_scalar(rank, rank, -1.0, None, ALU.add))
            link(nc.vector.tensor_scalar(q, r, float(SLOTS), None, ALU.is_ge))
            link(nc.vector.tensor_scalar(more, cnt, float(SLOTS), None, ALU.is_gt))
            for j in range(2, S // SLOTS):
                link(nc.vector.scalar_tensor_tensor(q, r, float(SLOTS * j), q, ALU.is_ge, ALU.add))
                link(nc.vector.scalar_tensor_tensor(more, cnt, float(SLOTS * j), more, ALU.is_gt, ALU.add))
            link(nc.vector.tensor_tensor_scan(base, K.one_row, more, 0.0, ALU.mult, ALU.add))
            link(nc.vector.tensor_copy(n_lots, base[:, N_EXP - 1:N_EXP]))
            link(nc.vector.tensor_tensor(base, base, more, ALU.subtract))
            link(nc.vector.tensor_tensor(t32, base, K.count[:, 0:N_EXP], ALU.subtract))
            link(nc.vector.tensor_tensor(t1, q, over_heads(t32, TT), ALU.add))
            link(nc.vector.tensor_scalar(t1, t1, float(N_EXP - 1), float(SLOTS), ALU.add, ALU.mult))
            link(nc.vector.scalar_tensor_tensor(t1, q, 0.0, t1, ALU.is_gt, ALU.mult))
            link(nc.vector.scalar_tensor_tensor(q, q, -float(SLOTS), r, ALU.mult, ALU.add))
            link(nc.vector.tensor_tensor(t1, t1, q, ALU.add))
            link(nc.vector.tensor_scalar(t32, K.count[:, 0:N_EXP], float(SLOTS), None, ALU.mult))
            link(nc.vector.tensor_tensor(t1, t1, over_heads(t32, TT), ALU.add))
            for i, choice in enumerate((first, second)):
                link(nc.vector.tensor_tensor(q, choice, t1, ALU.mult))
                link(nc.vector.tensor_reduce(r[:, 0:1, :].rearrange("p o t -> p (o t)"), q.rearrange("p e t -> p t e"), AX.X, ALU.add))
                link(nc.vector.tensor_copy(pos[:, i], r[:, 0:1, :].rearrange("p o t -> p (o t)")))
            m = scr[:, 5:9].rearrange("p a e t -> p (a e t)").rearrange("p (x e) -> p x e", e=N_EXP)
            m2 = scr[:, 9:13].rearrange("p a e t -> p (a e t)").rearrange("p (x e) -> p x e", e=N_EXP)
            x = K.count[:, 0:N_EXTRA]
            link(nc.vector.tensor_tensor(m, over_rows(base, N_EXTRA), over_heads(x, N_EXP), ALU.is_le))
            link(nc.vector.tensor_tensor(t32, base, more, ALU.add))
            link(nc.vector.tensor_tensor(m2, over_rows(t32, N_EXTRA), over_heads(x, N_EXP), ALU.is_gt))
            link(nc.vector.tensor_tensor(m, m, m2, ALU.mult))
            link(nc.vector.tensor_tensor(m2, m, over_rows(base, N_EXTRA), ALU.mult))
            link(nc.vector.tensor_reduce(lots[:, 1], m2, AX.X, ALU.add))
            link(nc.vector.tensor_tensor(m2, m, over_rows(K.count[:, 0:N_EXP], N_EXTRA), ALU.mult))
            link(nc.vector.tensor_reduce(lots[:, 0], m2, AX.X, ALU.add))
            link(nc.vector.tensor_tensor(lots[:, 1], x, lots[:, 1], ALU.subtract))
            link(nc.vector.tensor_scalar(lots[:, 1], lots[:, 1], 1.0, None, ALU.add))


def experts(nc, K, a, x1, mod, gains):
    ph = ExitStack()

    def sb(name, shape, stack=ph, dt=F32):
        return stack.enter_context(nc.sbuf_tensor(name, shape, dt))

    h_tok = sb("m_htok", [P, TT, D])
    rank = sb("m_rank", [P, N_EXP, TT])
    weights = sb("m_weights", [P, 2, TT])
    pos = sb("m_pos", [P, 2, TT], dt=mybir.dt.uint32)
    lots, lots_i = sb("m_lots", [P, 2, N_EXTRA]), sb("m_lots_i", [P, N_EXTRA], dt=mybir.dt.int32)
    n_lots = sb("m_nlots", [P, 1], dt=mybir.dt.int32)
    result = nc.dram_tensor("expert_rows", (LOTS * SLOTS, D), F32).ap()
    with ExitStack() as p2:
        hm = sb("m_h", [P, KD, S], p2)
        norm_stage(nc, K, "n4", lambda k: x1[:, k], S, lambda k: hm[:, k], gains[:, 2], shift=mod[:, 24:32, 0], square=K.tmp)
        lg, scr = sb("m_lg", [P, TT, 36], p2), sb("m_scr", [P, TT, 64], p2)
        first, second = sb("m_first", [P, N_EXP, TT], p2), sb("m_second", [P, N_EXP, TT], p2)
        pscr = sb("m_pscr", [P, 13, N_EXP, TT], p2)
        wr, br = sb("m_wr", [P, KD, 36], p2), sb("m_br", [P, 36], p2)
        load_stage(nc, "ml", [(wr[:], a["w_router"]), (br[:], a["b_router"])])
        with Stage(nc, "mr", "done", "zero", "cleared") as st:
            @st.block.gpsimd
            def _(pool):
                nc.gpsimd.memset(h_tok[:, 0], 0.0).then_inc(st.sem["zero"], 1)

            @st.block.sync
            def _(sync):
                sync.wait_ge(st.sem["zero"], 1)
                for x in range(0, N_EXTRA * SLOTS, P):
                    sync.dma_start(result[N_EXP * SLOTS + x:N_EXP * SLOTS + x + P, :], h_tok[:, 0]).then_inc(st.sem["cleared"], 16)
                sync.wait_ge(st.sem["cleared"], 16 * (N_EXTRA * SLOTS // P))

            @st.block.tensor
            def _(pe):
                for t in range(TT):
                    for k in range(KD):
                        m = nc.tensor.matmul(K.psum[:, t, 0:36], hm[:, k, t * P:(t + 1) * P], wr[:, k], start=(k == 0), stop=(k == KD - 1))
                    m.then_inc(st.sem["done"], 1)

            @st.block.vector
            def _(dve):
                for t in range(TT):
                    dve.wait_ge(st.sem["done"], t + 1)
                    nc.vector.tensor_tensor(lg[:, t], K.psum[:, t, 0:36], br[:], ALU.add)

        turn_stage(nc, K, "mt", [hm[:, k, t * P:(t + 1) * P] for t in range(TT) for k in range(KD)],
                   lambda g, ps: nc.vector.tensor_copy(h_tok[:, g // 2, (g % 2) * 512:(g % 2 + 1) * 512], ps))
        router_stage(nc, K, lg, first[:], second[:], weights, scr)
        place_stage(nc, K, first[:], second[:], rank[:], pos, lots, n_lots[:], pscr)
        with Stage(nc, "mi") as st:
            @st.block.vector
            def _(dve):
                nc.vector.tensor_copy(lots_i[:], lots[:, 0])
    with ExitStack() as p2:
        W = ExpertBuffers(nc, p2)
        experts_stage(nc, K, a, h_tok, rank, result, W)
        further_stage(nc, K, a, h_tok, rank, lots, lots_i, n_lots, result, W)
    fetched = sb("m_fetched", [P, 2, TT, D])
    with Stage(nc, "mf", *[f"soft{i}" for i in range(2 * TT)], "v") as st:
        sem = st.sem

        @st.block.gpsimd
        def _(pool):
            for t in range(TT):
                for i in range(2):
                    pool.indirect_dma_start(fetched[:, i, t], None, result, bass.IndirectOffsetOnAxis(ap=pos[:, i, t:t + 1], axis=0)).then_inc(sem[f"soft{2 * t + i}"], 16)

        @st.block.vector
        def _(dve):
            link = Chain(dve, sem["v"])
            for t in range(TT):
                dve.wait_ge(sem[f"soft{2 * t}"], 16)
                link(nc.vector.tensor_scalar(fetched[:, 0, t], fetched[:, 0, t], weights[:, 0, t:t + 1], None, ALU.mult))
                dve.wait_ge(sem[f"soft{2 * t + 1}"], 16)
                nc.vector.scalar_tensor_tensor(fetched[:, 0, t], fetched[:, 1, t], weights[:, 1, t:t + 1], fetched[:, 0, t], ALU.mult, ALU.add)
    turn_stage(nc, K, "mo", [fetched[:, 0, t, k * P:(k + 1) * P] for k in range(KD) for t in range(TT)],
               lambda k, ps: nc.vector.scalar_tensor_tensor(x1[:, k], ps, mod[:, 40 + k, 0:1], x1[:, k], ALU.mult, ALU.add))
    ph.close()


class ExpertBuffers:

    def __init__(self, nc, stack):
        def two(name, shape):
            return [stack.enter_context(nc.sbuf_tensor(f"m_{name}{i}", shape, F32)) for i in range(2)]

        self.wg, self.wu, self.wd = two("wg", [P, KD, D_EXP]), two("wu", [P, KD, D_EXP]), two("wd", [P, FT, D])
        self.sel, self.xg = two("sel", [P, TT, SLOTS]), two("xg", [P, KD, SLOTS])
        self.sg, self.hid, self.rows = two("sg", [P, FT, SLOTS]), two("hid", [P, FT, SLOTS]), two("rows", [SLOTS, D])


def expert_weights(w, e):
    return w[bass.ds(e, 1)].rearrange("o p k n -> (o p) k n")


def lot_select(nc, K, W, s, rank_e, slots):
    return nc.vector.tensor_tensor(W.sel[s][:], over_heads(rank_e, SLOTS), over_rows(slots, TT), ALU.is_equal)


def lot_gather(nc, K, W, s, h_tok):
    for k in range(KD):
        for t in range(TT):
            m = nc.tensor.matmul(K.psum[:, s, k * SLOTS:(k + 1) * SLOTS], h_tok[:, t, k * P:(k + 1) * P], W.sel[s][:, t], start=(t == 0), stop=(t == TT - 1))
    return m


def lot_up(nc, K, W, s):
    for i, w in enumerate((W.wg[s], W.wu[s])):
        for f in range(FT):
            at = (i * FT + f) * SLOTS
            for k in range(KD):
                m = nc.tensor.matmul(K.psum[:, 2 + s, at:at + SLOTS], w[:, k, f * P:(f + 1) * P], W.xg[s][:, k], start=(k == 0), stop=(k == KD - 1))
    return m


def lot_down(nc, K, W, s):
    for dh in range(2):
        for f in range(FT):
            m = nc.tensor.matmul(K.psum[0:SLOTS, 4 + 2 * s + dh], W.hid[s][:, f], W.wd[s][:, f, dh * 512:(dh + 1) * 512], start=(f == 0), stop=(f == FT - 1))
    return m


def half_bank(K, s, i):
    return K.psum[:, 2 + s, i * FT * SLOTS:(i + 1) * FT * SLOTS].rearrange("p (f n) -> p f n", f=FT)


def experts_stage(nc, K, a, h_tok, rank, result, W):
    FREE = 2
    with Stage(nc, "moe", "wg0", "wg1", "wu0", "wu1", "wd0", "wd1", "selected", "gathered", "xcopied", "upped", "gated",
               "hidden", "downed", "rcopied", "stored0", "stored1") as st:
        sem = st.sem

        @st.block.sync
        def _(sync):
            def store(e, s):
                sync.wait_ge(sem["rcopied"], e + (1 + FREE))
                sync.dma_start(result[bass.ds(e * SLOTS, SLOTS), :], W.rows[s][:]).then_inc(sem[f"stored{s}"], 16)

            for s in range(2):
                sync.dma_start(W.wg[s][:], a["w_gate"][s]).then_inc(sem[f"wg{s}"], 16)
                sync.dma_start(W.wu[s][:], a["w_up"][s]).then_inc(sem[f"wu{s}"], 16)
                sync.dma_start(W.wd[s][:], a["w_down"][s]).then_inc(sem[f"wd{s}"], 16)
            with sync.Fori(0, N_EXP // 2 - 1) as i:
                for s in range(2):
                    e = i * 2 + s
                    sync.wait_ge(sem["upped"], e + (1 + FREE))
                    sync.dma_start(W.wg[s][:], expert_weights(a["w_gate"], e + 2)).then_inc(sem[f"wg{s}"], 16)
                    sync.dma_start(W.wu[s][:], expert_weights(a["w_up"], e + 2)).then_inc(sem[f"wu{s}"], 16)
                    sync.wait_ge(sem["downed"], e + (1 + FREE))
                    sync.dma_start(W.wd[s][:], expert_weights(a["w_down"], e + 2)).then_inc(sem[f"wd{s}"], 16)
                    store(e, s)
            for s in range(2):
                store(N_EXP - 2 + s, s)
            for s in range(2):
                sync.wait_ge(sem[f"stored{s}"], 16 * (N_EXP // 2 + 1))

        @st.block.tensor
        def _(pe):
            def gather(e, s):
                pe.wait_ge(sem["selected"], e + 1)
                pe.wait_ge(sem["xcopied"], e + 1)
                lot_gather(nc, K, W, s, h_tok).then_inc(sem["gathered"], 1)

            def up(e, s, nth):
                pe.wait_ge(sem[f"wg{s}"], nth * 16)
                pe.wait_ge(sem[f"wu{s}"], nth * 16)
                pe.wait_ge(sem["xcopied"], e + (1 + FREE))
                pe.wait_ge(sem["hidden"], e + 1)
                lot_up(nc, K, W, s).then_inc(sem["upped"], 1)

            def down(e, s, nth):
                pe.wait_ge(sem[f"wd{s}"], nth * 16)
                pe.wait_ge(sem["hidden"], e + (1 + FREE))
                pe.wait_ge(sem["rcopied"], e + 1)
                lot_down(nc, K, W, s).then_inc(sem["downed"], 1)

            gather(0, 0)
            with pe.Fori(0, N_EXP // 2 - 1) as i:
                for s in range(2):
                    e = i * 2 + s
                    up(e, s, i + 1)
                    gather(e + 1, 1 - s)
                    down(e, s, i + 1)
            up(N_EXP - 2, 0, N_EXP // 2)
            gather(N_EXP - 1, 1)
            down(N_EXP - 2, 0, N_EXP // 2)
            up(N_EXP - 1, 1, N_EXP // 2)
            down(N_EXP - 1, 1, N_EXP // 2)

        @st.block.scalar
        def _(act):
            def copy(e, s):
                act.wait_ge(sem["gathered"], e + (1 + FREE))
                act.wait_ge(sem["upped"], e + 1)
                nc.scalar.activation(W.xg[s][:], K.psum[:, s].rearrange("p (k n) -> p k n", k=KD), ACT.Copy).then_inc(sem["xcopied"], 1)

            def gate(e, s):
                act.wait_ge(sem["upped"], e + (1 + FREE))
                act.wait_ge(sem["hidden"], e + 1)
                nc.scalar.activation(W.sg[s][:], half_bank(K, s, 0), ACT.Silu).then_inc(sem["gated"], 1)

            copy(0, 0)
            with act.Fori(0, N_EXP // 2 - 1) as i:
                for s in range(2):
                    e = i * 2 + s
                    gate(e, s)
                    copy(e + 1, 1 - s)
            gate(N_EXP - 2, 0)
            copy(N_EXP - 1, 1)
            gate(N_EXP - 1, 1)

        @st.block.vector
        def _(dve):
            def select(e, s):
                dve.wait_ge(sem["gathered"], e + 1)
                lot_select(nc, K, W, s, rank[:, bass.ds(e, 1), :].rearrange("p o t -> p (o t)"), K.count).then_inc(sem["selected"], 1)

            def hide(e, s):
                dve.wait_ge(sem["gated"], e + 1)
                dve.wait_ge(sem["downed"], e + 1)
                nc.vector.tensor_tensor(W.hid[s][:], W.sg[s][:], half_bank(K, s, 1), ALU.mult).then_inc(sem["hidden"], 1)

            def rows_out(e, s, nth):
                dve.wait_ge(sem["downed"], e + (1 + FREE))
                dve.wait_ge(sem[f"stored{s}"], nth * 16)
                nc.vector.tensor_copy(W.rows[s][:], K.psum[0:SLOTS, 4 + 2 * s:6 + 2 * s].rearrange("p b n -> p (b n)")).then_inc(sem["rcopied"], 1)

            for c, n in enumerate(("gathered", "xcopied", "upped", "hidden", "downed", "rcopied")):
                nc.vector.memset(K.stat[:, c:c + 1], 0.0).then_inc(sem[n], FREE)
            for s in range(2):
                nc.vector.memset(K.stat[:, 6 + s:7 + s], 0.0).then_inc(sem[f"stored{s}"], 16)
            select(0, 0)
            select(1, 1)
            with dve.Fori(0, N_EXP // 2 - 1) as i:
                for s in range(2):
                    e = i * 2 + s
                    hide(e, s)
                    select(e + 2, s)
                    rows_out(e, s, i + 1)
            for s in range(2):
                hide(N_EXP - 2 + s, s)
                rows_out(N_EXP - 2 + s, s, N_EXP // 2)


def further_stage(nc, K, a, h_tok, rank, lots, lots_i, n_lots, result, W):
    with Stage(nc, "more", "loaded", "selected", "gathered", "xcopied", "upped", "gated", "hidden", "downed",
               "rcopied", "stored", "turned", "v") as st:
        sem = st.sem

        def turns(eng, body):
            n = eng.value_load(n_lots[0:1, 0:1], min_val=0, max_val=N_EXTRA)
            with eng.If(n > 0):
                with eng.Fori(0, n) as x:
                    body(x)

        @st.block.sync
        def _(sync):
            def body(x):
                e = sync.value_load(lots_i[0:1, bass.ds(x, 1)], min_val=0, max_val=N_EXP - 1)
                sync.dma_start(W.wg[0][:], expert_weights(a["w_gate"], e)).then_inc(sem["loaded"], 16)
                sync.dma_start(W.wu[0][:], expert_weights(a["w_up"], e)).then_inc(sem["loaded"], 16)
                sync.dma_start(W.wd[0][:], expert_weights(a["w_down"], e)).then_inc(sem["loaded"], 16)
                sync.wait_ge(sem["rcopied"], x + 1)
                sync.dma_start(result[bass.ds(x * SLOTS + N_EXP * SLOTS, SLOTS), :], W.rows[0][:]).then_inc(sem["stored"], 16)
                sync.wait_ge(sem["stored"], x * 16 + 16)
                sync.sem_inc(sem["turned"], 1)

            turns(sync, body)

        @st.block.tensor
        def _(pe):
            def body(x):
                pe.wait_ge(sem["selected"], x + 1)
                lot_gather(nc, K, W, 0, h_tok).then_inc(sem["gathered"], 1)
                pe.wait_ge(sem["loaded"], x * 48 + 48)
                pe.wait_ge(sem["xcopied"], x + 1)
                lot_up(nc, K, W, 0).then_inc(sem["upped"], 1)
                pe.wait_ge(sem["hidden"], x + 1)
                lot_down(nc, K, W, 0).then_inc(sem["downed"], 1)

            turns(pe, body)

        @st.block.scalar
        def _(act):
            def body(x):
                act.wait_ge(sem["gathered"], x + 1)
                nc.scalar.activation(W.xg[0][:], K.psum[:, 0].rearrange("p (k n) -> p k n", k=KD), ACT.Copy).then_inc(sem["xcopied"], 1)
                act.wait_ge(sem["upped"], x + 1)
                nc.scalar.activation(W.sg[0][:], half_bank(K, 0, 0), ACT.Silu).then_inc(sem["gated"], 1)

            turns(act, body)

        @st.block.vector
        def _(dve):
            slots = W.sg[1][:, 0]

            def body(x):
                e = dve.value_load(lots_i[0:1, bass.ds(x, 1)], min_val=0, max_val=N_EXP - 1)
                nc.vector.tensor_scalar(W.sg[1][:, 1, 0:1], lots[:, 1, bass.ds(x, 1)], float(SLOTS), None, ALU.mult).then_inc(sem["v"], 1)
                dve.wait_ge(sem["v"], x * 2 + 1)
                nc.vector.tensor_scalar(slots, K.count, W.sg[1][:, 1, 0:1], None, ALU.add).then_inc(sem["v"], 1)
                dve.wait_ge(sem["v"], x * 2 + 2)
                lot_select(nc, K, W, 0, rank[:, bass.ds(e, 1), :].rearrange("p o t -> p (o t)"), slots).then_inc(sem["selected"], 1)
                dve.wait_ge(sem["gated"], x + 1)
                nc.vector.tensor_tensor(W.hid[0][:], W.sg[0][:], half_bank(K, 0, 1), ALU.mult).then_inc(sem["hidden"], 1)
                dve.wait_ge(sem["downed"], x + 1)
                nc.vector.tensor_copy(W.rows[0][:], K.psum[0:SLOTS, 4:6].rearrange("p b n -> p (b n)")).then_inc(sem["rcopied"], 1)

            turns(dve, body)



def second_block(nc, K, a, x1):
    ph = ExitStack()

    def sb(name, shape, stack=ph):
        return stack.enter_context(nc.sbuf_tensor(name, shape, F32))

    vecs = sb("vecs2", [P, N_VECS2])
    K.rows2 = sb("rows2", [P, 768])
    K.reset = sb("reset", [P, T2])
    at = 0

    def take(n):
        nonlocal at
        at += n
        return vecs[:, at - n:at]

    K.cond, K.b_ada, K.norm1, K.norm2 = take(16), take(48), take(8), take(8)
    K.hlb, K.mu, K.rw, K.na_gain, K.desc, K.eps_ln = take(8), take(9), take(18), take(2), take(8), take(1)
    K.count, K.one_row = take(SLOTS), take(N_EXP)
    mod, gains = sb("mod", [P, 48, 2]), sb("gains", [P, 3, KD])
    load_stage(nc, "l2", [(vecs[:], a["vecs2"]), (K.rows2[:], a["rows2"]), (K.reset[:], a["reset"])])
    with ExitStack() as p2:
        rings(nc, K, p2, "m", n=8)
        modulation_stage(nc, K, a, mod, gains)
    with ExitStack() as p1:
        mix = sb("mix", [P, KD, S], p1)
        with ExitStack() as p2:
            p_mix = sb("p_mix", [P, 9, T2], p2)
            with ExitStack() as p3:
                h2 = sb("h2", [P, KD, T2], p3)
                with ExitStack() as p4:
                    ctx = sb("ctx", [P, KD, CTX], p4)
                    load_stage(nc, "lx2", [(ctx[:], a["ctxT"])])
                    norm_stage(nc, K, "n3c", lambda k: ctx[:, k], CTX, lambda k: h2[:, k, 0:CTX], gains[:, 1], shift=mod[:, 0:8, 1], square=K.tmp)
                norm_stage(nc, K, "n3", lambda k: x1[:, k], S, lambda k: h2[:, k, CTX:], gains[:, 0], shift=mod[:, 0:8, 0], square=K.tmp)
                hgrn(nc, K, a, h2, mix)
                neighbourhood(nc, K, a, h2, mix)
                with ExitStack() as p4:
                    rings(nc, K, p4, "r", n=4)
                    px = sb("px", [P, 2, T2 + 3], p4)
                    rwkv_projections(nc, K, a, h2, p_mix, px)
            rwkv(nc, K, a, p_mix, mix)
        rings(nc, K, p1, "o2")
        out_stage(nc, K, "po2", a["wo2"], lambda k: mix[:, k], x1, mod[:, 16:24, 0])
    experts(nc, K, a, x1, mod, gains)
    ph.close()


N_VECS2 = 16 + 48 + 8 + 8 + 8 + 9 + 18 + 2 + 8 + 1 + SLOTS + N_EXP


def build(nc, a, out):
    Stage.turn = 0
    K = Kept()
    top = ExitStack()

    def sb(name, shape):
        return top.enter_context(nc.sbuf_tensor(name, shape, F32))

    K.psum = top.enter_context(nc.psum_tensor("psum", [P, 8, 512], F32))
    const = sb("const", [P, 8, P])
    K.ident, K.ones, K.head_ones, K.rot, K.upto, K.before, K.from_, K.after = (const[:, i] for i in range(8))
    K.level = sb("level", [P, 2 * LEVELS, P])
    K.tmp, K.rstd, K.stat = sb("tmp", [P, 2, S]), sb("rstd", [P, 2, S]), sb("stat", [P, 8])
    vecs = sb("vecs", [P, 2 * KD + 48 + 16 + 1])
    K.vec_norm, K.vec_fnorm = vecs[:, 0:KD], vecs[:, KD:2 * KD]
    K.conv = vecs[:, 2 * KD:2 * KD + 48].rearrange("p (t j) -> p t j", j=4)
    K.dt_bias, K.a_log = vecs[:, 2 * KD + 48:2 * KD + 56], vecs[:, 2 * KD + 56:2 * KD + 64]
    K.eps = vecs[:, 2 * KD + 64:2 * KD + 65]
    x1 = sb("x1", [P, KD, S])
    load_stage(nc, "lc", [(const[:], a["const"]), (K.level[:], a["level"]), (vecs[:], a["vecs"])])
    first_block(nc, K, a, x1)
    second_block(nc, K, a, x1)
    store_stage(nc, x1, out)
    top.close()


def store_stage(nc, x, out):
    with Stage(nc, "store", "stored") as st:
        @st.block.sync
        def _(sync):
            sync.dma_start(out, x[:]).then_inc(st.sem["stored"], 16)
            sync.wait_ge(st.sem["stored"], 16)


def feature_tiles(w):
    k, n = w.shape
    return np.ascontiguousarray(w.reshape(k // P, P, n // P, P).transpose(2, 1, 0, 3))


def blocks(w):
    k, n = w.shape
    return np.ascontiguousarray(w.reshape(k // P, P, n).transpose(1, 0, 2))


def columns(v):
    return np.ascontiguousarray(v.reshape(-1, P).T)


def rows(v):
    return np.ascontiguousarray(np.broadcast_to(v.reshape(1, -1), (P, v.size)))


def constants():
    i, j = np.meshgrid(np.arange(P), np.arange(P), indexing="ij")
    rot = np.zeros((P, P), np.float32)
    for o in range(P):
        rot[o + 32 if o % 64 < 32 else o - 32, o] = -1.0 if o % 64 < 32 else 1.0
    const = np.stack([i == j, np.ones((P, P)), i // HD == j // HD, rot, i <= j, i < j, i >= j, i > j], 1)
    low = []
    for lv in range(LEVELS):
        b = 2 << lv
        low.append((i // b == j // b) & (i % b < b // 2) & (j % b >= b // 2))
    level = np.stack(low + [m.T for m in low], 1)
    f32 = np.float32
    q, k = np.meshgrid(np.arange(P), np.arange(P), indexing="ij")
    neg = lambda ok: np.where(ok, 0.0, NEG)
    mask0 = np.concatenate([neg(k >= q), neg(k <= q)], 1)
    dil = lambda d: np.concatenate([neg((q - k) % d == 0)] * 3 + [neg(((q - k) % d == 0) & (k <= q))], 1)
    inv = (f32(10000.0) ** (-np.arange(0, HD, 2, dtype=f32) / f32(HD))).astype(f32)
    ang = (np.arange(S, dtype=f32)[:, None] * inv[None]).astype(f32)
    ang = np.tile(ang, (1, 4)).T
    out = dict(const=const, level=level, mask0=mask0, mask1=dil(4), mask2=dil(16), cos1=np.cos(ang), sin1=np.sin(ang))
    return {n: np.ascontiguousarray(v.astype(f32)) for n, v in out.items()}


def second_arrays(c, ctx, c_ctx, norm1_gain, norm2_gain, w_ada, b_ada, w_in, w_out, hgrn_lb_logits, hgrn_gn_gain,
                  rwkv_mu, rwkv_w0, rwkv_w_up, rwkv_a0, rwkv_a_up, rwkv_g_up, rwkv_kk_scale, rwkv_k_a, rwkv_r_k,
                  rwkv_ln_gain, rwkv_ln_bias, na_q_gain, na_k_gain, na_rpb, w_router_group, b_router_group,
                  w_router_expert, b_router_expert, w_exp_gate, w_exp_up, w_exp_down):
    f32 = np.float32
    out = {}
    out["ctxT"] = blocks(np.ascontiguousarray(ctx[0].T))
    out["w_ada"] = feature_tiles(w_ada[0])
    w = w_in[0]
    out["w2f"] = feature_tiles(np.concatenate([w[:, 0:768], w[:, 1280:2432], w[:, 2432:3456]], 1))
    out["w2t"] = np.stack([blocks(w[:, 768:1280]), blocks(w[:, 3456:3968])])
    out["wo2"] = feature_tiles(w_out[0])
    cond = np.stack([columns(c[0]), columns(c_ctx)], -1).reshape(P, 16)
    hlb = np.concatenate([columns(hgrn_lb_logits[0, 0]), columns(hgrn_lb_logits[1, 0]), np.zeros((P, 4), f32)], 1)
    rw = [np.zeros((P, 4), f32), columns(rwkv_kk_scale[0]), columns(rwkv_k_a[0]), columns(rwkv_r_k[0].reshape(-1)),
          columns(rwkv_w0[0, 0]), columns(rwkv_w0[0, 1]), columns(rwkv_a0[0, 0]), columns(rwkv_a0[0, 1])]
    na = [columns(np.tile(na_q_gain[0], 2)), columns(np.tile(na_k_gain[0], 2))]
    desc = rows(np.arange(8, 0, -1).astype(f32))
    out["vecs2"] = np.concatenate([cond, columns(b_ada[0]), columns(norm1_gain[0]), columns(norm2_gain[0]), hlb,
                                   columns(rwkv_mu[0]), *rw, *na, desc, np.full((P, 1), 64e-5, f32),
                                   rows(np.arange(SLOTS).astype(f32)), np.ones((P, N_EXP), f32)], 1)
    out["rows2"] = np.concatenate([rows(hgrn_gn_gain[0].reshape(-1)), rows(rwkv_ln_gain[0]), rows(rwkv_ln_bias[0])], 1)
    out["reset"] = rows((np.arange(T2) % P != 0).astype(f32))
    out["rw_up"] = np.stack([rwkv_w_up[0].reshape(P, 256), rwkv_a_up[0].reshape(P, 256), rwkv_g_up[0]], 1)
    cq, ck = np.meshgrid(np.arange(64), np.arange(64), indexing="ij")
    bias = na_rpb[0][:, :, np.clip(ck - cq + 15, 0, 30)].transpose(2, 0, 1, 3)
    out["na_table"] = np.concatenate([bias[:, :, 1:15], bias[:, :, 0:14]], 0).reshape(P, 8, 14 * 64)
    ws = np.clip(cq - 8, 0, 48)
    out["na_window"] = np.tile(np.where((ck >= ws) & (ck < ws + 16), 0.0, NEG).astype(f32), (2, 1))
    inv = (f32(10000.0) ** (-np.arange(16, dtype=f32) / f32(16))).astype(f32)
    pos = np.arange(S)
    ang = np.concatenate([(pos // 64).astype(f32)[:, None] * inv, (pos % 64).astype(f32)[:, None] * inv], -1)
    ang = np.tile(ang, (1, 4)).T
    out["cos2"], out["sin2"] = np.cos(ang).astype(f32), np.sin(ang).astype(f32)
    out["w_router"] = blocks(np.concatenate([w_router_group[0], w_router_expert[0]], 1))
    out["b_router"] = rows(np.concatenate([b_router_group[0], b_router_expert[0]]))
    out["w_gate"] = w_exp_gate[0].reshape(N_EXP, KD, P, D_EXP).transpose(0, 2, 1, 3)
    out["w_up"] = w_exp_up[0].reshape(N_EXP, KD, P, D_EXP).transpose(0, 2, 1, 3)
    out["w_down"] = w_exp_down[0].reshape(N_EXP, FT, P, D).transpose(0, 2, 1, 3)
    return out


def arrays_of(x, norm_w, w_in, conv_w, a_log, dt_bias, gdn_norm_w, w_up_a, w_up_b, w_out, final_norm_w, **r):
    w = w_in[0]
    G = 1536
    feat = [w[:, g * G:g * G + 1024] for g in range(3)] + [w[:, 4608:5120], w[:, 5120:6656], w[:, 6656:7168], w[:, 7184:9232]]
    out = constants()
    out["xT"] = blocks(np.ascontiguousarray(x[0].T))
    out["w1f"] = feature_tiles(np.concatenate(feat, 1))
    out["w1v"] = np.stack([blocks(w[:, g * G + 1024:(g + 1) * G]) for g in range(3)])
    out["w1ba"] = blocks(w[:, 7168:7184])
    out["upa"], out["upb"], out["wo1"] = feature_tiles(w_up_a[0]), feature_tiles(w_up_b[0]), feature_tiles(w_out[0])
    conv = conv_w[0].T.reshape(12, P, 4).transpose(1, 0, 2).reshape(P, 48)
    out["vecs"] = np.concatenate([columns(norm_w[0]), columns(final_norm_w), conv, rows(dt_bias[0]), rows(a_log[0]), np.full((P, 1), EPS, np.float32)], 1)
    out["gdn_gain"] = rows(np.tile(gdn_norm_w[0], 8))
    out.update(second_arrays(**{n[:-2]: v for n, v in r.items()}))
    return out


def kernel(**inputs):
    import concourse.bacc as bacc
    from concourse.bass_utils import run_bass_kernel_spmd

    nc = bacc.Bacc("TRN2", target_bir_lowering=False, num_devices=1)
    arrays = {n: np.ascontiguousarray(v) for n, v in arrays_of(**{k: np.asarray(v) for k, v in inputs.items()}).items()}
    a = {n: nc.dram_tensor("in_" + n, v.shape, mybir.dt.from_np(v.dtype), kind="ExternalInput").ap() for n, v in arrays.items()}
    out = nc.dram_tensor("out", (P, KD, S), F32, kind="ExternalOutput").ap()
    build(nc, a, out)
    r = run_bass_kernel_spmd(nc, [{"in_" + n: v for n, v in arrays.items()}], core_ids=[0])
    y = r.results[0]["out"]
    return np.ascontiguousarray(y.transpose(2, 1, 0)).reshape(1, S, D)
```

```python
import math
from contextlib import ExitStack

import numpy as np

import concourse.bass as bass
from concourse import mybir

F32 = mybir.dt.float32
ALU = mybir.AluOpType
ACT = mybir.ActivationFunctionType
AX = mybir.AxisListType

P = 128
S = 512
CTX = 256
T2 = CTX + S
D = 1024
KD = D // P
TT = S // P
TC = T2 // P
CT = CTX // P
HD = 64
N_EXP = 32
N_GRP = 4
EPG = N_EXP // N_GRP
D_EXP = 512
FT = D_EXP // P
EPS = 1e-6
NEG = -1e30
LEVELS = 7


class Kept:
    pass


class Item:

    def __init__(self, segs, values):
        self.segs, self.values = segs, values


class Chain:

    def __init__(self, eng, sem):
        self.eng, self.sem, self.n = eng, sem, 0

    def __call__(self, ins):
        self.n += 1
        ins.then_inc(self.sem, 1)
        self.eng.wait_ge(self.sem, self.n)


class Stage:

    FIRST, SET = 150, 24
    turn = 0

    def __init__(self, nc, name, *sems):
        self.nc, self.name, self.sems, self.ctx = nc, name, sems, ExitStack()

    def __enter__(self):
        nc, s = self.nc, Kept()
        assert len(self.sems) <= self.SET
        mine = self.FIRST + self.SET * (Stage.turn % 2)
        other = self.FIRST + self.SET * ((Stage.turn + 1) % 2)
        if Stage.turn:
            nc.sync.sem_clear(range(other, other + self.SET))
        Stage.turn += 1
        names = [n for n in self.sems if not n.startswith("soft")]
        self.handles = [nc.alloc_semaphore(f"{self.name}_{n}", num=mine + i) for i, n in enumerate(names)]
        s.sem = dict(zip(names, self.handles))
        for n in self.sems:
            if n.startswith("soft"):
                s.sem[n] = nc.alloc_semaphore(f"{self.name}_{n}")
        s.block = self.ctx.enter_context(self.nc.Block())
        return s

    def __exit__(self, *exc):
        self.ctx.__exit__(*exc)
        for h in self.handles:
            self.nc.release_semaphore(h)


def load_stage(nc, name, pairs):
    with Stage(nc, name, "loaded") as st:
        @st.block.sync
        def _(sync):
            for to, of in pairs:
                sync.dma_start(to, of).then_inc(st.sem["loaded"], 16)
            sync.wait_ge(st.sem["loaded"], 16 * len(pairs))


def norm_stage(nc, K, name, x_tiles, n_tok, out, gain, shift=None, square=None):
    with Stage(nc, name, "squared", "rooted", "v", "used") as st:
        sem = st.sem

        @st.block.scalar
        def _(act):
            for k in range(KD):
                if k >= 2:
                    act.wait_ge(sem["used"], k - 1)
                nc.scalar.activation(square[:, k % 2, :n_tok], x_tiles(k), ACT.Square).then_inc(sem["squared"], 1)
            rstd = K.rstd[:, 0, :n_tok]
            act.wait_ge(sem["used"], KD)
            nc.scalar.activation(rstd, K.psum[:, 0, :n_tok], ACT.Ln, scale=1.0 / D, bias=K.eps).then_inc(sem["rooted"], 1)
            act.wait_ge(sem["rooted"], 1)
            nc.scalar.activation(rstd, rstd, ACT.Exp, scale=-0.5).then_inc(sem["rooted"], 1)

        @st.block.tensor
        def _(pe):
            for k in range(KD):
                pe.wait_ge(sem["squared"], k + 1)
                m = nc.tensor.matmul(K.psum[:, 0, :n_tok], K.ones[:], square[:, k % 2, :n_tok],
                                     start=(k == 0), stop=(k == KD - 1))
                m.then_inc(sem["used"], 1)

        @st.block.vector
        def _(dve):
            link = Chain(dve, sem["v"])
            dve.wait_ge(sem["rooted"], 2)
            for k in range(KD):
                m = nc.vector.scalar_tensor_tensor(out(k), x_tiles(k), gain[:, k:k + 1], K.rstd[:, 0, :n_tok],
                                                   ALU.mult, ALU.mult)
                if shift is not None:
                    link(m)
                    nc.vector.tensor_scalar(out(k), out(k), shift[:, k:k + 1], None, ALU.add)


def project_feature(nc, K, name, weights, n_tiles, src, segs, evac, kd=KD, dve_post=None,
                    extra_sems=(), gpsimd=None, base=0):
    nseg = len(segs)
    per = 4 // nseg if nseg > 1 else 4
    wring = K.wring[:, :, :kd * P].rearrange("p s (k n) -> p s k n", k=kd)
    ns = K.nring
    with Stage(nc, name, *[f"w{j}" for j in range(ns)], "done", "emptied", "posted", "v", "a") as st:
        sem = st.sem

        @st.block.sync
        def _(sync):
            for t in range(n_tiles):
                if t >= ns:
                    sync.wait_ge(sem["done"], t - ns + 1)
                sync.dma_start(wring[:, t % ns], weights[base + t]).then_inc(sem[f"w{t % ns}"], 16)

        @st.block.tensor
        def _(pe):
            for t in range(n_tiles):
                pe.wait_ge(sem[f"w{t % ns}"], 16 * (t // ns + 1))
                if t >= per:
                    pe.wait_ge(sem["emptied"], t - per + 1)
                for g, (at, n) in enumerate(segs):
                    for k in range(kd):
                        m = nc.tensor.matmul(K.psum[:, (t % per) * nseg + g, :n], wring[:, t % ns, k],
                                             src(k)[:, at:at + n], start=(k == 0), stop=(k == kd - 1))
                m.then_inc(sem["done"], 1)

        @st.block.scalar
        def _(act):
            link = Chain(act, sem["a"])
            for t in range(n_tiles):
                act.wait_ge(sem["done"], t + 1)
                for g, (at, n) in enumerate(segs):
                    m = evac(t, g, at, n, K.psum[:, (t % per) * nseg + g, :n], link)
                m.then_inc(sem["emptied"], 1)

        if dve_post is not None:
            @st.block.vector
            def _(dve):
                link = Chain(dve, sem["v"])
                for t in range(n_tiles):
                    dve.wait_ge(sem["emptied"], t + 1)
                    dve_post(t, link)


def project_token(nc, K, name, weights, n_w, src, tiles, evac, width=512, kd=KD):
    ring = K.vring[:, :, :kd * width].rearrange("p s (k n) -> p s k n", k=kd)
    nt = len(tiles)
    with Stage(nc, name, "w0", "w1", "done", "emptied", "a") as st:
        sem = st.sem

        @st.block.sync
        def _(sync):
            for w in range(n_w):
                if w >= 2:
                    sync.wait_ge(sem["done"], (w - 1) * nt)
                sync.dma_start(ring[:, w % 2], weights(w)).then_inc(sem[f"w{w % 2}"], 16)

        @st.block.tensor
        def _(pe):
            for w in range(n_w):
                pe.wait_ge(sem[f"w{w % 2}"], 16 * (w // 2 + 1))
                for j, t in enumerate(tiles):
                    n = w * nt + j
                    if n >= 4:
                        pe.wait_ge(sem["emptied"], n - 3)
                    for k in range(kd):
                        m = nc.tensor.matmul(K.psum[:, n % 4, :width], src(k)[:, t * P:(t + 1) * P],
                                             ring[:, w % 2, k], start=(k == 0), stop=(k == kd - 1))
                    m.then_inc(sem["done"], 1)

        @st.block.scalar
        def _(act):
            for n in range(n_w * nt):
                act.wait_ge(sem["done"], n + 1)
                evac(n // nt, n % nt, K.psum[:, n % 4, :width]).then_inc(sem["emptied"], 1)


def rope_stage(nc, K, name, tiles, n, cos, sin):
    with Stage(nc, name, "rotated", "read", "scaled", "v") as st:
        sem = st.sem

        @st.block.gpsimd
        def _(pool):
            for t, x in enumerate(tiles):
                pool.wait_ge(sem["rotated"], t + 1)
                nc.gpsimd.tensor_tensor(x, x, cos, ALU.mult).then_inc(sem["scaled"], 1)

        @st.block.tensor
        def _(pe):
            for t, x in enumerate(tiles):
                if t >= 4:
                    pe.wait_ge(sem["read"], t - 3)
                nc.tensor.matmul(K.psum[:, t % 4, :n], K.rot[:], x, start=True, stop=True).then_inc(sem["rotated"], 1)

        @st.block.vector
        def _(dve):
            link = Chain(dve, sem["v"])
            for t, x in enumerate(tiles):
                dve.wait_ge(sem["rotated"], t + 1)
                nc.vector.tensor_tensor(K.tmp[:, t % 2, :n], K.psum[:, t % 4, :n], sin, ALU.mult).then_inc(sem["read"], 1)
                dve.wait_ge(sem["scaled"], t + 1)
                dve.wait_ge(sem["read"], t + 1)
                link(nc.vector.tensor_tensor(x, x, K.tmp[:, t % 2, :n], ALU.add))


def attention_stage(nc, K, name, items, s_sb, pt_sb, diag, take):
    with Stage(nc, name, "scored", "masked", "maxed", "exped", "inverse", "scaled", "turned", "copied", "mixed",
               "taken") as st:
        sem = st.sem
        n_items = len(items)

        @st.block.tensor
        def _(pe):
            def turn(i):
                pe.wait_ge(sem["scaled"], i + 1)
                if i >= 1:
                    pe.wait_ge(sem["copied"], i)
                for j in range(len(items[i].values)):
                    m = nc.tensor.matmul(K.psum[:, 3 + j // 4, (j % 4) * P:(j % 4 + 1) * P],
                                         s_sb[:, i % 3, j * P:(j + 1) * P], diag[:, i % 2], start=True, stop=True)
                m.then_inc(sem["turned"], 1)

            def mix(p):
                n_keys = len(items[2 * p].values)
                pe.wait_ge(sem["copied"], 2 * p + 2)
                if p >= 2:
                    pe.wait_ge(sem["taken"], p - 1)
                for j in range(n_keys):
                    for par in range(2):
                        i = 2 * p + par
                        m = nc.tensor.matmul(K.psum[par * HD:(par + 1) * HD, 6 + p % 2, :P], items[i].values[j],
                                             pt_sb[:, i % 4, j * P:(j + 1) * P], start=(j == 0), stop=(j == n_keys - 1))
                m.then_inc(sem["mixed"], 1)

            for i in range(n_items + 3):
                if i < n_items:
                    if i >= 1:
                        pe.wait_ge(sem["masked"], i)
                    for b, (q, k, n, col, mask) in enumerate(items[i].segs):
                        m = nc.tensor.matmul(K.psum[:, b, :n], q, k, start=True, stop=True)
                    m.then_inc(sem["scored"], 1)
                if 2 <= i < n_items + 2:
                    turn(i - 2)
                if i >= 4 and i % 2 == 0:
                    mix((i - 4) // 2)

        @st.block.gpsimd
        def _(pool):
            for i in range(n_items):
                pool.wait_ge(sem["inverse"], i + 1)
                if i >= 2:
                    pool.wait_ge(sem["turned"], i - 1)
                nc.gpsimd.tensor_scalar(diag[:, i % 2], K.ident[:], K.stat[:, 6 + i % 2:7 + i % 2], None,
                                        ALU.mult).then_inc(sem["scaled"], 1)

        @st.block.vector
        def _(dve):
            def take_pair(p):
                dve.wait_ge(sem["mixed"], p + 1)
                take(p, K.psum[:, 6 + p % 2, :P]).then_inc(sem["taken"], 1)

            def invert(i):
                dve.wait_ge(sem["exped"], i + 1)
                if i >= 2:
                    dve.wait_ge(sem["scaled"], i - 1)
                nc.vector.reciprocal(K.stat[:, 6 + i % 2:7 + i % 2], K.stat[:, 2 + i % 4:3 + i % 4]).then_inc(sem["inverse"], 1)

            for i, it in enumerate(items):
                dve.wait_ge(sem["scored"], i + 1)
                if i >= 3:
                    dve.wait_ge(sem["turned"], i - 2)
                for b, (q, k, n, col, mask) in enumerate(it.segs):
                    to = s_sb[:, i % 3, col:col + n]
                    if mask is None:
                        m = nc.vector.tensor_scalar(to, K.psum[:, b, :n], HD ** -0.5, None, ALU.mult)
                    else:
                        m = nc.vector.scalar_tensor_tensor(to, K.psum[:, b, :n], HD ** -0.5, mask, ALU.mult, ALU.add)
                m.then_inc(sem["masked"], 1)
                if i >= 1:
                    invert(i - 1)
                dve.wait_ge(sem["masked"], i + 1)
                n_all = len(it.values) * P
                nc.vector.tensor_reduce(K.stat[:, i % 2:i % 2 + 1], s_sb[:, i % 3, :n_all], AX.X, ALU.max,
                                        negate=True).then_inc(sem["maxed"], 1)
                if i >= 5 and i % 2 == 1:
                    take_pair((i - 5) // 2)
            invert(n_items - 1)
            for p in range(n_items // 2 - 2, n_items // 2):
                take_pair(p)

        @st.block.scalar
        def _(act):
            def copy(i):
                act.wait_ge(sem["turned"], i + 1)
                if i >= 4:
                    act.wait_ge(sem["mixed"], i // 2 - 1)
                n_keys = len(items[i].values)
                for b in range(0, n_keys, 4):
                    n = min(4, n_keys - b) * P
                    m = nc.scalar.activation(pt_sb[:, i % 4, b * P:b * P + n], K.psum[:, 3 + b // 4, :n], ACT.Copy)
                m.then_inc(sem["copied"], 1)

            for i, it in enumerate(items):
                if i >= 2:
                    copy(i - 2)
                n_all = len(it.values) * P
                act.wait_ge(sem["maxed"], i + 1)
                if i >= 4:
                    act.wait_ge(sem["inverse"], i - 3)
                nc.scalar.activation(s_sb[:, i % 3, :n_all], s_sb[:, i % 3, :n_all], ACT.Exp,
                                     bias=K.stat[:, i % 2:i % 2 + 1],
                                     accum_out=K.stat[:, 2 + i % 4:3 + i % 4]).then_inc(sem["exped"], 1)
            copy(n_items - 2)
            copy(n_items - 1)


def turn_stage(nc, K, name, jobs, emit):
    groups = [jobs[i:i + 4] for i in range(0, len(jobs), 4)]
    with Stage(nc, name, "turned", "taken") as st:
        sem = st.sem

        @st.block.tensor
        def _(pe):
            for g, group in enumerate(groups):
                if g >= 4:
                    pe.wait_ge(sem["taken"], g - 3)
                for j, x in enumerate(group):
                    m = nc.tensor.transpose(K.psum[:, g % 4, j * P:(j + 1) * P], x, K.ident[:])
                m.then_inc(sem["turned"], 1)

        @st.block.vector
        def _(dve):
            for g, group in enumerate(groups):
                dve.wait_ge(sem["turned"], g + 1)
                emit(g, K.psum[:, g % 4, :len(group) * P]).then_inc(sem["taken"], 1)


def first_block(nc, K, a, x1):
    top = ExitStack()

    def sb(name, shape, stack=top):
        return stack.enter_context(nc.sbuf_tensor(name, shape, F32))

    h = sb("h1", [P, KD, S])
    K.gdn_gain = sb("gdn_gain", [P, S])
    load_stage(nc, "lx", [(x1[:], a["xT"]), (K.gdn_gain[:], a["gdn_gain"])])
    norm_stage(nc, K, "n1", lambda k: x1[:, k], S, lambda k: h[:, k], K.vec_norm, square=K.tmp)
    gatedA = sb("gatedA", [P, 4, S])
    gatedB = sb("gatedB", [P, 4, S])
    with ExitStack() as ph:
        qk = sb("qk", [P, 24, S], ph)
        v, z = sb("v", [P, 3, TT, S], ph), sb("z_dsa", [P, 4, S], ph)
        with ExitStack() as ph2:
            rings(nc, K, ph2, "a", vring=True)
            project_feature(nc, K, "pqk", a["w1f"], 24, lambda k: h[:, k], [(0, S)],
                            lambda t, g, at, n, ps, link: nc.scalar.activation(qk[:, t], ps, ACT.Copy))
            project_token(nc, K, "pv", lambda w: a["w1v"][w], 3, lambda k: h[:, k], range(TT),
                          lambda w, t, ps: nc.scalar.activation(v[:, w, t], ps, ACT.Copy))
            project_feature(nc, K, "pz", a["w1f"], 4, lambda k: h[:, k], [(0, S)],
                            lambda t, g, at, n, ps, link: nc.scalar.activation(z[:, t], ps, ACT.Silu), base=24)
        with ExitStack() as ph2:
            mask0 = sb("mask0", [P, 2 * P], ph2)
            mask1 = sb("mask1", [P, 4 * P], ph2)
            mask2 = sb("mask2", [P, 4 * P], ph2)
            cos, sin = sb("cos1", [P, S], ph2), sb("sin1", [P, S], ph2)
            load_stage(nc, "lm", [(mask0[:], a["mask0"]), (mask1[:], a["mask1"]), (mask2[:], a["mask2"]),
                                  (cos[:], a["cos1"]), (sin[:], a["sin1"])])
            rope_stage(nc, K, "r1", [qk[:, t] for t in range(24)], S, cos[:], sin[:])
            s_sb = sb("s_sb", [P, 3, 10 * P], ph2)
            pt_sb = sb("pt_sb", [P, 4, 10 * P], ph2)
            items = []
            diag = sb("diag1", [P, 2, P], ph2)
            for m in range(4):
                for t, hh in [(t, hh) for t in range(TT) for hh in (2 * m, 2 * m + 1)]:
                    r = (hh % 2) * HD
                    lo = max(0, t - 1)
                    n0, n1 = (t + 1 - lo) * P, (t + 1) * P
                    segs, vals, col = [], [], 0
                    for g, (k0, n, mask) in enumerate([(lo, n0, mask0[:, 2 * P - n0:]),
                                                       (0, n1, mask1[:, 4 * P - n1:]),
                                                       (0, n1, mask2[:, 4 * P - n1:])]):
                        segs.append((qk[r:r + HD, 8 * g + m, t * P:(t + 1) * P],
                                     qk[r:r + HD, 8 * g + 4 + m, k0 * P:k0 * P + n], n, col, mask))
                        vals += [v[:, g, k0 + j, hh * HD:(hh + 1) * HD] for j in range(n // P)]
                        col += n
                    items.append(Item(segs, vals))
            attention_stage(nc, K, "dsa", items, s_sb, pt_sb, diag,
                            lambda p, ps: nc.vector.tensor_tensor(gatedA[:, p // TT, p % TT * P:(p % TT + 1) * P], ps,
                                                                  z[:, p // TT, p % TT * P:(p % TT + 1) * P], ALU.mult))
    gated_delta(nc, K, a, h, gatedB)
    with ExitStack() as ph:
        rings(nc, K, ph, "u")
        merged = sb("merged", [P, KD, S], ph)
        gate = sb("gate", [P, 2, S], ph)
        merge_stage(nc, K, a, h, gatedA, gatedB, merged)
        out_stage(nc, K, "po1", a["wo1"], lambda k: merged[:, k], x1, None)
    norm_stage(nc, K, "n2", lambda k: x1[:, k], S, lambda k: x1[:, k], K.vec_fnorm, square=K.tmp)
    top.close()


def rings(nc, K, stack, name, vring=False, n=4):
    K.nring = n
    K.wring = stack.enter_context(nc.sbuf_tensor(f"wring_{name}", [P, n, KD * P], F32))
    if vring:
        K.vring = stack.enter_context(nc.sbuf_tensor(f"vring_{name}", [P, 2, KD * 512], F32))


def merge_stage(nc, K, a, h, gatedA, gatedB, merged):
    def src(j, k):
        return h[:, k] if j % 2 == 0 else (gatedA, gatedB)[j // 2][:, k]

    with Stage(nc, "merge", "w0", "w1", "w2", "w3", "done", "gated", "taken", "v") as st:
        sem = st.sem

        def slot(j, k):
            return K.wring[:, j, k * P:(k + 1) * P]

        @st.block.sync
        def _(sync):
            for n in range(KD):
                for j in range(4):
                    i = 4 * n + j
                    if i >= 4:
                        sync.wait_ge(sem["done"], i - 3)
                    if j % 2 == 0:
                        sync.dma_start(K.wring[:, j], a["w1f"][44 + 8 * (j // 2) + n].rearrange("p k n -> p (k n)")).then_inc(sem[f"w{j}"], 16)
                    else:
                        sync.dma_start(K.wring[:, j, :4 * P], (a["upa"], a["upb"])[j // 2][n].rearrange("p k n -> p (k n)")).then_inc(sem[f"w{j}"], 16)

        @st.block.tensor
        def _(pe):
            for i in range(4 * KD):
                j = i % 4
                pe.wait_ge(sem[f"w{j}"], 16 * (i // 4 + 1))
                if i >= 8:
                    pe.wait_ge(sem["taken"], i // 4 - 1)
                nk = KD if j % 2 == 0 else 4
                for k in range(nk):
                    m = nc.tensor.matmul(K.psum[:, i % 8], slot(j, k), src(j, k), start=(k == 0), stop=(k == nk - 1))
                m.then_inc(sem["done"], 1)

        @st.block.scalar
        def _(act):
            for n in range(KD):
                for g in range(2):
                    act.wait_ge(sem["done"], 4 * n + 2 * g + 1)
                    if n >= 1:
                        act.wait_ge(sem["taken"], n)
                    nc.scalar.activation(K.tmp[:, g], K.psum[:, (4 * n + 2 * g) % 8], ACT.Sigmoid).then_inc(sem["gated"], 1)

        @st.block.vector
        def _(dve):
            link = Chain(dve, sem["v"])
            for n in range(KD):
                dve.wait_ge(sem["done"], 4 * n + 4)
                dve.wait_ge(sem["gated"], 2 * n + 2)
                b = (4 * n) % 8
                nc.vector.tensor_tensor(merged[:, n], K.tmp[:, 0], K.psum[:, b + 1], ALU.mult)
                link(nc.vector.tensor_tensor(K.rstd[:, 0], K.tmp[:, 1], K.psum[:, b + 3], ALU.mult))
                nc.vector.tensor_tensor(merged[:, n], merged[:, n], K.rstd[:, 0], ALU.add).then_inc(sem["taken"], 1)
                dve.wait_ge(sem["taken"], n + 1)


def out_stage(nc, K, name, weights, src, x, gain):
    ns = K.nring
    wring = K.wring[:].rearrange("p s (k n) -> p s k n", k=KD)
    with Stage(nc, name, *[f"w{j}" for j in range(ns)], "done", "taken") as st:
        sem = st.sem

        @st.block.sync
        def _(sync):
            for t in range(KD):
                if t >= ns:
                    sync.wait_ge(sem["done"], t - ns + 1)
                sync.dma_start(wring[:, t % ns], weights[t]).then_inc(sem[f"w{t % ns}"], 16)

        @st.block.tensor
        def _(pe):
            for t in range(KD):
                pe.wait_ge(sem[f"w{t % ns}"], 16 * (t // ns + 1))
                if t >= 4:
                    pe.wait_ge(sem["taken"], t - 3)
                for k in range(KD):
                    m = nc.tensor.matmul(K.psum[:, t % 4], wring[:, t % ns, k], src(k), start=(k == 0), stop=(k == KD - 1))
                m.then_inc(sem["done"], 1)

        @st.block.vector
        def _(dve):
            for t in range(KD):
                dve.wait_ge(sem["done"], t + 1)
                if gain is None:
                    m = nc.vector.tensor_tensor(x[:, t], K.psum[:, t % 4], x[:, t], ALU.add)
                else:
                    m = nc.vector.scalar_tensor_tensor(x[:, t], K.psum[:, t % 4], gain[:, t:t + 1], x[:, t], ALU.mult, ALU.add)
                m.then_inc(sem["taken"], 1)


def over_heads(ap, n=HD):
    shape = list(ap.shape) + [n]
    return ap.unsqueeze(len(ap.shape)).broadcast_to(shape)


def over_rows(ap, n):
    return ap.unsqueeze(1).broadcast_to([ap.shape[0], n] + list(ap.shape[1:]))


def invert_stage(nc, K, name, at, xt, n_batch, upper, work, lanes=4):
    bt, xs, ys = work[:, 0], work[:, 1], work[:, 2]
    steps = [(lanes * g + lane, lv, lane) for g in range(n_batch // lanes) for lv in range(LEVELS) for lane in range(lanes)]
    has_xy = [lv > 0 for b, lv, lane in steps]
    with Stage(nc, name, "between", "y", "ycopied", "xy", "updated") as st:
        sem = st.sem

        def count_xy(s):
            return sum(has_xy[:s + 1])

        @st.block.gpsimd
        def _(pool):
            for s, (b, lv, lane) in enumerate(steps):
                if s >= lanes:
                    pool.wait_ge(sem["y"], s - lanes + 1)
                    if not has_xy[s - lanes]:
                        pool.wait_ge(sem["updated"], s - lanes + 1)
                mask = K.level[:, (LEVELS if upper(b) else 0) + lv]
                nc.gpsimd.tensor_tensor(bt[:, lane], at[:, b], over_rows(mask, 4), ALU.mult).then_inc(sem["between"], 1)

        @st.block.tensor
        def _(pe):
            def products(s):
                b, lv, lane = steps[s]
                pe.wait_ge(sem["ycopied"], s + 1)
                if s >= 2:
                    pe.wait_ge(sem["updated"], s - 1)
                for i in range(4):
                    if lv < LEVELS - 1:
                        nc.tensor.matmul(K.psum[:, 2 + 2 * (s % 2), i * P:(i + 1) * P], xt[:, b, i], ys[:, lane, i], start=True, stop=True)
                    m = nc.tensor.matmul(K.psum[:, 3 + 2 * (s % 2), i * P:(i + 1) * P], ys[:, lane, i], xt[:, b, i], start=True, stop=True)
                m.then_inc(sem["xy"], 1)

            for s, (b, lv, lane) in enumerate(steps):
                pe.wait_ge(sem["between"], s + 1)
                if s >= lanes:
                    pe.wait_ge(sem["updated"], s - lanes + 1)
                if s >= 2:
                    pe.wait_ge(sem["ycopied"], s - 1)
                for i in range(4):
                    x = K.ident[:] if lv == 0 else xs[:, lane, i]
                    m = nc.tensor.matmul(K.psum[:, s % 2, i * P:(i + 1) * P], bt[:, lane, i], x, start=True, stop=True)
                m.then_inc(sem["y"], 1)
                if s >= 1 and has_xy[s - 1]:
                    products(s - 1)
            products(len(steps) - 1)

        @st.block.scalar
        def _(act):
            for s, (b, lv, lane) in enumerate(steps):
                act.wait_ge(sem["y"], s + 1)
                if s >= lanes and has_xy[s - lanes]:
                    act.wait_ge(sem["xy"], count_xy(s - lanes))
                elif s >= lanes:
                    act.wait_ge(sem["updated"], s - lanes + 1)
                nc.scalar.activation(ys[:, lane], K.psum[:, s % 2].rearrange("p (i n) -> p i n", i=4), ACT.Copy).then_inc(sem["ycopied"], 1)

        @st.block.vector
        def _(dve):
            for s, (b, lv, lane) in enumerate(steps):
                if not has_xy[s]:
                    dve.wait_ge(sem["ycopied"], s + 1)
                    eye = over_rows(K.ident[:], 4)
                    nc.vector.tensor_tensor(xs[:, lane], eye, ys[:, lane], ALU.subtract)
                    nc.vector.tensor_tensor(xt[:, b], eye, bt[:, lane], ALU.subtract).then_inc(sem["updated"], 1)
                    continue
                dve.wait_ge(sem["xy"], count_xy(s))
                xy = K.psum[:, 2 + 2 * (s % 2)].rearrange("p (i n) -> p i n", i=4)
                yx = K.psum[:, 3 + 2 * (s % 2)].rearrange("p (i n) -> p i n", i=4)
                if lv < LEVELS - 1:
                    nc.vector.tensor_tensor(xs[:, lane], xs[:, lane], xy, ALU.subtract)
                nc.vector.tensor_tensor(xt[:, b], xt[:, b], yx, ALU.subtract).then_inc(sem["updated"], 1)


def head_norm_stage(nc, K, name, x, nt, nh, gain, square, stat, bias=None, eps=None):
    with Stage(nc, name, "squared", "summed", "rooted", "v") as st:
        sem = st.sem

        @st.block.scalar
        def _(act):
            for t in range(nt):
                nc.scalar.activation(square[:, t], x[:, t], ACT.Square).then_inc(sem["squared"], 1)
            act.wait_ge(sem["summed"], 1)
            nc.scalar.activation(stat, stat, ACT.Ln, scale=1.0 / HD, bias=K.eps if eps is None else eps).then_inc(sem["rooted"], 1)
            act.wait_ge(sem["rooted"], 1)
            nc.scalar.activation(stat, stat, ACT.Exp, scale=-0.5).then_inc(sem["rooted"], 1)

        @st.block.vector
        def _(dve):
            link = Chain(dve, sem["v"])
            dve.wait_ge(sem["squared"], nt)
            nc.vector.tensor_reduce(stat, square.rearrange("p t (h d) -> p (t h) d", d=HD), AX.X, ALU.add).then_inc(sem["summed"], 1)
            dve.wait_ge(sem["rooted"], 2)
            for t in range(nt):
                xh = x[:, t].rearrange("p (h d) -> p h d", d=HD)
                link(nc.vector.tensor_tensor(xh, xh, over_heads(stat[:, t * nh:(t + 1) * nh]), ALU.mult))
                link(nc.vector.tensor_tensor(x[:, t], x[:, t], gain, ALU.mult))
                if bias is not None:
                    link(nc.vector.tensor_tensor(x[:, t], x[:, t], bias, ALU.add))


def rms_stage(nc, K, name, tiles, n, gains, mean=1.0):
    groups = [range(g, min(g + 4, len(tiles))) for g in range(0, len(tiles), 4)]
    with Stage(nc, name, "squared", "summed", "logged", "rooted", "v") as st:
        sem = st.sem

        @st.block.scalar
        def _(act):
            for group in groups:
                for t in group:
                    if t >= 2:
                        act.wait_ge(sem["summed"], t - 1)
                    nc.scalar.activation(K.tmp[:, t % 2, :n(t)], tiles[t], ACT.Square).then_inc(sem["squared"], 1)
                for t in group:
                    r = K.psum[:, t % 8, :n(t)]
                    act.wait_ge(sem["summed"], t + 1)
                    nc.scalar.activation(r, r, ACT.Ln, scale=mean, bias=K.eps).then_inc(sem["logged"], 1)
                for t in group:
                    r = K.psum[:, t % 8, :n(t)]
                    act.wait_ge(sem["logged"], t + 1)
                    nc.scalar.activation(r, r, ACT.Exp, scale=-0.5).then_inc(sem["rooted"], 1)

        @st.block.tensor
        def _(pe):
            for t in range(len(tiles)):
                pe.wait_ge(sem["squared"], t + 1)
                if t >= 8:
                    pe.wait_ge(sem["v"], t - 7)
                nc.tensor.matmul(K.psum[:, t % 8, :n(t)], K.head_ones[:], K.tmp[:, t % 2, :n(t)], start=True, stop=True).then_inc(sem["summed"], 1)

        @st.block.vector
        def _(dve):
            for t, x in enumerate(tiles):
                dve.wait_ge(sem["rooted"], t + 1)
                nc.vector.scalar_tensor_tensor(x, K.psum[:, t % 8, :n(t)], gains[t], x, ALU.mult, ALU.mult).then_inc(sem["v"], 1)


def l2_stage(nc, K, name, tiles, n, gains, floor):
    with Stage(nc, name, "squared", "summed", "floored", "rooted", "inverse", "v") as st:
        sem = st.sem

        @st.block.scalar
        def _(act):
            def root(t):
                r = K.rstd[:, t % 2, :n(t)]
                if t >= 2:
                    act.wait_ge(sem["v"], t - 1)
                act.wait_ge(sem["floored"], t + 1)
                nc.scalar.activation(r, r, ACT.Sqrt).then_inc(sem["rooted"], 1)

            for t, x in enumerate(tiles):
                if t >= 2:
                    act.wait_ge(sem["summed"], t - 1)
                nc.scalar.activation(K.tmp[:, t % 2, :n(t)], x, ACT.Square).then_inc(sem["squared"], 1)
                if t >= 1:
                    root(t - 1)
            root(len(tiles) - 1)

        @st.block.tensor
        def _(pe):
            for t, x in enumerate(tiles):
                pe.wait_ge(sem["squared"], t + 1)
                if t >= 4:
                    pe.wait_ge(sem["floored"], t - 3)
                nc.tensor.matmul(K.psum[:, t % 4, :n(t)], K.head_ones[:], K.tmp[:, t % 2, :n(t)], start=True, stop=True).then_inc(sem["summed"], 1)

        @st.block.vector
        def _(dve):
            for t, x in enumerate(tiles):
                r = K.rstd[:, t % 2, :n(t)]
                dve.wait_ge(sem["summed"], t + 1)
                nc.vector.tensor_scalar(r, K.psum[:, t % 4, :n(t)], floor, None, ALU.max).then_inc(sem["floored"], 1)
                dve.wait_ge(sem["rooted"], t + 1)
                nc.vector.reciprocal(r, r).then_inc(sem["inverse"], 1)
                dve.wait_ge(sem["inverse"], t + 1)
                nc.vector.scalar_tensor_tensor(x, r, gains[t], x, ALU.mult, ALU.mult).then_inc(sem["v"], 1)


def gated_delta(nc, K, a, h, gatedB):
    ph = ExitStack()

    def sb(name, shape, stack=ph):
        return stack.enter_context(nc.sbuf_tensor(name, shape, F32))

    at, xt, attn = sb("g_at", [P, 8, 4, P]), sb("g_xt", [P, 8, 4, P]), sb("g_attn", [P, 8, 4, P])
    k_decay, v_beta = sb("g_kdecay", [P, TT, S]), sb("g_vbeta", [P, TT, S])
    q_e, kb_e, row_e = sb("g_qe", [P, 4, S]), sb("g_kbe", [P, 4, S]), sb("g_rowe", [P, 4, S])
    z = sb("g_z", [P, 4, S])
    ba = sb("g_ba", [P, TT, 16])
    g, beta, Gt, g_scr = sb("g_g", [P, TT, 8]), sb("g_beta", [P, TT, 8]), sb("g_G", [P, TT * 8]), sb("g_scr", [P, 2, TT * 8])
    with ExitStack() as p2:
        qkv = sb("g_qkv", [P, 12, S], p2)
        with ExitStack() as p3:
            rings(nc, K, p3, "g", n=3)
            K.vring = p3.enter_context(nc.sbuf_tensor("vring_g", [P, 2, KD * 16], F32))
            x_c = sb("g_xc", [P, 2, S + 3], p3)
            with Stage(nc, "gz", "m") as st:
                @st.block.vector
                def _(dve):
                    nc.vector.memset(x_c[:, :, 0:3], 0.0)

            conv_stage(nc, K, a, h, x_c, qkv)
            project_feature(nc, K, "gpz", a["w1f"], 4, lambda k: h[:, k], [(0, S)],
                            lambda t, g_, at_, n, ps, link: nc.scalar.activation(z[:, t], ps, ACT.Silu), base=40)
            project_token(nc, K, "gba", lambda w: a["w1ba"], 1, lambda k: h[:, k], range(TT),
                          lambda w, t, ps: nc.scalar.activation(ba[:, t], ps, ACT.Copy), width=16)
        rms_stage(nc, K, "gl2", [qkv[:, t] for t in range(8)], lambda t: S, [HD ** -0.5] * 4 + [1.0] * 4)

        with Stage(nc, "gg", "v", "x0", "x", "e") as st:
            sem = st.sem
            x, y = g_scr[:, 0].rearrange("p (t h) -> p t h", h=8), g_scr[:, 1].rearrange("p (t h) -> p t h", h=8)

            @st.block.vector
            def _(dve):
                link = Chain(dve, sem["v"])
                link(nc.vector.tensor_tensor(x, ba[:, :, 8:16], over_rows(K.dt_bias[:], TT), ALU.add))
                nc.vector.tensor_tensor(y, ba[:, :, 8:16], over_rows(K.dt_bias[:], TT), ALU.add).then_inc(sem["x0"], 1)
                nc.vector.tensor_scalar(x, x, 0.0, None, ALU.max).then_inc(sem["x"], 1)
                dve.wait_ge(sem["x"], 1)
                dve.wait_ge(sem["e"], 5)
                link(nc.vector.tensor_tensor(x, x, y, ALU.add))
                link(nc.vector.tensor_tensor(g[:], x, over_rows(K.a_log[:], TT), ALU.mult))
                link(nc.vector.tensor_scalar(g[:], g[:], -1.0, None, ALU.mult))

            @st.block.scalar
            def _(act):
                nc.scalar.activation(beta[:], ba[:, :, 0:8], ACT.Sigmoid).then_inc(sem["e"], 1)
                act.wait_ge(sem["x0"], 1)
                nc.scalar.activation(K.a_log[:], K.a_log[:], ACT.Exp).then_inc(sem["e"], 1)
                nc.scalar.activation(y, y, ACT.Abs).then_inc(sem["e"], 1)
                act.wait_ge(sem["e"], 3)
                nc.scalar.activation(y, y, ACT.Exp, scale=-1.0).then_inc(sem["e"], 1)
                act.wait_ge(sem["e"], 4)
                nc.scalar.activation(y, y, ACT.Ln, bias=1.0).then_inc(sem["e"], 1)

        p3 = ExitStack()
        wide = sb("g_wide", [P, 2, TT * 8, HD], p3)
        with Stage(nc, "gc", "wide", "sums", "rows", "betas", "v", "exped", "kb", "d") as st:
            sem = st.sem

            @st.block.gpsimd
            def _(pool):
                nc.gpsimd.tensor_copy(wide[:, 0], over_heads(g[:].rearrange("p t h -> p (t h)"))).then_inc(sem["wide"], 1)
                nc.gpsimd.tensor_copy(wide[:, 1], over_heads(beta[:].rearrange("p t h -> p (t h)"))).then_inc(sem["wide"], 1)

            def pair(which, c, m):
                return wide[:, which, 8 * c + 2 * m:8 * c + 2 * m + 2].rearrange("p a b -> p (a b)")

            @st.block.tensor
            def _(pe):
                pe.wait_ge(sem["wide"], 2)
                gf = g[:].rearrange("p t h -> p (t h)")
                nc.tensor.matmul(K.psum[:, 0, 0:32], K.upto[:], gf, start=True, stop=True)
                nc.tensor.matmul(K.psum[:, 0, 32:64], K.ones[:], gf, start=True, stop=True).then_inc(sem["sums"], 1)
                for m in range(4):
                    for c in range(TT):
                        ins = nc.tensor.matmul(K.psum[:, 1 + m % 3, c * P:(c + 1) * P], pair(0, c, m),
                                               K.upto[:], start=True, stop=True) if m < 3 else None
                    if m < 3:
                        ins.then_inc(sem["rows"], 1)
                for m in range(4):
                    for c in range(TT):
                        ins = nc.tensor.matmul(K.psum[:, 4 + m, c * P:(c + 1) * P], pair(1, c, m),
                                               K.ident[:], start=True, stop=True)
                    ins.then_inc(sem["betas"], 1)
                pe.wait_ge(sem["exped"], 1)
                for c in range(TT):
                    ins = nc.tensor.matmul(K.psum[:, 1, c * P:(c + 1) * P], pair(0, c, 3), K.upto[:], start=True, stop=True)
                ins.then_inc(sem["rows"], 1)

            @st.block.scalar
            def _(act):
                for m in range(4):
                    act.wait_ge(sem["rows"], m + 1)
                    nc.scalar.activation(row_e[:, m], K.psum[:, 1 + m % 3], ACT.Exp).then_inc(sem["exped"], 1)
                act.wait_ge(sem["d"], 1)
                nc.scalar.activation(g_scr[:, 0], g_scr[:, 0], ACT.Exp).then_inc(sem["exped"], 1)

            @st.block.vector
            def _(dve):
                link = Chain(dve, sem["v"])
                dve.wait_ge(sem["sums"], 1)
                link(nc.vector.tensor_copy(Gt[:], K.psum[:, 0, 0:32]))
                nc.vector.tensor_tensor(g_scr[:, 0], K.psum[:, 0, 32:64], Gt[:], ALU.subtract).then_inc(sem["d"], 1)
                for m in range(4):
                    dve.wait_ge(sem["betas"], m + 1)
                    link(nc.vector.tensor_tensor(kb_e[:, m], qkv[:, 4 + m], K.psum[:, 4 + m], ALU.mult))
                    dve.wait_ge(sem["exped"], m + 1)
                    link(nc.vector.tensor_tensor(q_e[:, m], qkv[:, m], row_e[:, m], ALU.mult))

        p3.close()

        kd = g_scr[:, 0].rearrange("p (t h) -> p t h", h=8)
        turn_stage(nc, K, "gtk", [qkv[:, 4 + m, c * P:(c + 1) * P] for c in range(TT) for m in range(4)],
                   lambda c, ps: nc.vector.tensor_tensor(k_decay[:, c].rearrange("p (h d) -> p h d", d=HD),
                                                         ps.rearrange("p (h d) -> p h d", d=HD), over_heads(kd[:, c]), ALU.mult))
        turn_stage(nc, K, "gtv", [qkv[:, 8 + m, c * P:(c + 1) * P] for c in range(TT) for m in range(4)],
                   lambda c, ps: nc.vector.tensor_tensor(v_beta[:, c].rearrange("p (h d) -> p h d", d=HD),
                                                         ps.rearrange("p (h d) -> p h d", d=HD), over_heads(beta[:, c]), ALU.mult))

        dec = sb("g_dec", [P, 2, 4, P], p2)
        dec2 = sb("g_dec2", [P, 2, 2, 4, P], p2)
        with Stage(nc, "gm", "rowed", "prods", "diffed", "exped", "masked", "used", "v") as st:
            sem = st.sem
            batches = [(c, half) for c in range(TT) for half in range(2)]

            @st.block.tensor
            def _(pe):
                for b, (c, half) in enumerate(batches):
                    if b >= 1:
                        pe.wait_ge(sem["diffed"], b)
                    for i in range(4):
                        hh = 2 * i + half
                        ins = nc.tensor.matmul(K.psum[:, 0, i * P:(i + 1) * P], g[:, c, hh:hh + 1].broadcast_to([P, P]),
                                               K.upto[:], start=True, stop=True)
                    ins.then_inc(sem["rowed"], 1)
                    if b >= 2:
                        pe.wait_ge(sem["used"], b - 1)
                    for i in range(4):
                        hh = 2 * i + half
                        m, r = hh // 2, (hh % 2) * HD
                        kk = qkv[r:r + HD, 4 + m, c * P:(c + 1) * P]
                        nc.tensor.matmul(K.psum[:, 1 + 2 * (b % 2), i * P:(i + 1) * P], kk, kb_e[r:r + HD, m, c * P:(c + 1) * P], start=True, stop=True)
                        ins = nc.tensor.matmul(K.psum[:, 2 + 2 * (b % 2), i * P:(i + 1) * P], kk, qkv[r:r + HD, m, c * P:(c + 1) * P], start=True, stop=True)
                    ins.then_inc(sem["prods"], 1)

            @st.block.vector
            def _(dve):
                def use(b):
                    dve.wait_ge(sem["prods"], b + 1)
                    dve.wait_ge(sem["masked"], b + 1)
                    nc.vector.tensor_tensor(at[:, b], K.psum[:, 1 + 2 * (b % 2)].rearrange("p (i n) -> p i n", i=4), dec2[:, b % 2, 0], ALU.mult)
                    nc.vector.tensor_tensor(attn[:, b], K.psum[:, 2 + 2 * (b % 2)].rearrange("p (i n) -> p i n", i=4), dec2[:, b % 2, 1], ALU.mult).then_inc(sem["used"], 1)

                for b, (c, half) in enumerate(batches):
                    dve.wait_ge(sem["rowed"], b + 1)
                    if b >= 2:
                        dve.wait_ge(sem["masked"], b - 1)
                    for i in range(4):
                        hh = 8 * c + 2 * i + half
                        ins = nc.vector.tensor_scalar(dec[:, b % 2, i], K.psum[:, 0, i * P:(i + 1) * P], Gt[:, hh:hh + 1], 0.0, ALU.subtract, ALU.min)
                    ins.then_inc(sem["diffed"], 1)
                    if b >= 1:
                        use(b - 1)
                use(len(batches) - 1)

            @st.block.scalar
            def _(act):
                for b in range(len(batches)):
                    act.wait_ge(sem["diffed"], b + 1)
                    nc.scalar.activation(dec[:, b % 2], dec[:, b % 2], ACT.Exp).then_inc(sem["exped"], 1)

            @st.block.gpsimd
            def _(pool):
                for b in range(len(batches)):
                    pool.wait_ge(sem["exped"], b + 1)
                    if b >= 2:
                        pool.wait_ge(sem["used"], b - 1)
                    nc.gpsimd.tensor_tensor(dec2[:, b % 2, 0], dec[:, b % 2], over_rows(K.before[:], 4), ALU.mult)
                    nc.gpsimd.tensor_tensor(dec2[:, b % 2, 1], dec[:, b % 2], over_rows(K.upto[:], 4), ALU.mult).then_inc(sem["masked"], 1)

        with Stage(nc, "gk", "v") as st:
            @st.block.vector
            def _(dve):
                for m in range(4):
                    nc.vector.tensor_tensor(kb_e[:, m], kb_e[:, m], row_e[:, m], ALU.mult)
    with ExitStack() as p2:
        work = sb("g_work", [P, 3, 4, 4, P], p2)
        invert_stage(nc, K, "gi", at, xt, 8, lambda b: False, work)
    o = sb("g_o", [P, TT, S])
    with ExitStack() as p2:
        state = sb("g_state", [P, 4, P], p2)
        zz, vn, upd = sb("g_zz", [P, S], p2), sb("g_vn", [P, S], p2), sb("g_upd", [P, 4, P], p2)
        with Stage(nc, "gs", "ks", "z", "vn", "vcopied", "kv", "out", "state", "v", "ocopied") as st:
            sem = st.sem

            @st.block.tensor
            def _(pe):
                for c in range(TT):
                    pe.wait_ge(sem["state"], c + 1)
                    for m in range(4):
                        ins = nc.tensor.matmul(K.psum[:, 0, m * P:(m + 1) * P], kb_e[:, m, c * P:(c + 1) * P], state[:, m], start=True, stop=True)
                    ins.then_inc(sem["ks"], 1)
                    if c >= 1:
                        pe.wait_ge(sem["ocopied"], c)
                    for m in range(4):
                        nc.tensor.matmul(K.psum[:, 2, m * P:(m + 1) * P], q_e[:, m, c * P:(c + 1) * P], state[:, m], start=(m == 0), stop=False, skip_group_check=True)
                    pe.wait_ge(sem["z"], c + 1)
                    for hh in range(8):
                        ins = nc.tensor.matmul(K.psum[:, 1, hh * HD:(hh + 1) * HD], xt[:, 2 * c + hh % 2, hh // 2], zz[:, hh * HD:(hh + 1) * HD], start=True, stop=True)
                    ins.then_inc(sem["vn"], 1)
                    pe.wait_ge(sem["vcopied"], c + 1)
                    for m in range(4):
                        ins = nc.tensor.matmul(K.psum[:, 3, m * P:(m + 1) * P], k_decay[:, c, m * P:(m + 1) * P], vn[:, m * P:(m + 1) * P], start=True, stop=True)
                    ins.then_inc(sem["kv"], 1)
                    for m in range(4):
                        for hh in (2 * m, 2 * m + 1):
                            ins = nc.tensor.matmul(K.psum[:, 2, hh * HD:(hh + 1) * HD], attn[:, 2 * c + hh % 2, hh // 2], vn[:, hh * HD:(hh + 1) * HD],
                                                   start=False, stop=(hh % 2 == 1), skip_group_check=True)
                    ins.then_inc(sem["out"], 1)

            @st.block.vector
            def _(dve):
                link = Chain(dve, sem["v"])
                nc.vector.memset(state[:], 0.0).then_inc(sem["state"], 1)
                for c in range(TT):
                    dve.wait_ge(sem["ks"], c + 1)
                    nc.vector.tensor_tensor(zz[:], v_beta[:, c], K.psum[:, 0], ALU.subtract).then_inc(sem["z"], 1)
                    dve.wait_ge(sem["kv"], c + 1)
                    link(nc.vector.tensor_tensor(upd[:], K.psum[:, 3].rearrange("p (m n) -> p m n", m=4), over_rows(K.head_ones[:], 4), ALU.mult))
                    for m in range(4):
                        ins = nc.vector.scalar_tensor_tensor(state[:, m], state[:, m], row_e[:, m, c * P + P - 1:c * P + P], upd[:, m], ALU.mult, ALU.add)
                    ins.then_inc(sem["state"], 1)
                    dve.wait_ge(sem["state"], c + 2)

            @st.block.scalar
            def _(act):
                for c in range(TT):
                    act.wait_ge(sem["vn"], c + 1)
                    if c >= 1:
                        act.wait_ge(sem["out"], c)
                    nc.scalar.activation(vn[:], K.psum[:, 1], ACT.Copy).then_inc(sem["vcopied"], 1)
                    act.wait_ge(sem["out"], c + 1)
                    nc.scalar.activation(o[:, c], K.psum[:, 2], ACT.Copy).then_inc(sem["ocopied"], 1)
    with ExitStack() as p2:
        sq = sb("g_sq", [P, TT, S], p2)
        head_norm_stage(nc, K, "gn", o, TT, 8, K.gdn_gain[:], sq, g_scr[:, 1])
        turn_stage(nc, K, "gto", [o[:, c, m * P:(m + 1) * P] for m in range(4) for c in range(TT)],
                   lambda m, ps: nc.vector.tensor_tensor(gatedB[:, m], ps, z[:, m], ALU.mult))
    ph.close()


def conv_stage(nc, K, a, h, x_c, qkv):
    ns = K.nring
    wring = K.wring[:].rearrange("p s (k n) -> p s k n", k=KD)
    with Stage(nc, "gp", *[f"w{j}" for j in range(ns)], "done", "emptied", "convd", "silud", "v") as st:
        sem = st.sem

        @st.block.sync
        def _(sync):
            for t in range(12):
                if t >= ns:
                    sync.wait_ge(sem["done"], t - ns + 1)
                sync.dma_start(wring[:, t % ns], a["w1f"][28 + t]).then_inc(sem[f"w{t % ns}"], 16)

        @st.block.tensor
        def _(pe):
            for t in range(12):
                pe.wait_ge(sem[f"w{t % ns}"], 16 * (t // ns + 1))
                if t >= 4:
                    pe.wait_ge(sem["emptied"], t - 3)
                for k in range(KD):
                    m = nc.tensor.matmul(K.psum[:, t % 4], wring[:, t % ns, k], h[:, k], start=(k == 0), stop=(k == KD - 1))
                m.then_inc(sem["done"], 1)

        @st.block.scalar
        def _(act):
            def silu(t):
                act.wait_ge(sem["convd"], t + 1)
                nc.scalar.activation(qkv[:, t], qkv[:, t], ACT.Silu).then_inc(sem["silud"], 1)

            for t in range(12):
                act.wait_ge(sem["done"], t + 1)
                if t >= 2:
                    act.wait_ge(sem["convd"], t - 1)
                nc.scalar.activation(x_c[:, t % 2, 3:], K.psum[:, t % 4], ACT.Copy).then_inc(sem["emptied"], 1)
                if t >= 1:
                    silu(t - 1)
            silu(11)

        @st.block.vector
        def _(dve):
            link = Chain(dve, sem["v"])
            for t in range(12):
                dve.wait_ge(sem["emptied"], t + 1)
                link(nc.vector.tensor_scalar(qkv[:, t], x_c[:, t % 2, 0:S], K.conv[:, t, 0:1], None, ALU.mult))
                for j in range(1, 4):
                    m = nc.vector.scalar_tensor_tensor(qkv[:, t], x_c[:, t % 2, j:j + S], K.conv[:, t, j:j + 1], qkv[:, t], ALU.mult, ALU.add)
                    if j < 3:
                        link(m)
                m.then_inc(sem["convd"], 1)


NCH = TC
ORDER = (list(range(NCH)), list(range(CT))[::-1] + list(range(CT, NCH))[::-1])


ADA_GROUPS, ADA_PARTS = 3, 4


def modulation_stage(nc, K, a, mod, gains):
    ns = 4
    with ExitStack() as ph:
        def sb(name, shape):
            return ph.enter_context(nc.sbuf_tensor(name, shape, F32))

        ring = sb("ada_ring", [P, ns, KD // ADA_PARTS, 4, 512])
        wide, out = sb("ada_cond", [P, KD, 32]), sb("ada_out", [P, ADA_GROUPS, 512])
        with Stage(nc, "ada", *[f"w{j}" for j in range(ns)], "zero", "silud", "used", "done", "copied", "turned", "v") as st:
            sem = st.sem
            n_all = ADA_GROUPS * ADA_PARTS

            @st.block.sync
            def _(sync):
                for i in range(n_all):
                    if i >= ns:
                        sync.wait_ge(sem["used"], i - ns + 1)
                    sync.dma_start(ring[:, i % ns], a["w_ada"][i]).then_inc(sem[f"w{i % ns}"], 16)

            @st.block.scalar
            def _(act):
                act.wait_ge(sem["zero"], 1)
                nc.scalar.activation(wide[:, :, 0:2], K.cond.rearrange("p (k c) -> p k c", c=2), ACT.Silu).then_inc(sem["silud"], 1)
                for g in range(ADA_GROUPS):
                    act.wait_ge(sem["used"], (g + 1) * ADA_PARTS)
                    nc.scalar.activation(out[:, g], K.psum[:, g], ACT.Copy).then_inc(sem["copied"], 1)

            @st.block.tensor
            def _(pe):
                def turn(g):
                    pe.wait_ge(sem["copied"], g + 1)
                    for q in range(4):
                        m = nc.tensor.transpose(K.psum[:, 3 + g, q * P:(q + 1) * P], out[:, g, q * P:(q + 1) * P], K.ident[:])
                    m.then_inc(sem["turned"], 1)

                pe.wait_ge(sem["silud"], 1)
                for g in range(ADA_GROUPS):
                    for part in range(ADA_PARTS):
                        i = g * ADA_PARTS + part
                        pe.wait_ge(sem[f"w{i % ns}"], 16 * (i // ns + 1))
                        for kk in range(KD // ADA_PARTS):
                            k = part * (KD // ADA_PARTS) + kk
                            for j in range(4):
                                m = nc.tensor.matmul(K.psum[32 * j:32 * j + 32, g], wide[:, k], ring[:, i % ns, kk, j],
                                                     start=(k == 0), stop=(k == KD - 1))
                        m.then_inc(sem["used"], 1)
                    if g >= 1:
                        turn(g - 1)
                turn(ADA_GROUPS - 1)

            @st.block.vector
            def _(dve):
                link = Chain(dve, sem["v"])
                nc.vector.memset(wide[:], 0.0).then_inc(sem["zero"], 1)
                for g in range(ADA_GROUPS):
                    dve.wait_ge(sem["turned"], g + 1)
                    ps = K.psum[:, 3 + g].rearrange("p (q j w) -> p q j w", q=4, w=32)[:, :, :, 0:2]
                    bias = K.b_ada[:, 16 * g:16 * g + 16].rearrange("p (j q) -> p q j", q=4)
                    link(nc.vector.tensor_tensor(mod[:, 16 * g:16 * g + 16].rearrange("p (j q) c -> p q j c", q=4), ps, over_heads(bias, 2), ALU.add))
                for j, (at, who, norm) in enumerate([(8, 0, K.norm1), (8, 1, K.norm1), (32, 0, K.norm2)]):
                    nc.vector.scalar_tensor_tensor(gains[:, j], mod[:, at:at + 8, who], 1.0, norm, ALU.add, ALU.mult)


def running_sums(nc, K, dve, link, lw, cum, tiles):
    for t in tiles:
        link(nc.vector.tensor_tensor_scan(cum[:, t], K.reset[:], lw[:, t], 0.0, ALU.mult, ALU.add))


def chunks(ap):
    return ap.rearrange("p (c n) -> p c n", n=P)


def hgrn(nc, K, a, h2, mix):
    ph = ExitStack()

    def sb(name, shape, stack=ph):
        return stack.enter_context(nc.sbuf_tensor(name, shape, F32))

    def proj(w, t, ps):
        return nc.scalar.activation(ig[:, t], ps, ACT.Copy)

    ig = sb("h_ig", [P, NCH, 512])
    acc = sb("h_acc", [P, 2, 2, TT, P])
    q_in = sb("h_qin", [P, 4, S])
    k_outT = sb("h_koutT", [P, NCH, 4 * P])
    e_tot = sb("h_etot", [P, 4, NCH])
    with ExitStack() as p2:
        q = sb("h_q", [P, 2, T2], p2)
        f = sb("h_f", [P, 4, T2], p2)
        with ExitStack() as p3:
            rings(nc, K, p3, "h", vring=False, n=2)
            K.vring = p3.enter_context(nc.sbuf_tensor("vring_h", [P, 1, KD * 512], F32))

            def evac(t, g, at, n, ps, link):
                to = q[:, t] if t < 2 else f[:, t - 2]
                return nc.scalar.activation(to[:, at:at + n], ps, ACT.Copy)

            project_feature(nc, K, "hp", a["w2f"], 6, lambda k_: h2[:, k_], [(0, CTX), (CTX, S)], evac)
            project_token(nc, K, "ht", lambda w: a["w2t"][0], 1, lambda k_: h2[:, k_], range(NCH), proj)
        with ExitStack() as p3:
            k = sb("h_k", [P, 4, T2], p3)
            c = sb("h_c", [P, 4, T2], p3)
            e = sb("h_e", [P, 4, T2], p3)
            with Stage(nc, "hg", "l", "x", "v", "a", "b", "sig", "f", "logf") as st:
                sem = st.sem
                lb, oml = K.hlb[:, 0:4], K.hlb[:, 4:8]

                @st.block.scalar
                def _(act):
                    act.wait_ge(sem["l"], 1)
                    nc.scalar.activation(lb, lb, ACT.Exp).then_inc(sem["b"], 1)
                    for n in range(4):
                        nc.scalar.activation(e[:, n], f[:, n], ACT.Abs).then_inc(sem["a"], 1)
                    act.wait_ge(sem["a"], 4)
                    nc.scalar.activation(e[:], e[:], ACT.Exp, scale=-1.0).then_inc(sem["a"], 1)
                    act.wait_ge(sem["a"], 5)
                    nc.scalar.activation(e[:], e[:], ACT.Ln, bias=1.0).then_inc(sem["a"], 1)
                    act.wait_ge(sem["x"], 1)
                    nc.scalar.activation(k[:], k[:], ACT.Exp, scale=-1.0)
                    nc.scalar.activation(f[:], f[:], ACT.Exp).then_inc(sem["sig"], 1)
                    act.wait_ge(sem["f"], 1)
                    nc.scalar.activation(f[:], f[:], ACT.Ln, scale=8.0).then_inc(sem["logf"], 1)

                @st.block.vector
                def _(dve):
                    link = Chain(dve, sem["v"])
                    nc.vector.tensor_tensor(lb, lb, lb, ALU.subtract).then_inc(sem["l"], 1)
                    dve.wait_ge(sem["b"], 1)
                    link(nc.vector.reciprocal(oml, lb))
                    link(nc.vector.tensor_tensor(lb, lb, oml, ALU.mult))
                    link(nc.vector.tensor_tensor(lb, lb, lb, ALU.subtract))
                    link(nc.vector.tensor_scalar(oml, lb, -1.0, 1.0, ALU.mult, ALU.add))
                    dve.wait_ge(sem["a"], 6)
                    link(nc.vector.scalar_tensor_tensor(k[:], f[:], 0.0, e[:], ALU.max, ALU.add))
                    nc.vector.scalar_tensor_tensor(f[:], f[:], 0.0, e[:], ALU.min, ALU.subtract).then_inc(sem["x"], 1)
                    dve.wait_ge(sem["sig"], 1)
                    for n in range(4):
                        nc.vector.tensor_scalar(k[:, n], k[:, n], oml[:, n:n + 1], None, ALU.mult)
                        link(nc.vector.tensor_scalar(f[:, n], f[:, n], oml[:, n:n + 1], lb[:, n:n + 1], ALU.mult, ALU.add))
                    nc.vector.tensor_scalar(f[:], f[:], 1e-20, None, ALU.max).then_inc(sem["f"], 1)
                    dve.wait_ge(sem["logf"], 1)
                    link(nc.vector.tensor_scalar(f[:], f[:], -math.log(8.0), None, ALU.add))
                    running_sums(nc, K, dve, link, f, c, range(4))
                    for n in (2, 3):
                        link(nc.vector.tensor_copy(e_tot[:, n], chunks(c[:, n])[:, :, P - 1]))
                        nc.vector.tensor_copy(e_tot[:, n - 2], chunks(c[:, n - 2])[:, :, P - 1])
                        link(nc.vector.tensor_tensor(c[:, n], f[:, n], c[:, n], ALU.subtract))
                        link(nc.vector.tensor_tensor(chunks(c[:, n]), chunks(c[:, n]), over_heads(e_tot[:, n], P), ALU.add))

            with Stage(nc, "hd", "v", "d", "exped", "x") as st:
                sem = st.sem

                @st.block.vector
                def _(dve):
                    link = Chain(dve, sem["v"])
                    for n in range(4):
                        nc.vector.tensor_tensor(chunks(e[:, n]), over_heads(e_tot[:, n], P), chunks(c[:, n]), ALU.subtract).then_inc(sem["d"], 1)
                    for n in range(4):
                        dve.wait_ge(sem["exped"], 2 * n + 2)
                        nc.vector.tensor_tensor(e[:, n], k[:, n], e[:, n], ALU.mult)
                        nc.vector.tensor_tensor(q_in[:, n], q[:, n % 2, CTX:], q_in[:, n], ALU.mult)

                @st.block.scalar
                def _(act):
                    for n in range(4):
                        act.wait_ge(sem["d"], n + 1)
                        nc.scalar.activation(e[:, n], e[:, n], ACT.Exp).then_inc(sem["exped"], 1)
                        nc.scalar.activation(q_in[:, n], c[:, n, CTX:], ACT.Exp).then_inc(sem["exped"], 1)
                    act.wait_ge(sem["d"], 4)
                    nc.scalar.activation(e_tot[:], e_tot[:], ACT.Exp)

            turn_stage(nc, K, "hkt", [e[:, n, j * P:(j + 1) * P] for j in range(NCH) for n in range(4)],
                       lambda g, ps: nc.vector.tensor_copy(k_outT[:, g], ps))
            level_stage(nc, K, q, k, c, acc, e, f, sb, p3)
    o = sb("h_o", [P, TT, 256])
    with ExitStack() as p2:
        kv = sb("h_kv", [P, NCH, 4, P], p2)
        states = sb("h_states", [P, NCH, 4, P], p2)
        with Stage(nc, "hs", "kv", "masked", "state", "v", "out") as st:
            sem = st.sem

            @st.block.tensor
            def _(pe):
                for j in range(NCH):
                    if j >= 4:
                        pe.wait_ge(sem["masked"], j - 3)
                    for n in range(4):
                        ins = nc.tensor.matmul(K.psum[:, j % 4, n * P:(n + 1) * P], k_outT[:, j, n * P:(n + 1) * P],
                                               ig[:, j, (n % 2) * P:(n % 2 + 1) * P], start=True, stop=True)
                    ins.then_inc(sem["kv"], 1)
                pe.wait_ge(sem["state"], 1)
                for t in range(TT):
                    j = CT + t
                    for m in range(2):
                        for d in range(2):
                            nc.tensor.matmul(K.psum[:, 4 + t, m * P:(m + 1) * P], q_in[:, 2 * d + m, t * P:(t + 1) * P], states[:, j, 2 * d + m],
                                             start=(d == 0), stop=False, skip_group_check=True)
                        for par in range(2):
                            hh = 2 * m + par
                            ins = nc.tensor.matmul(K.psum[:, 4 + t, hh * HD:(hh + 1) * HD], acc[:, par, m, t], ig[:, j, hh * HD:(hh + 1) * HD],
                                                   start=False, stop=(par == 1), skip_group_check=True)
                    ins.then_inc(sem["out"], 1)

            @st.block.vector
            def _(dve):
                link = Chain(dve, sem["v"])
                for j in range(NCH):
                    dve.wait_ge(sem["kv"], j + 1)
                    nc.vector.tensor_tensor(kv[:, j], K.psum[:, j % 4].rearrange("p (n x) -> p n x", n=4), over_rows(K.head_ones[:], 4), ALU.mult).then_inc(sem["masked"], 1)
                dve.wait_ge(sem["masked"], NCH)
                for d in range(2):
                    link(nc.vector.memset(states[:, ORDER[d][0], 2 * d:2 * d + 2], 0.0))
                for i in range(NCH - 1):
                    for d in range(2):
                        j, nx = ORDER[d][i], ORDER[d][i + 1]
                        for m in range(2):
                            n = 2 * d + m
                            ins = nc.vector.scalar_tensor_tensor(states[:, nx, n], states[:, j, n], e_tot[:, n, j:j + 1], kv[:, j, n], ALU.mult, ALU.add)
                    if i < NCH - 2:
                        link(ins)
                ins.then_inc(sem["state"], 1)

            @st.block.scalar
            def _(act):
                for t in range(TT):
                    act.wait_ge(sem["out"], t + 1)
                    nc.scalar.activation(o[:, t], K.psum[:, 4 + t, 0:256], ACT.Copy)
        sq = sb("h_sq", [P, TT, 256], p2)
        stat = sb("h_stat", [P, 16], p2)
        head_norm_stage(nc, K, "hn", o, TT, 4, K.rows2[:, 0:256], sq, stat[:])
        gate_stage(nc, K, "hgt", o, lambda t: ig[:, CT + t, 256:512], ACT.Silu)
    turn_stage(nc, K, "hto", [o[:, t, m * P:(m + 1) * P] for m in range(2) for t in range(TT)],
               lambda m, ps: nc.vector.tensor_copy(mix[:, m], ps))
    ph.close()


def gate_stage(nc, K, name, o, gate, func):
    with Stage(nc, name, "g", "v") as st:
        @st.block.scalar
        def _(act):
            for t in range(TT):
                nc.scalar.activation(gate(t), gate(t), func).then_inc(st.sem["g"], 1)

        @st.block.vector
        def _(dve):
            for t in range(TT):
                dve.wait_ge(st.sem["g"], t + 1)
                nc.vector.tensor_tensor(o[:, t], o[:, t], gate(t), ALU.mult)


def level_stage(nc, K, q, k, c, acc, e, f, sb, stack):
    part = [x[:].rearrange("p n t -> p (n t)")[:, i * 2 * S:(i + 1) * 2 * S].rearrange("p (n t) -> p n t", n=2)
            for x in (e, f) for i in range(3)]
    E, Q, KK = part[0:2], part[2:4], part[4:6]
    items = [(0, -1)] + [(d, lv) for lv in range(LEVELS) for d in range(2)]

    def blocked(x, b):
        return x[:, :, :].rearrange("p n (g b) -> p (n g) b", b=b)

    with Stage(nc, "hl", "diff", "abs", "exped", "keys", "queries", "scored", "picked", "v") as st:
        sem = st.sem

        @st.block.vector
        def _(dve):
            def pick(i):
                d, lv = items[i]
                dve.wait_ge(sem["scored"], i + 1)
                mask = (K.ident if lv < 0 else K.level[:, d * LEVELS + lv]).bitcast(mybir.dt.uint32)
                for par in range(2):
                    for m in range(2):
                        ins = nc.vector.copy_predicated(acc[:, par, m], over_rows(mask, TT),
                                                        K.psum[:, (i % 2) * 4 + 2 * par + m].rearrange("p (c t) -> p c t", t=P))
                ins.then_inc(sem["picked"], 1)
                dve.wait_ge(sem["picked"], i + 1)

            def diff(i):
                d, lv = items[i]
                if i >= 3:
                    dve.wait_ge(sem["keys"], i - 2)
                b = 2 << lv
                mid = b // 2 - 1 if d == 0 else b // 2
                for n in range(2):
                    cb = c[:, 2 * d + n, CTX:].rearrange("p (g b) -> p g b", b=b)
                    ins = nc.vector.tensor_tensor(E[i % 2][:, n].rearrange("p (g b) -> p g b", b=b), cb,
                                                  cb[:, :, mid:mid + 1].broadcast_to([P, S // b, b]), ALU.subtract)
                ins.then_inc(sem["diff"], 1)

            diff(1)
            nc.vector.tensor_tensor(KK[0][:], k[:, 0:2, CTX:], k[:, 2:4, CTX:], ALU.add).then_inc(sem["queries"], 1)
            for i in range(1, len(items)):
                if i >= 2:
                    dve.wait_ge(sem["scored"], i - 1)
                dve.wait_ge(sem["exped"], i)
                nc.vector.tensor_tensor(Q[i % 2][:], q[:, :, CTX:], E[i % 2][:], ALU.mult).then_inc(sem["queries"], 1)
                if i + 1 < len(items):
                    diff(i + 1)
                pick(i - 1)
            pick(len(items) - 1)

        @st.block.scalar
        def _(act):
            for i in range(1, len(items)):
                act.wait_ge(sem["diff"], i)
                nc.scalar.activation(E[i % 2][:], E[i % 2][:], ACT.Abs).then_inc(sem["abs"], 1)
                act.wait_ge(sem["abs"], i)
                nc.scalar.activation(E[i % 2][:], E[i % 2][:], ACT.Exp, scale=-1.0).then_inc(sem["exped"], 1)

        @st.block.gpsimd
        def _(pool):
            for i, (d, lv) in enumerate(items):
                if lv < 0:
                    continue
                pool.wait_ge(sem["exped"], i)
                if i >= 2:
                    pool.wait_ge(sem["scored"], i - 1)
                nc.gpsimd.tensor_tensor(KK[i % 2][:], k[:, 2 * d:2 * d + 2, CTX:], E[i % 2][:], ALU.mult).then_inc(sem["keys"], 1)

        @st.block.tensor
        def _(pe):
            for i, (d, lv) in enumerate(items):
                pe.wait_ge(sem["queries"], i + 1)
                if lv >= 0:
                    pe.wait_ge(sem["keys"], i)
                if i >= 2:
                    pe.wait_ge(sem["picked"], i - 1)
                for m in range(2):
                    for t in range(TT):
                        for par in range(2):
                            r = par * HD
                            at = slice(t * P, (t + 1) * P)
                            qq = q[r:r + HD, m, CTX + t * P:CTX + (t + 1) * P] if lv < 0 else Q[i % 2][r:r + HD, m, at]
                            ins = nc.tensor.matmul(K.psum[:, (i % 2) * 4 + 2 * par + m, at], KK[i % 2][r:r + HD, m, at], qq, start=True, stop=True)
                ins.then_inc(sem["scored"], 1)


def neighbourhood(nc, K, a, h2, mix):
    ph = ExitStack()

    def sb(name, shape, stack=ph):
        return stack.enter_context(nc.sbuf_tensor(name, shape, F32))

    with ExitStack() as p2:
        q, k, v = sb("n_q", [P, 4, S], p2), sb("n_k", [P, 4, T2], p2), sb("n_v", [P, NCH, 512], p2)
        with ExitStack() as p3:
            rings(nc, K, p3, "n", vring=True)
            project_feature(nc, K, "nq", a["w2f"], 4, lambda k_: h2[:, k_, CTX:], [(0, S)],
                            lambda t, g, at, n, ps, link: nc.scalar.activation(q[:, t], ps, ACT.Copy), base=15)
            project_feature(nc, K, "nk", a["w2f"], 4, lambda k_: h2[:, k_], [(0, CTX), (CTX, S)],
                            lambda t, g, at, n, ps, link: nc.scalar.activation(k[:, t, at:at + n], ps, ACT.Copy), base=19)
            project_token(nc, K, "nv", lambda w: a["w2t"][1], 1, lambda k_: h2[:, k_], range(NCH),
                          lambda w, t, ps: nc.scalar.activation(v[:, t], ps, ACT.Copy))
        table = sb("n_table", [P, 8, 14 * HD], p2)
        window = sb("n_window", [P, HD], p2)
        cos, sin = sb("cos2", [P, S], p2), sb("sin2", [P, S], p2)
        load_stage(nc, "nl", [(table[:], a["na_table"]), (window[:], a["na_window"]), (cos[:], a["cos2"]), (sin[:], a["sin2"])])
        with Stage(nc, "nw", "m") as st:
            @st.block.gpsimd
            def _(pool):
                for hh in range(8):
                    tb = table[:, hh].rearrange("p (j n) -> p j n", n=HD)
                    nc.gpsimd.tensor_tensor(tb, tb, over_rows(window[:], 14), ALU.add)
        tiles = [q[:, m] for m in range(4)] + [k[:, m, CTX:] for m in range(4)] + [k[:, m, 0:CTX] for m in range(4)]
        rms_stage(nc, K, "nn", tiles, lambda t: S if t < 8 else CTX, [K.na_gain[:, 0:1]] * 4 + [K.na_gain[:, 1:2]] * 8, mean=1.0 / HD)
        rope_stage(nc, K, "nr", tiles[:8], S, cos[:], sin[:])
        s_sb, pt_sb = sb("n_s", [P, 3, 6 * P], p2), sb("n_pt", [P, 4, 6 * P], p2)
        items = []
        diag = sb("n_diag", [P, 2, P], p2)
        for m in range(4):
            for t, hh in [(t, hh) for t in range(TT) for hh in (2 * m, 2 * m + 1)]:
                r = (hh % 2) * HD
                qq = q[r:r + HD, m, t * P:(t + 1) * P]
                off = (6 - 2 * t) * HD
                segs = [(qq, k[r:r + HD, m, CTX:], S, 0, table[:, hh, off:off + S]), (qq, k[r:r + HD, m, 0:CTX], CTX, S, None)]
                vals = [v[:, j, hh * HD:(hh + 1) * HD] for j in list(range(CT, NCH)) + list(range(CT))]
                items.append(Item(segs, vals))
        attention_stage(nc, K, "na", items, s_sb, pt_sb, diag,
                        lambda p, ps: nc.vector.tensor_copy(mix[:, 4 + p // TT, p % TT * P:(p % TT + 1) * P], ps))
    ph.close()


def rwkv_projections(nc, K, a, h2, p_mix, px):
    ns = K.nring
    wring = K.wring[:].rearrange("p s (k n) -> p s k n", k=KD)
    segs = [(0, CTX, 1), (CTX, S, CTX + 2)]
    with Stage(nc, "rp", *[f"w{j}" for j in range(ns)], "zeroed", "done", "emptied", "shifted", "v") as st:
        sem = st.sem

        @st.block.gpsimd
        def _(pool):
            nc.gpsimd.memset(px[:], 0.0).then_inc(sem["zeroed"], 1)

        @st.block.sync
        def _(sync):
            for t in range(9):
                if t >= ns:
                    sync.wait_ge(sem["done"], t - ns + 1)
                sync.dma_start(wring[:, t % ns], a["w2f"][6 + t]).then_inc(sem[f"w{t % ns}"], 16)

        @st.block.tensor
        def _(pe):
            for t in range(9):
                pe.wait_ge(sem[f"w{t % ns}"], 16 * (t // ns + 1))
                if t >= 2:
                    pe.wait_ge(sem["emptied"], t - 1)
                for g, (at, n, col) in enumerate(segs):
                    for k in range(KD):
                        m = nc.tensor.matmul(K.psum[:, (t % 2) * 2 + g, :n], wring[:, t % ns, k], h2[:, k, at:at + n], start=(k == 0), stop=(k == KD - 1))
                m.then_inc(sem["done"], 1)

        @st.block.scalar
        def _(act):
            act.wait_ge(sem["zeroed"], 1)
            for t in range(9):
                act.wait_ge(sem["done"], t + 1)
                if t >= 2:
                    act.wait_ge(sem["shifted"], t - 1)
                for g, (at, n, col) in enumerate(segs):
                    m = nc.scalar.activation(px[:, t % 2, col:col + n], K.psum[:, (t % 2) * 2 + g, :n], ACT.Copy)
                m.then_inc(sem["emptied"], 1)

        @st.block.vector
        def _(dve):
            link = Chain(dve, sem["v"])
            for t in range(9):
                dve.wait_ge(sem["emptied"], t + 1)
                for at, n, col in segs:
                    m = nc.vector.tensor_tensor(p_mix[:, t, at:at + n], px[:, t % 2, col - 1:col - 1 + n], px[:, t % 2, col + 1:col + 1 + n], ALU.add)
                link(m)
                for at, n, col in segs:
                    m = nc.vector.scalar_tensor_tensor(p_mix[:, t, at:at + n], p_mix[:, t, at:at + n], 0.5, px[:, t % 2, col:col + n], ALU.mult, ALU.subtract)
                link(m)
                for at, n, col in segs:
                    m = nc.vector.scalar_tensor_tensor(p_mix[:, t, at:at + n], p_mix[:, t, at:at + n], K.mu[:, t:t + 1], px[:, t % 2, col:col + n], ALU.mult, ALU.add)
                m.then_inc(sem["shifted"], 1)


def rwkv(nc, K, a, p_mix, mix):
    ph = ExitStack()

    def sb(name, shape, stack=ph):
        return stack.enter_context(nc.sbuf_tensor(name, shape, F32))

    v_T, g_T = sb("r_vT", [P, NCH, 256]), sb("r_gT", [P, TT, 256])
    kk = sb("r_kk", [P, 2, T2])
    bonus, y = sb("r_bonus", [P, 2, S]), sb("r_y", [P, TT, 256])
    r_, k_, v_ = p_mix[:, 0:2], p_mix[:, 2:4], p_mix[:, 4:6]
    up_w = sb("r_up", [P, 3, 256])
    load_stage(nc, "rl", [(up_w[:], a["rw_up"])])
    with Stage(nc, "rt", "v", "a") as st:
        @st.block.scalar
        def _(act):
            nc.scalar.activation(p_mix[:, 6], p_mix[:, 6], ACT.Tanh)
            nc.scalar.activation(p_mix[:, 8], p_mix[:, 8], ACT.Sigmoid)

        @st.block.vector
        def _(dve):
            for m in range(2):
                nc.vector.tensor_scalar(kk[:, m], k_[:, m], K.rw[:, 4 + m:5 + m], None, ALU.mult)
    l2_stage(nc, K, "rk", [kk[:, m, at:at + n] for m in range(2) for at, n in ((0, S), (S, CTX))],
             lambda t: (S, CTX)[t % 2], [1.0] * 4, floor=1e-24)
    vjobs = [v_[:, m, j * P:(j + 1) * P] for j in range(NCH) for m in range(2)]
    turn_stage(nc, K, "rv", vjobs, lambda g, ps: nc.vector.tensor_copy(v_T[:, 2 * g:2 * g + 2], ps.rearrange("p (j n) -> p j n", j=2)))
    with Stage(nc, "rg", "done") as st:
        @st.block.tensor
        def _(pe):
            for t in range(TT):
                m = nc.tensor.matmul(K.psum[:, t, 0:256], p_mix[:, 8, CTX + t * P:CTX + (t + 1) * P], up_w[:, 2], start=True, stop=True)
                m.then_inc(st.sem["done"], 1)

        @st.block.scalar
        def _(act):
            for t in range(TT):
                act.wait_ge(st.sem["done"], t + 1)
                nc.scalar.activation(g_T[:, t], K.psum[:, t, 0:256], ACT.Copy)

    for d in range(2):
        rwkv_direction(nc, K, d, up_w, r_, k_, p_mix, kk, v_T, bonus, y)

    mean = sb("r_mean", [P, 32])
    with Stage(nc, "rb", "z", "done", "v", "b") as st:
        sem = st.sem

        @st.block.vector
        def _(dve):
            link = Chain(dve, sem["v"])
            for m in range(2):
                nc.vector.scalar_tensor_tensor(bonus[:, m], r_[:, m, CTX:], K.rw[:, 8 + m:9 + m], bonus[:, m], ALU.mult, ALU.mult).then_inc(sem["z"], 1)
            link(nc.vector.tensor_reduce(mean[:, 16:32], y[:].rearrange("p t (h d) -> p (t h) d", d=HD), AX.X, ALU.add))
            link(nc.vector.tensor_scalar(mean[:, 16:32], mean[:, 16:32], 1.0 / HD, None, ALU.mult))
            yh = y[:].rearrange("p t (h d) -> p (t h) d", d=HD)
            link(nc.vector.tensor_tensor(yh, yh, over_heads(mean[:, 16:32]), ALU.subtract))
            dve.wait_ge(sem["done"], 1)
            link(nc.vector.tensor_copy(mean[:, 0:16], K.psum[:, 0, 0:16]))

        @st.block.tensor
        def _(pe):
            pe.wait_ge(sem["z"], 2)
            for t in range(TT):
                for m in range(2):
                    ins = nc.tensor.matmul(K.psum[:, 0, 4 * t + 2 * m:4 * t + 2 * m + 2], bonus[:, m, t * P:(t + 1) * P], K.head_ones[:, 0:65:64], start=True, stop=True)
            ins.then_inc(sem["done"], 1)
    with ExitStack() as p2:
        sq = sb("r_sq", [P, TT, 256], p2)
        head_norm_stage(nc, K, "rn", y, TT, 4, K.rows2[:, 256:512], sq, mean[:, 16:32], bias=K.rows2[:, 512:768], eps=K.eps_ln)
        with Stage(nc, "ro", "v") as st:
            @st.block.vector
            def _(dve):
                link = Chain(dve, st.sem["v"])
                for t in range(TT):
                    nc.vector.tensor_tensor(sq[:, t].rearrange("p (h d) -> p h d", d=HD), v_T[:, CT + t].rearrange("p (h d) -> p h d", d=HD),
                                            over_heads(mean[:, 4 * t:4 * t + 4]), ALU.mult)
                    link(nc.vector.tensor_copy(K.stat[:, 0:1], mean[:, 0:1]))
                    link(nc.vector.tensor_tensor(y[:, t], y[:, t], sq[:, t], ALU.add))
                    link(nc.vector.tensor_tensor(y[:, t], y[:, t], g_T[:, t], ALU.mult))
    turn_stage(nc, K, "rto", [y[:, t, m * P:(m + 1) * P] for m in range(2) for t in range(TT)],
               lambda m, ps: nc.vector.tensor_copy(mix[:, 2 + m], ps))
    ph.close()


def rwkv_direction(nc, K, d, up_w, r_, k_, p_mix, kk, v_T, bonus, y):
    ph = ExitStack()

    def sb(name, shape, stack=ph):
        return stack.enter_context(nc.sbuf_tensor(f"r{d}_{name}", shape, F32))

    at, bt = sb("at", [P, NCH, 4, P]), sb("bt", [P, NCH, 4, P])
    cd = sb("cd", [P, TT, 2, 4, P])
    kke, re = sb("kke", [P, 2, T2]), sb("re", [P, 2, S])
    koT = sb("koT", [P, NCH, 4 * P])
    e_tot = sb("etot", [P, 2, NCH])
    half = HD
    with ExitStack() as p2:
        kd, ak, lw = sb("kd", [P, 2, T2], p2), sb("ak", [P, 2, T2], p2), sb("lw", [P, 2, T2], p2)
        ci, ce = sb("ci", [P, 2, T2], p2), sb("ce", [P, 2, T2], p2)
        rows = slice(d * HD, (d + 1) * HD)
        with Stage(nc, f"ru{d}", "up", "sig", "v") as st:
            sem = st.sem

            @st.block.tensor
            def _(pe):
                for j in range(4):
                    for s_, (at_, n) in enumerate(((0, S), (S, CTX))):
                        ins = nc.tensor.matmul(K.psum[:, 2 * j + s_, :n], up_w[rows, j // 2, (j % 2) * P:(j % 2 + 1) * P],
                                               p_mix[rows, 6 + j // 2, at_:at_ + n], start=True, stop=True)
                    ins.then_inc(sem["up"], 1)

            @st.block.scalar
            def _(act):
                for j in range(4):
                    act.wait_ge(sem["up"], j + 1)
                    for s_, (at_, n) in enumerate(((0, S), (S, CTX))):
                        to = (lw, ak)[j // 2][:, j % 2, at_:at_ + n]
                        ins = nc.scalar.activation(to, K.psum[:, 2 * j + s_, :n], ACT.Sigmoid, bias=K.rw[:, 10 + 4 * (j // 2) + 2 * d + j % 2:11 + 4 * (j // 2) + 2 * d + j % 2])
                    ins.then_inc(sem["sig"], 1)

            @st.block.vector
            def _(dve):
                link = Chain(dve, sem["v"])
                dve.wait_ge(sem["sig"], 2)
                link(nc.vector.tensor_scalar(lw[:], lw[:], -math.exp(-0.5), None, ALU.mult))
                running_sums(nc, K, dve, link, lw, ci, range(2))
                dve.wait_ge(sem["sig"], 4)
                for m in range(2):
                    link(nc.vector.tensor_scalar(kd[:, m], ak[:, m], -1.0, K.rw[:, 6 + m:7 + m], ALU.add, ALU.mult))
                    link(nc.vector.scalar_tensor_tensor(kd[:, m], kd[:, m], 1.0, k_[:, m], ALU.add, ALU.mult))
                link(nc.vector.tensor_tensor(ak[:], ak[:], kk[:], ALU.mult))
                if d == 0:
                    nc.vector.tensor_copy(bonus[:], kd[:, :, CTX:])
                else:
                    nc.vector.tensor_tensor(bonus[:], bonus[:], kd[:, :, CTX:], ALU.add)
                for m in range(2):
                    link(nc.vector.tensor_copy(e_tot[:, m], chunks(ci[:, m])[:, :, P - 1]))
                    if d == 0:
                        link(nc.vector.tensor_tensor(ce[:, m], ci[:, m], lw[:, m], ALU.subtract))
                    else:
                        link(nc.vector.tensor_tensor(chunks(ce[:, m]), over_heads(e_tot[:, m], P), chunks(ci[:, m]), ALU.subtract))
                        link(nc.vector.tensor_tensor(ci[:, m], ce[:, m], lw[:, m], ALU.add))
        tmp = lw
        with Stage(nc, f"re{d}", "diffed", "exped", "v", "used") as st:
            sem = st.sem

            @st.block.vector
            def _(dve):
                link = Chain(dve, sem["v"])
                for m in range(2):
                    ins = nc.vector.tensor_tensor(chunks(tmp[:, m]), over_heads(e_tot[:, m], P), chunks(ci[:, m]), ALU.subtract)
                ins.then_inc(sem["diffed"], 1)
                dve.wait_ge(sem["exped"], 3)
                nc.vector.tensor_tensor(kke[:], kk[:], kke[:], ALU.mult)
                link(nc.vector.tensor_tensor(re[:], r_[:, :, CTX:], re[:], ALU.mult))

            @st.block.scalar
            def _(act):
                nc.scalar.activation(kke[:], ce[:], ACT.Exp).then_inc(sem["exped"], 1)
                nc.scalar.activation(re[:], ci[:, :, CTX:], ACT.Exp).then_inc(sem["exped"], 1)
                act.wait_ge(sem["diffed"], 1)
                nc.scalar.activation(tmp[:], tmp[:], ACT.Exp).then_inc(sem["exped"], 1)
                nc.scalar.activation(e_tot[:], e_tot[:], ACT.Exp).then_inc(sem["exped"], 1)
        ko = at[:].rearrange("p c i t -> p (c i t)").rearrange("p (w m t) -> p w m t", w=2, m=2)
        with Stage(nc, f"rko{d}", "v") as st:
            @st.block.vector
            def _(dve):
                nc.vector.tensor_tensor(ko[:, 0], kd[:], tmp[:], ALU.mult)
                nc.vector.tensor_tensor(ko[:, 1], ak[:], tmp[:], ALU.mult)
        turn_stage(nc, K, f"rkt{d}", [ko[:, w, m, j * P:(j + 1) * P] for j in range(NCH) for w in range(2) for m in range(2)],
                   lambda g, ps: nc.vector.tensor_copy(koT[:, g], ps))
        rwkv_scores(nc, K, d, r_, kk, kd, ak, ci, ce, at, bt, cd, (lw[:], p_mix[:, 4:6]), sb, p2)
    xt = sb("xt", [P, NCH, 4, P])
    with ExitStack() as p2:
        work = sb("work", [P, 3, 3, 4, P], p2)
        invert_stage(nc, K, f"ri{d}", at, xt, NCH, lambda b: d == 1, work, lanes=3)
    with ExitStack() as p2:
        state, upd, zz, un = sb("state", [P, 2, P], p2), sb("upd", [P, 2, P], p2), sb("zz", [P, 256], p2), sb("un", [P, 256], p2)
        lat_seen = {}
        for i, j in enumerate(ORDER[d]):
            lat_seen[i] = sum(x >= CT for x in ORDER[d][:i])
        with Stage(nc, f"rs{d}", "state", "z", "zcopied", "u", "ucopied", "out", "kv", "ytaken", "v") as st:
            sem = st.sem

            @st.block.tensor
            def _(pe):
                for i, j in enumerate(ORDER[d]):
                    lat = j - CT
                    pe.wait_ge(sem["state"], i + 1)
                    for m in range(2):
                        nc.tensor.matmul(K.psum[:, 0, m * P:(m + 1) * P], kke[:, m, j * P:(j + 1) * P], state[:, m], start=True, stop=False, skip_group_check=True)
                        for par in range(2):
                            hh = 2 * m + par
                            ins = nc.tensor.matmul(K.psum[:, 0, hh * HD:(hh + 1) * HD], bt[:, j, 2 * par + m], v_T[:, j, hh * HD:(hh + 1) * HD],
                                                   start=False, stop=(par == 1), skip_group_check=True)
                    ins.then_inc(sem["z"], 1)
                    if lat >= 0:
                        if lat_seen[i] >= 1:
                            pe.wait_ge(sem["ytaken"], lat_seen[i])
                        for m in range(2):
                            nc.tensor.matmul(K.psum[:, 2, m * P:(m + 1) * P], re[:, m, lat * P:(lat + 1) * P], state[:, m], start=(m == 0), stop=False, skip_group_check=True)
                            for hh in (2 * m, 2 * m + 1):
                                nc.tensor.matmul(K.psum[:, 2, hh * HD:(hh + 1) * HD], cd[:, lat, 0, 2 * (hh % 2) + m], v_T[:, j, hh * HD:(hh + 1) * HD], start=False, stop=False, skip_group_check=True)
                    pe.wait_ge(sem["zcopied"], i + 1)
                    for hh in range(4):
                        ins = nc.tensor.matmul(K.psum[:, 1, hh * HD:(hh + 1) * HD], xt[:, j, 2 * (hh % 2) + hh // 2], zz[:, hh * HD:(hh + 1) * HD], start=True, stop=True)
                    ins.then_inc(sem["u"], 1)
                    pe.wait_ge(sem["ucopied"], i + 1)
                    for m in range(2):
                        nc.tensor.matmul(K.psum[:, 3, m * P:(m + 1) * P], koT[:, j, m * P:(m + 1) * P], v_T[:, j, m * P:(m + 1) * P], start=True, stop=False)
                        ins = nc.tensor.matmul(K.psum[:, 3, m * P:(m + 1) * P], koT[:, j, (2 + m) * P:(3 + m) * P], un[:, m * P:(m + 1) * P], start=False, stop=True)
                    ins.then_inc(sem["kv"], 1)
                    if lat >= 0:
                        for hh in range(4):
                            ins = nc.tensor.matmul(K.psum[:, 2, hh * HD:(hh + 1) * HD], cd[:, lat, 1, 2 * (hh % 2) + hh // 2], un[:, hh * HD:(hh + 1) * HD], start=False, stop=(hh == 3), skip_group_check=True)
                        ins.then_inc(sem["out"], 1)

            @st.block.scalar
            def _(act):
                for i, j in enumerate(ORDER[d]):
                    act.wait_ge(sem["z"], i + 1)
                    nc.scalar.activation(zz[:], K.psum[:, 0, 0:256], ACT.Copy).then_inc(sem["zcopied"], 1)
                    act.wait_ge(sem["u"], i + 1)
                    nc.scalar.activation(un[:], K.psum[:, 1, 0:256], ACT.Copy, scale=-1.0).then_inc(sem["ucopied"], 1)
                    act.wait_ge(sem["kv"], i + 1)
                    if j >= CT:
                        act.wait_ge(sem["out"], lat_seen[i] + 1)

            @st.block.vector
            def _(dve):
                link = Chain(dve, sem["v"])
                nc.vector.memset(state[:], 0.0).then_inc(sem["state"], 1)
                for i, j in enumerate(ORDER[d]):
                    lat = j - CT
                    dve.wait_ge(sem["kv"], i + 1)
                    link(nc.vector.tensor_tensor(upd[:], K.psum[:, 3, 0:256].rearrange("p (m n) -> p m n", m=2), over_rows(K.head_ones[:], 2), ALU.mult))
                    for m in range(2):
                        ins = nc.vector.scalar_tensor_tensor(state[:, m], state[:, m], e_tot[:, m, j:j + 1], upd[:, m], ALU.mult, ALU.add)
                    ins.then_inc(sem["state"], 1)
                    if lat >= 0:
                        dve.wait_ge(sem["out"], lat_seen[i] + 1)
                        if d == 0:
                            ins = nc.vector.tensor_copy(y[:, lat], K.psum[:, 2, 0:256])
                        else:
                            ins = nc.vector.tensor_tensor(y[:, lat], K.psum[:, 2, 0:256], y[:, lat], ALU.add)
                        ins.then_inc(sem["ytaken"], 1)
                    dve.wait_ge(sem["state"], i + 2)
    ph.close()


def rwkv_scores(nc, K, d, r_, kk, kd, ak, ci, ce, at, bt, cd, spare, sb, stack):
    half = HD
    s0, s1 = (x.rearrange("p m t -> p (m t)") for x in spare)
    kb, qb = (x[:, 0:8 * P].rearrange("p (s a b t) -> p s a b t", s=2, a=2, b=2) for x in (s0, s1))
    kc, qc = (x[:, 8 * P:12 * P].rearrange("p (s a b t) -> p s a b t", s=2, a=2, b=2) for x in (s0, s1))
    ek = sb("ek", [P, 2, 2, P], stack)
    ekc = sb("ekc", [P, 2, 2, half], stack)
    early, late = (0, half) if d == 0 else (half, 0)
    border = half - 1 if d == 0 else half
    with Stage(nc, f"rq{d}", "zero", "diffed", "exped", "q", "k", "scored", "taken", "v") as st:
        sem = st.sem

        def views(j):
            t = slice(j * P, (j + 1) * P)
            ts = slice(j * P + late, j * P + late + half)
            es = slice(j * P + early, j * P + early + half)
            return t, ts, es

        @st.block.gpsimd
        def _(pool):
            nc.gpsimd.memset(at[:], 0.0).then_inc(sem["zero"], 1)
            nc.gpsimd.memset(bt[:], 0.0).then_inc(sem["zero"], 1)
            nc.gpsimd.memset(cd[:], 0.0).then_inc(sem["zero"], 1)
            for j in range(NCH):
                t, ts, es = views(j)
                s = j % 2
                pool.wait_ge(sem["exped"], j + 1)
                if j >= 2:
                    pool.wait_ge(sem["scored"], j - 1)
                nc.gpsimd.tensor_tensor(kb[:, s, 0], ak[:, :, t], ek[:, s], ALU.mult)
                nc.gpsimd.tensor_tensor(kb[:, s, 1], kd[:, :, t], ek[:, s], ALU.mult)
                nc.gpsimd.tensor_tensor(kc[:, s, 0], ak[:, :, es], ekc[:, s], ALU.mult)
                nc.gpsimd.tensor_tensor(kc[:, s, 1], kd[:, :, es], ekc[:, s], ALU.mult).then_inc(sem["k"], 1)

        @st.block.scalar
        def _(act):
            for j in range(NCH):
                s = j % 2
                act.wait_ge(sem["diffed"], j + 1)
                nc.scalar.activation(qb[:, s], qb[:, s], ACT.Exp)
                nc.scalar.activation(qc[:, s], qc[:, s], ACT.Exp)
                nc.scalar.activation(ek[:, s], ek[:, s], ACT.Exp, scale=-1.0)
                nc.scalar.activation(ekc[:, s], ekc[:, s], ACT.Exp, scale=-1.0).then_inc(sem["exped"], 1)

        @st.block.vector
        def _(dve):
            def take(j):
                dve.wait_ge(sem["scored"], j + 1)
                b = 4 * (j % 2)
                for par in range(2):
                    for kt in range(2):
                        for qt in range(2 if j >= CT else 1):
                            mask = (K.before, K.upto)[qt] if d == 0 else (K.after, K.from_)[qt]
                            to = ((at, bt)[kt][:, j, 2 * par:2 * par + 2] if qt == 0 else cd[:, j - CT, 1 - kt, 2 * par:2 * par + 2])
                            ps = K.psum[:, b + 2 * par + kt].rearrange("p (m q t) -> p m q t", m=2, q=2)[:, :, qt]
                            for p0, c0 in ((0, 0), (half, half)):
                                c = slice(0, P) if p0 == early else slice(c0, c0 + half)
                                ins = nc.vector.tensor_tensor(to[p0:p0 + half, :, c], ps[p0:p0 + half, :, c],
                                                              over_rows(mask[p0:p0 + half, c], 2), ALU.mult)
                ins.then_inc(sem["taken"], 1)

            def diff(j):
                t, ts, es = views(j)
                s = j % 2
                if j >= 2:
                    dve.wait_ge(sem["scored"], j - 1)
                    dve.wait_ge(sem["k"], j - 1)
                for m in range(2):
                    mids = ci[:, m, t].rearrange("p (h n) -> p h n", h=2)[:, :, 31:32].broadcast_to([P, 2, half])
                    edge = ci[:, m, j * P + border:j * P + border + 1]
                    for qt, x in enumerate((ce, ci)):
                        nc.vector.tensor_tensor(qb[:, s, m, qt].rearrange("p (h n) -> p h n", h=2), x[:, m, t].rearrange("p (h n) -> p h n", h=2), mids, ALU.subtract)
                        nc.vector.tensor_scalar(qc[:, s, m, qt], x[:, m, ts], edge, None, ALU.subtract)
                    nc.vector.tensor_tensor(ek[:, s, m].rearrange("p (h n) -> p h n", h=2), ci[:, m, t].rearrange("p (h n) -> p h n", h=2), mids, ALU.subtract)
                    ins = nc.vector.tensor_scalar(ekc[:, s, m], ci[:, m, es], edge, None, ALU.subtract)
                ins.then_inc(sem["diffed"], 1)

            diff(0)
            for j in range(NCH):
                t, ts, es = views(j)
                s = j % 2
                dve.wait_ge(sem["exped"], j + 1)
                for m in range(2):
                    for qt, x in enumerate((kk, r_)):
                        nc.vector.tensor_tensor(qb[:, s, m, qt], x[:, m, t], qb[:, s, m, qt], ALU.mult)
                        ins = nc.vector.tensor_tensor(qc[:, s, m, qt], x[:, m, ts], qc[:, s, m, qt], ALU.mult)
                ins.then_inc(sem["q"], 1)
                if j + 1 < NCH:
                    diff(j + 1)
                if j == 0:
                    dve.wait_ge(sem["zero"], 3)
                else:
                    take(j - 1)
            take(NCH - 1)

        @st.block.tensor
        def _(pe):
            for j in range(NCH):
                s, b = j % 2, 4 * (j % 2)
                pe.wait_ge(sem["q"], j + 1)
                pe.wait_ge(sem["k"], j + 1)
                if j >= 2:
                    pe.wait_ge(sem["taken"], j - 1)
                for par in range(2):
                    r = slice(par * HD, (par + 1) * HD)
                    for kt in range(2):
                        bank = K.psum[:, b + 2 * par + kt].rearrange("p (m q t) -> p m q t", m=2, q=2)
                        for m in range(2):
                            for h0 in (0, half):
                                hs = slice(h0, h0 + half)
                                nc.tensor.matmul(bank[hs, m, :, hs], kb[r, s, kt, m, hs], qb[r, s, m, :, hs], start=True, stop=True)
                            ins = nc.tensor.matmul(bank[early:early + half, m, :, late:late + half], kc[r, s, kt, m], qc[r, s, m], start=True, stop=True)
                ins.then_inc(sem["scored"], 1)


def router_stage(nc, K, lg, first, second, weights, scr):
    with Stage(nc, "route", "v", "x", "e") as st:
        sem = st.sem
        gl, el = lg[:, :, 0:N_GRP], lg[:, :, N_GRP:]
        gx, ind, fg = scr[:, :, 0:4], scr[:, :, 4:8], scr[:, :, 8:12]
        es, e2, f1, f2, t8 = (scr[:, :, 16 + 8 * i:24 + 8 * i] for i in range(5))
        one = [scr[:, :, 56 + i] for i in range(8)]
        gmax, gsum, mx, m1, m2, ratio, w1, w2 = one

        @st.block.vector
        def _(dve):
            link = Chain(dve, sem["v"])

            def first_of(x, top, to, n):
                link(nc.vector.tensor_tensor(to, x, over_heads(top, n), ALU.is_equal))
                link(nc.vector.tensor_tensor(to, to, over_rows(K.desc[:, 8 - n:8], TT), ALU.mult))
                link(nc.vector.tensor_reduce(mx, to, AX.X, ALU.max))
                link(nc.vector.tensor_tensor(to, to, over_heads(mx, n), ALU.is_equal))

            link(nc.vector.tensor_reduce(gmax, gl, AX.X, ALU.max))
            nc.vector.tensor_tensor(gx, gl, over_heads(gmax, 4), ALU.subtract).then_inc(sem["x"], 1)
            first_of(gl, gmax, fg, 4)
            link(nc.vector.tensor_tensor(es, el[:, :, 0:8], over_heads(fg[:, :, 0], 8), ALU.mult))
            for g in range(1, N_GRP):
                link(nc.vector.tensor_tensor(t8, el[:, :, 8 * g:8 * g + 8], over_heads(fg[:, :, g], 8), ALU.mult))
                link(nc.vector.tensor_tensor(es, es, t8, ALU.add))
            link(nc.vector.tensor_reduce(m1, es, AX.X, ALU.max))
            first_of(es, m1, f1, 8)
            link(nc.vector.scalar_tensor_tensor(e2, f1, -3e38, es, ALU.mult, ALU.add))
            link(nc.vector.tensor_reduce(m2, e2, AX.X, ALU.max))
            first_of(e2, m2, f2, 8)
            nc.vector.tensor_tensor(ratio, m2, m1, ALU.subtract).then_inc(sem["x"], 1)
            dve.wait_ge(sem["e"], 2)
            link(nc.vector.tensor_reduce(gsum, gx, AX.X, ALU.add))
            link(nc.vector.scalar_tensor_tensor(w1, ratio, 1.0, gsum, ALU.add, ALU.mult))
            link(nc.vector.reciprocal(weights[:, 0], w1))
            link(nc.vector.tensor_tensor(weights[:, 1], weights[:, 0], ratio, ALU.mult))
            for g in range(N_GRP):
                for to, f in ((first, f1), (second, f2)):
                    nc.vector.tensor_tensor(to[:, 8 * g:8 * g + 8, :].rearrange("p e t -> p t e"), f, over_heads(fg[:, :, g], 8), ALU.mult)

        @st.block.scalar
        def _(act):
            act.wait_ge(sem["x"], 1)
            nc.scalar.activation(gx, gx, ACT.Exp).then_inc(sem["e"], 1)
            act.wait_ge(sem["x"], 2)
            nc.scalar.activation(ratio, ratio, ACT.Exp).then_inc(sem["e"], 1)


SLOTS = 64
N_EXTRA = 2 * S // SLOTS
LOTS = N_EXP + N_EXTRA


def place_stage(nc, K, first, second, rank, pos, lots, n_lots, scr):
    both = scr[:, 0]
    q, r, t1 = scr[:, 1], scr[:, 2], scr[:, 3]
    cnt, more, base, t32 = (scr[:, 4, :, i] for i in range(4))
    with Stage(nc, "place", "both", "ranked", "v") as st:
        sem = st.sem

        @st.block.tensor
        def _(pe):
            pe.wait_ge(sem["both"], 1)
            for t in range(TT):
                for u in range(t + 1):
                    nc.tensor.matmul(K.psum[:, t, 0:N_EXP], (K.before if u == t else K.ones)[:], both[:, :, u], start=(u == 0), stop=(u == t))
            for u in range(TT):
                ins = nc.tensor.matmul(K.psum[:, TT, 0:N_EXP], K.ones[:], both[:, :, u], start=(u == 0), stop=(u == TT - 1))
            ins.then_inc(sem["ranked"], 1)

        @st.block.vector
        def _(dve):
            link = Chain(dve, sem["v"])
            nc.vector.tensor_tensor(both, first, second, ALU.add).then_inc(sem["both"], 1)
            dve.wait_ge(sem["ranked"], 1)
            for t in range(TT):
                link(nc.vector.tensor_copy(r[:, :, t], K.psum[:, t, 0:N_EXP]))
            link(nc.vector.tensor_copy(cnt, K.psum[:, TT, 0:N_EXP]))
            link(nc.vector.scalar_tensor_tensor(rank, r, 1.0, both, ALU.add, ALU.mult))
            link(nc.vector.tensor_scalar(rank, rank, -1.0, None, ALU.add))
            link(nc.vector.tensor_scalar(q, r, float(SLOTS), None, ALU.is_ge))
            link(nc.vector.tensor_scalar(more, cnt, float(SLOTS), None, ALU.is_gt))
            for j in range(2, S // SLOTS):
                link(nc.vector.scalar_tensor_tensor(q, r, float(SLOTS * j), q, ALU.is_ge, ALU.add))
                link(nc.vector.scalar_tensor_tensor(more, cnt, float(SLOTS * j), more, ALU.is_gt, ALU.add))
            link(nc.vector.tensor_tensor_scan(base, K.one_row, more, 0.0, ALU.mult, ALU.add))
            link(nc.vector.tensor_copy(n_lots, base[:, N_EXP - 1:N_EXP]))
            link(nc.vector.tensor_tensor(base, base, more, ALU.subtract))
            link(nc.vector.tensor_tensor(t32, base, K.count[:, 0:N_EXP], ALU.subtract))
            link(nc.vector.tensor_tensor(t1, q, over_heads(t32, TT), ALU.add))
            link(nc.vector.tensor_scalar(t1, t1, float(N_EXP - 1), float(SLOTS), ALU.add, ALU.mult))
            link(nc.vector.scalar_tensor_tensor(t1, q, 0.0, t1, ALU.is_gt, ALU.mult))
            link(nc.vector.scalar_tensor_tensor(q, q, -float(SLOTS), r, ALU.mult, ALU.add))
            link(nc.vector.tensor_tensor(t1, t1, q, ALU.add))
            link(nc.vector.tensor_scalar(t32, K.count[:, 0:N_EXP], float(SLOTS), None, ALU.mult))
            link(nc.vector.tensor_tensor(t1, t1, over_heads(t32, TT), ALU.add))
            for i, choice in enumerate((first, second)):
                link(nc.vector.tensor_tensor(q, choice, t1, ALU.mult))
                link(nc.vector.tensor_reduce(r[:, 0:1, :].rearrange("p o t -> p (o t)"), q.rearrange("p e t -> p t e"), AX.X, ALU.add))
                link(nc.vector.tensor_copy(pos[:, i], r[:, 0:1, :].rearrange("p o t -> p (o t)")))
            m = scr[:, 5:9].rearrange("p a e t -> p (a e t)").rearrange("p (x e) -> p x e", e=N_EXP)
            m2 = scr[:, 9:13].rearrange("p a e t -> p (a e t)").rearrange("p (x e) -> p x e", e=N_EXP)
            x = K.count[:, 0:N_EXTRA]
            link(nc.vector.tensor_tensor(m, over_rows(base, N_EXTRA), over_heads(x, N_EXP), ALU.is_le))
            link(nc.vector.tensor_tensor(t32, base, more, ALU.add))
            link(nc.vector.tensor_tensor(m2, over_rows(t32, N_EXTRA), over_heads(x, N_EXP), ALU.is_gt))
            link(nc.vector.tensor_tensor(m, m, m2, ALU.mult))
            link(nc.vector.tensor_tensor(m2, m, over_rows(base, N_EXTRA), ALU.mult))
            link(nc.vector.tensor_reduce(lots[:, 1], m2, AX.X, ALU.add))
            link(nc.vector.tensor_tensor(m2, m, over_rows(K.count[:, 0:N_EXP], N_EXTRA), ALU.mult))
            link(nc.vector.tensor_reduce(lots[:, 0], m2, AX.X, ALU.add))
            link(nc.vector.tensor_tensor(lots[:, 1], x, lots[:, 1], ALU.subtract))
            link(nc.vector.tensor_scalar(lots[:, 1], lots[:, 1], 1.0, None, ALU.add))


def experts(nc, K, a, x1, mod, gains):
    ph = ExitStack()

    def sb(name, shape, stack=ph, dt=F32):
        return stack.enter_context(nc.sbuf_tensor(name, shape, dt))

    h_tok = sb("m_htok", [P, TT, D])
    rank = sb("m_rank", [P, N_EXP, TT])
    weights = sb("m_weights", [P, 2, TT])
    pos = sb("m_pos", [P, 2, TT], dt=mybir.dt.uint32)
    lots, lots_i = sb("m_lots", [P, 2, N_EXTRA]), sb("m_lots_i", [P, N_EXTRA], dt=mybir.dt.int32)
    n_lots = sb("m_nlots", [P, 1], dt=mybir.dt.int32)
    result = nc.dram_tensor("expert_rows", (LOTS * SLOTS, D), F32).ap()
    with ExitStack() as p2:
        hm = sb("m_h", [P, KD, S], p2)
        norm_stage(nc, K, "n4", lambda k: x1[:, k], S, lambda k: hm[:, k], gains[:, 2], shift=mod[:, 24:32, 0], square=K.tmp)
        lg, scr = sb("m_lg", [P, TT, 36], p2), sb("m_scr", [P, TT, 64], p2)
        first, second = sb("m_first", [P, N_EXP, TT], p2), sb("m_second", [P, N_EXP, TT], p2)
        pscr = sb("m_pscr", [P, 13, N_EXP, TT], p2)
        wr, br = sb("m_wr", [P, KD, 36], p2), sb("m_br", [P, 36], p2)
        load_stage(nc, "ml", [(wr[:], a["w_router"]), (br[:], a["b_router"])])
        with Stage(nc, "mr", "done", "zero", "cleared") as st:
            @st.block.gpsimd
            def _(pool):
                nc.gpsimd.memset(h_tok[:, 0], 0.0).then_inc(st.sem["zero"], 1)

            @st.block.sync
            def _(sync):
                sync.wait_ge(st.sem["zero"], 1)
                for x in range(0, N_EXTRA * SLOTS, P):
                    sync.dma_start(result[N_EXP * SLOTS + x:N_EXP * SLOTS + x + P, :], h_tok[:, 0]).then_inc(st.sem["cleared"], 16)
                sync.wait_ge(st.sem["cleared"], 16 * (N_EXTRA * SLOTS // P))

            @st.block.tensor
            def _(pe):
                for t in range(TT):
                    for k in range(KD):
                        m = nc.tensor.matmul(K.psum[:, t, 0:36], hm[:, k, t * P:(t + 1) * P], wr[:, k], start=(k == 0), stop=(k == KD - 1))
                    m.then_inc(st.sem["done"], 1)

            @st.block.vector
            def _(dve):
                for t in range(TT):
                    dve.wait_ge(st.sem["done"], t + 1)
                    nc.vector.tensor_tensor(lg[:, t], K.psum[:, t, 0:36], br[:], ALU.add)

        turn_stage(nc, K, "mt", [hm[:, k, t * P:(t + 1) * P] for t in range(TT) for k in range(KD)],
                   lambda g, ps: nc.vector.tensor_copy(h_tok[:, g // 2, (g % 2) * 512:(g % 2 + 1) * 512], ps))
        router_stage(nc, K, lg, first[:], second[:], weights, scr)
        place_stage(nc, K, first[:], second[:], rank[:], pos, lots, n_lots[:], pscr)
        with Stage(nc, "mi") as st:
            @st.block.vector
            def _(dve):
                nc.vector.tensor_copy(lots_i[:], lots[:, 0])
    with ExitStack() as p2:
        W = ExpertBuffers(nc, p2)
        experts_stage(nc, K, a, h_tok, rank, result, W)
        further_stage(nc, K, a, h_tok, rank, lots, lots_i, n_lots, result, W)
    fetched = sb("m_fetched", [P, 2, TT, D])
    with Stage(nc, "mf", *[f"soft{i}" for i in range(2 * TT)], "v") as st:
        sem = st.sem

        @st.block.gpsimd
        def _(pool):
            for t in range(TT):
                for i in range(2):
                    pool.indirect_dma_start(fetched[:, i, t], None, result, bass.IndirectOffsetOnAxis(ap=pos[:, i, t:t + 1], axis=0)).then_inc(sem[f"soft{2 * t + i}"], 16)

        @st.block.vector
        def _(dve):
            link = Chain(dve, sem["v"])
            for t in range(TT):
                dve.wait_ge(sem[f"soft{2 * t}"], 16)
                link(nc.vector.tensor_scalar(fetched[:, 0, t], fetched[:, 0, t], weights[:, 0, t:t + 1], None, ALU.mult))
                dve.wait_ge(sem[f"soft{2 * t + 1}"], 16)
                nc.vector.scalar_tensor_tensor(fetched[:, 0, t], fetched[:, 1, t], weights[:, 1, t:t + 1], fetched[:, 0, t], ALU.mult, ALU.add)
    turn_stage(nc, K, "mo", [fetched[:, 0, t, k * P:(k + 1) * P] for k in range(KD) for t in range(TT)],
               lambda k, ps: nc.vector.scalar_tensor_tensor(x1[:, k], ps, mod[:, 40 + k, 0:1], x1[:, k], ALU.mult, ALU.add))
    ph.close()


class ExpertBuffers:

    def __init__(self, nc, stack):
        def one(name, shape):
            return stack.enter_context(nc.sbuf_tensor(f"m_{name}", shape, F32))

        def two(name, shape):
            return [one(f"{name}{i}", shape) for i in range(2)]

        self.wg, self.wu, self.wd = two("wg", [P, KD, D_EXP]), two("wu", [P, KD, D_EXP]), two("wd", [P, FT, D])
        self.sel, self.xg = one("sel", [P, TT, 2, SLOTS]), one("xg", [P, KD, 2, SLOTS])
        self.sg, self.hid = two("sg", [P, D_EXP]), one("hid", [P, D_EXP])
        self.hid_t, self.rows = one("hid_t", [P, FT, 2 * SLOTS]), one("rows", [P, D])


GATHER, UP, TURN, DOWN = 0, 2, 4, 5


def expert_weights(w, e):
    return w[bass.ds(e, 1)].rearrange("o p k n -> (o p) k n")


def lot_select(nc, K, W, s, rank_e, slots):
    return nc.vector.tensor_tensor(W.sel[:, :, s], over_heads(rank_e, SLOTS), over_rows(slots, TT), ALU.is_equal)


def lot_gather(nc, K, W, h_tok, both):
    n = 2 * SLOTS if both else SLOTS
    for k in range(KD):
        for t in range(TT):
            at = (k % 4) * P
            m = nc.tensor.matmul(K.psum[:, GATHER + k // 4, at:at + n], h_tok[:, t, k * P:(k + 1) * P],
                                 W.sel[:, t].rearrange("p s n -> p (s n)")[:, :n], start=(t == 0), stop=(t == TT - 1))
    return m


def gathered_copy(nc, K, W):
    return nc.scalar.activation(W.xg[:].rearrange("p k s n -> p (k s n)"),
                                K.psum[:, GATHER:GATHER + 2].rearrange("p b n -> p (b n)"), ACT.Copy)


def lot_up(nc, K, W, s):
    for k in range(KD):
        for i, w in enumerate((W.wg[s], W.wu[s])):
            m = nc.tensor.matmul(K.psum[i * SLOTS:(i + 1) * SLOTS, UP + s], W.xg[:, k, s], w[:, k], start=(k == 0), stop=(k == KD - 1))
    return m


def lot_gate(nc, K, W, s):
    return nc.scalar.activation(W.sg[s][SLOTS:], K.psum[0:SLOTS, UP + s], ACT.Silu)


def lot_hide(nc, K, W, s):
    return nc.vector.tensor_tensor(W.hid[s * SLOTS:(s + 1) * SLOTS], W.sg[s][SLOTS:], K.psum[SLOTS:, UP + s], ALU.mult)


def lots_turn(nc, K, W):
    for f in range(FT):
        m = nc.tensor.transpose(K.psum[:, TURN, f * P:(f + 1) * P], W.hid[:, f * P:(f + 1) * P], K.ident[:])
    return m


def lots_down(nc, K, W, members):
    for dh in range(2):
        for f in range(FT):
            for s in members:
                at = slice(s * SLOTS, (s + 1) * SLOTS)
                m = nc.tensor.matmul(K.psum[at, DOWN + dh], W.hid_t[:, f, at], W.wd[s][:, f, dh * 512:(dh + 1) * 512], start=(f == 0), stop=(f == FT - 1))
    return m


def rows_copy(nc, K, W, n):
    return nc.vector.tensor_copy(W.rows[0:n], K.psum[0:n, DOWN:DOWN + 2].rearrange("p b n -> p (b n)"))


def experts_stage(nc, K, a, h_tok, rank, result, W):
    FREE = 2
    PAIRS = N_EXP // 2
    with Stage(nc, "moe", "wg0", "wg1", "wu0", "wu1", "wd0", "wd1", "selected", "gathered", "xcopied", "upped", "gated",
               "hidden", "turned", "tcopied", "downed", "rcopied", "stored") as st:
        sem = st.sem

        @st.block.sync
        def _(sync):
            def store(i):
                sync.wait_ge(sem["rcopied"], i + 2)
                sync.dma_start(result[bass.ds(i * P, P), :], W.rows[:]).then_inc(sem["stored"], 16)

            for s in range(2):
                sync.dma_start(W.wg[s][:], a["w_gate"][s]).then_inc(sem[f"wg{s}"], 16)
                sync.dma_start(W.wu[s][:], a["w_up"][s]).then_inc(sem[f"wu{s}"], 16)
            for s in range(2):
                sync.dma_start(W.wd[s][:], a["w_down"][s]).then_inc(sem[f"wd{s}"], 16)
            with sync.Fori(0, PAIRS - 1) as i:
                for s in range(2):
                    e = i * 2 + s
                    sync.wait_ge(sem["upped"], e + (1 + FREE))
                    sync.dma_start(W.wg[s][:], expert_weights(a["w_gate"], e + 2)).then_inc(sem[f"wg{s}"], 16)
                    sync.dma_start(W.wu[s][:], expert_weights(a["w_up"], e + 2)).then_inc(sem[f"wu{s}"], 16)
                sync.wait_ge(sem["downed"], i + 2)
                for s in range(2):
                    sync.dma_start(W.wd[s][:], expert_weights(a["w_down"], i * 2 + (2 + s))).then_inc(sem[f"wd{s}"], 16)
                store(i)
            store(PAIRS - 1)
            sync.wait_ge(sem["stored"], 16 * (PAIRS + 1))

        @st.block.tensor
        def _(pe):
            def gather(i):
                pe.wait_ge(sem["selected"], i * 2 + 2)
                pe.wait_ge(sem["xcopied"], i + 1)
                lot_gather(nc, K, W, h_tok, True).then_inc(sem["gathered"], 1)

            def up(i):
                pe.wait_ge(sem["xcopied"], i + 2)
                for s in range(2):
                    pe.wait_ge(sem[f"wg{s}"], i * 16 + 16)
                    pe.wait_ge(sem[f"wu{s}"], i * 16 + 16)
                    pe.wait_ge(sem["hidden"], i * 2 + (s + 1))
                    lot_up(nc, K, W, s).then_inc(sem["upped"], 1)

            def down(i):
                pe.wait_ge(sem["hidden"], i * 2 + (2 + FREE))
                pe.wait_ge(sem["tcopied"], i + 1)
                lots_turn(nc, K, W).then_inc(sem["turned"], 1)
                pe.wait_ge(sem["wd0"], i * 16 + 16)
                pe.wait_ge(sem["wd1"], i * 16 + 16)
                pe.wait_ge(sem["tcopied"], i + 2)
                pe.wait_ge(sem["rcopied"], i + 1)
                lots_down(nc, K, W, (0, 1)).then_inc(sem["downed"], 1)

            gather(0)
            with pe.Fori(0, PAIRS - 1) as i:
                up(i)
                gather(i + 1)
                down(i)
            up(PAIRS - 1)
            down(PAIRS - 1)

        @st.block.scalar
        def _(act):
            def copy(i):
                act.wait_ge(sem["gathered"], i + 1)
                act.wait_ge(sem["upped"], i * 2 + FREE)
                gathered_copy(nc, K, W).then_inc(sem["xcopied"], 1)

            def gates(i):
                for s in range(2):
                    act.wait_ge(sem["upped"], i * 2 + (s + 1 + FREE))
                    act.wait_ge(sem["hidden"], i * 2 + (s + 1))
                    lot_gate(nc, K, W, s).then_inc(sem["gated"], 1)

            def copy_turned(i):
                act.wait_ge(sem["turned"], i + 2)
                act.wait_ge(sem["downed"], i + 1)
                nc.scalar.activation(W.hid_t[:].rearrange("p f n -> p (f n)"), K.psum[:, TURN], ACT.Copy).then_inc(sem["tcopied"], 1)

            copy(0)
            with act.Fori(0, PAIRS - 1) as i:
                gates(i)
                copy(i + 1)
                copy_turned(i)
            gates(PAIRS - 1)
            copy_turned(PAIRS - 1)

        @st.block.vector
        def _(dve):
            def select(i):
                for s in range(2):
                    lot_select(nc, K, W, s, rank[:, bass.ds(i * 2 + s, 1), :].rearrange("p o t -> p (o t)"), K.count).then_inc(sem["selected"], 1)

            def hide(i):
                for s in range(2):
                    dve.wait_ge(sem["gated"], i * 2 + (s + 1))
                    dve.wait_ge(sem["turned"], i + 1)
                    lot_hide(nc, K, W, s).then_inc(sem["hidden"], 1)

            def rows_out(i):
                dve.wait_ge(sem["downed"], i + 2)
                dve.wait_ge(sem["stored"], i * 16 + 16)
                rows_copy(nc, K, W, P).then_inc(sem["rcopied"], 1)

            for c, (n, free) in enumerate((("xcopied", 1), ("upped", FREE), ("hidden", FREE), ("turned", 1), ("tcopied", 1),
                                           ("downed", 1), ("rcopied", 1), ("stored", 16))):
                nc.vector.memset(K.stat[:, c:c + 1], 0.0).then_inc(sem[n], free)
            select(0)
            dve.wait_ge(sem["gathered"], 1)
            select(1)
            with dve.Fori(0, PAIRS - 2) as i:
                hide(i)
                dve.wait_ge(sem["gathered"], i + 2)
                select(i + 2)
                rows_out(i)
            for i in (PAIRS - 2, PAIRS - 1):
                hide(i)
                rows_out(i)


def further_stage(nc, K, a, h_tok, rank, lots, lots_i, n_lots, result, W):
    with Stage(nc, "more", "loaded", "selected", "gathered", "xcopied", "upped", "gated", "hidden", "turned", "tcopied",
               "downed", "rcopied", "stored", "over", "v") as st:
        sem = st.sem

        def turns(eng, body):
            n = eng.value_load(n_lots[0:1, 0:1], min_val=0, max_val=N_EXTRA)
            with eng.If(n > 0):
                with eng.Fori(0, n) as x:
                    body(x)

        @st.block.sync
        def _(sync):
            def body(x):
                e = sync.value_load(lots_i[0:1, bass.ds(x, 1)], min_val=0, max_val=N_EXP - 1)
                sync.dma_start(W.wg[0][:], expert_weights(a["w_gate"], e)).then_inc(sem["loaded"], 16)
                sync.dma_start(W.wu[0][:], expert_weights(a["w_up"], e)).then_inc(sem["loaded"], 16)
                sync.dma_start(W.wd[0][:], expert_weights(a["w_down"], e)).then_inc(sem["loaded"], 16)
                sync.wait_ge(sem["rcopied"], x + 1)
                sync.dma_start(result[bass.ds(x * SLOTS + N_EXP * SLOTS, SLOTS), :], W.rows[0:SLOTS]).then_inc(sem["stored"], 16)
                sync.wait_ge(sem["stored"], x * 16 + 16)
                sync.sem_inc(sem["over"], 1)

            turns(sync, body)

        @st.block.tensor
        def _(pe):
            def body(x):
                pe.wait_ge(sem["selected"], x + 1)
                lot_gather(nc, K, W, h_tok, False).then_inc(sem["gathered"], 1)
                pe.wait_ge(sem["loaded"], x * 48 + 48)
                pe.wait_ge(sem["xcopied"], x + 1)
                lot_up(nc, K, W, 0).then_inc(sem["upped"], 1)
                pe.wait_ge(sem["hidden"], x + 1)
                lots_turn(nc, K, W).then_inc(sem["turned"], 1)
                pe.wait_ge(sem["tcopied"], x + 1)
                lots_down(nc, K, W, (0,)).then_inc(sem["downed"], 1)

            turns(pe, body)

        @st.block.scalar
        def _(act):
            def body(x):
                act.wait_ge(sem["gathered"], x + 1)
                for b in range(2):
                    m = nc.scalar.activation(W.xg[:, 4 * b:4 * b + 4, 0], K.psum[:, GATHER + b].rearrange("p (k n) -> p k n", k=4)[:, :, :SLOTS], ACT.Copy)
                m.then_inc(sem["xcopied"], 1)
                act.wait_ge(sem["upped"], x + 1)
                lot_gate(nc, K, W, 0).then_inc(sem["gated"], 1)
                act.wait_ge(sem["turned"], x + 1)
                nc.scalar.activation(W.hid_t[:, :, :SLOTS], K.psum[:, TURN].rearrange("p (f n) -> p f n", f=FT)[:, :, :SLOTS], ACT.Copy).then_inc(sem["tcopied"], 1)

            turns(act, body)

        @st.block.vector
        def _(dve):
            slots, first = W.sg[1][:, :SLOTS], W.sg[1][:, SLOTS:SLOTS + 1]

            def body(x):
                e = dve.value_load(lots_i[0:1, bass.ds(x, 1)], min_val=0, max_val=N_EXP - 1)
                nc.vector.tensor_scalar(first, lots[:, 1, bass.ds(x, 1)], float(SLOTS), None, ALU.mult).then_inc(sem["v"], 1)
                dve.wait_ge(sem["v"], x * 2 + 1)
                nc.vector.tensor_scalar(slots, K.count, first, None, ALU.add).then_inc(sem["v"], 1)
                dve.wait_ge(sem["v"], x * 2 + 2)
                lot_select(nc, K, W, 0, rank[:, bass.ds(e, 1), :].rearrange("p o t -> p (o t)"), slots).then_inc(sem["selected"], 1)
                dve.wait_ge(sem["gated"], x + 1)
                lot_hide(nc, K, W, 0).then_inc(sem["hidden"], 1)
                dve.wait_ge(sem["downed"], x + 1)
                rows_copy(nc, K, W, SLOTS).then_inc(sem["rcopied"], 1)

            turns(dve, body)



def second_block(nc, K, a, x1):
    ph = ExitStack()

    def sb(name, shape, stack=ph):
        return stack.enter_context(nc.sbuf_tensor(name, shape, F32))

    vecs = sb("vecs2", [P, N_VECS2])
    K.rows2 = sb("rows2", [P, 768])
    K.reset = sb("reset", [P, T2])
    at = 0

    def take(n):
        nonlocal at
        at += n
        return vecs[:, at - n:at]

    K.cond, K.b_ada, K.norm1, K.norm2 = take(16), take(48), take(8), take(8)
    K.hlb, K.mu, K.rw, K.na_gain, K.desc, K.eps_ln = take(8), take(9), take(18), take(2), take(8), take(1)
    K.count, K.one_row = take(SLOTS), take(N_EXP)
    mod, gains = sb("mod", [P, 48, 2]), sb("gains", [P, 3, KD])
    load_stage(nc, "l2", [(vecs[:], a["vecs2"]), (K.rows2[:], a["rows2"]), (K.reset[:], a["reset"])])
    modulation_stage(nc, K, a, mod, gains)
    with ExitStack() as p1:
        mix = sb("mix", [P, KD, S], p1)
        with ExitStack() as p2:
            p_mix = sb("p_mix", [P, 9, T2], p2)
            with ExitStack() as p3:
                h2 = sb("h2", [P, KD, T2], p3)
                with ExitStack() as p4:
                    ctx = sb("ctx", [P, KD, CTX], p4)
                    load_stage(nc, "lx2", [(ctx[:], a["ctxT"])])
                    norm_stage(nc, K, "n3c", lambda k: ctx[:, k], CTX, lambda k: h2[:, k, 0:CTX], gains[:, 1], shift=mod[:, 0:8, 1], square=K.tmp)
                norm_stage(nc, K, "n3", lambda k: x1[:, k], S, lambda k: h2[:, k, CTX:], gains[:, 0], shift=mod[:, 0:8, 0], square=K.tmp)
                hgrn(nc, K, a, h2, mix)
                neighbourhood(nc, K, a, h2, mix)
                with ExitStack() as p4:
                    rings(nc, K, p4, "r", n=4)
                    px = sb("px", [P, 2, T2 + 3], p4)
                    rwkv_projections(nc, K, a, h2, p_mix, px)
            rwkv(nc, K, a, p_mix, mix)
        rings(nc, K, p1, "o2")
        out_stage(nc, K, "po2", a["wo2"], lambda k: mix[:, k], x1, mod[:, 16:24, 0])
    experts(nc, K, a, x1, mod, gains)
    ph.close()


N_VECS2 = 16 + 48 + 8 + 8 + 8 + 9 + 18 + 2 + 8 + 1 + SLOTS + N_EXP


def build(nc, a, out):
    Stage.turn = 0
    K = Kept()
    top = ExitStack()

    def sb(name, shape):
        return top.enter_context(nc.sbuf_tensor(name, shape, F32))

    K.psum = top.enter_context(nc.psum_tensor("psum", [P, 8, 512], F32))
    const = sb("const", [P, 8, P])
    K.ident, K.ones, K.head_ones, K.rot, K.upto, K.before, K.from_, K.after = (const[:, i] for i in range(8))
    K.level = sb("level", [P, 2 * LEVELS, P])
    K.tmp, K.rstd, K.stat = sb("tmp", [P, 2, S]), sb("rstd", [P, 2, S]), sb("stat", [P, 8])
    vecs = sb("vecs", [P, 2 * KD + 48 + 16 + 1])
    K.vec_norm, K.vec_fnorm = vecs[:, 0:KD], vecs[:, KD:2 * KD]
    K.conv = vecs[:, 2 * KD:2 * KD + 48].rearrange("p (t j) -> p t j", j=4)
    K.dt_bias, K.a_log = vecs[:, 2 * KD + 48:2 * KD + 56], vecs[:, 2 * KD + 56:2 * KD + 64]
    K.eps = vecs[:, 2 * KD + 64:2 * KD + 65]
    x1 = sb("x1", [P, KD, S])
    load_stage(nc, "lc", [(const[:], a["const"]), (K.level[:], a["level"]), (vecs[:], a["vecs"])])
    first_block(nc, K, a, x1)
    second_block(nc, K, a, x1)
    store_stage(nc, x1, out)
    top.close()


def store_stage(nc, x, out):
    with Stage(nc, "store", "stored") as st:
        @st.block.sync
        def _(sync):
            sync.dma_start(out, x[:]).then_inc(st.sem["stored"], 16)
            sync.wait_ge(st.sem["stored"], 16)


def feature_tiles(w):
    k, n = w.shape
    return np.ascontiguousarray(w.reshape(k // P, P, n // P, P).transpose(2, 1, 0, 3))


def blocks(w):
    k, n = w.shape
    return np.ascontiguousarray(w.reshape(k // P, P, n).transpose(1, 0, 2))


def columns(v):
    return np.ascontiguousarray(v.reshape(-1, P).T)


def rows(v):
    return np.ascontiguousarray(np.broadcast_to(v.reshape(1, -1), (P, v.size)))


def constants():
    i, j = np.meshgrid(np.arange(P), np.arange(P), indexing="ij")
    rot = np.zeros((P, P), np.float32)
    for o in range(P):
        rot[o + 32 if o % 64 < 32 else o - 32, o] = -1.0 if o % 64 < 32 else 1.0
    const = np.stack([i == j, np.ones((P, P)), i // HD == j // HD, rot, i <= j, i < j, i >= j, i > j], 1)
    low = []
    for lv in range(LEVELS):
        b = 2 << lv
        low.append((i // b == j // b) & (i % b < b // 2) & (j % b >= b // 2))
    level = np.stack(low + [m.T for m in low], 1)
    f32 = np.float32
    q, k = np.meshgrid(np.arange(P), np.arange(P), indexing="ij")
    neg = lambda ok: np.where(ok, 0.0, NEG)
    mask0 = np.concatenate([neg(k >= q), neg(k <= q)], 1)
    dil = lambda d: np.concatenate([neg((q - k) % d == 0)] * 3 + [neg(((q - k) % d == 0) & (k <= q))], 1)
    inv = (f32(10000.0) ** (-np.arange(0, HD, 2, dtype=f32) / f32(HD))).astype(f32)
    ang = (np.arange(S, dtype=f32)[:, None] * inv[None]).astype(f32)
    ang = np.tile(ang, (1, 4)).T
    out = dict(const=const, level=level, mask0=mask0, mask1=dil(4), mask2=dil(16), cos1=np.cos(ang), sin1=np.sin(ang))
    return {n: np.ascontiguousarray(v.astype(f32)) for n, v in out.items()}


def second_arrays(c, ctx, c_ctx, norm1_gain, norm2_gain, w_ada, b_ada, w_in, w_out, hgrn_lb_logits, hgrn_gn_gain,
                  rwkv_mu, rwkv_w0, rwkv_w_up, rwkv_a0, rwkv_a_up, rwkv_g_up, rwkv_kk_scale, rwkv_k_a, rwkv_r_k,
                  rwkv_ln_gain, rwkv_ln_bias, na_q_gain, na_k_gain, na_rpb, w_router_group, b_router_group,
                  w_router_expert, b_router_expert, w_exp_gate, w_exp_up, w_exp_down):
    f32 = np.float32
    out = {}
    out["ctxT"] = blocks(np.ascontiguousarray(ctx[0].T))
    parts = w_ada[0].reshape(ADA_PARTS, KD // ADA_PARTS, P, ADA_GROUPS, 4, 512).transpose(3, 0, 2, 1, 4, 5)
    out["w_ada"] = parts.reshape(ADA_GROUPS * ADA_PARTS, P, KD // ADA_PARTS, 4, 512)
    w = w_in[0]
    out["w2f"] = feature_tiles(np.concatenate([w[:, 0:768], w[:, 1280:2432], w[:, 2432:3456]], 1))
    out["w2t"] = np.stack([blocks(w[:, 768:1280]), blocks(w[:, 3456:3968])])
    out["wo2"] = feature_tiles(w_out[0])
    cond = np.stack([columns(c[0]), columns(c_ctx)], -1).reshape(P, 16)
    hlb = np.concatenate([columns(hgrn_lb_logits[0, 0]), columns(hgrn_lb_logits[1, 0]), np.zeros((P, 4), f32)], 1)
    rw = [np.zeros((P, 4), f32), columns(rwkv_kk_scale[0]), columns(rwkv_k_a[0]), columns(rwkv_r_k[0].reshape(-1)),
          columns(rwkv_w0[0, 0]), columns(rwkv_w0[0, 1]), columns(rwkv_a0[0, 0]), columns(rwkv_a0[0, 1])]
    na = [columns(np.tile(na_q_gain[0], 2)), columns(np.tile(na_k_gain[0], 2))]
    desc = rows(np.arange(8, 0, -1).astype(f32))
    out["vecs2"] = np.concatenate([cond, columns(b_ada[0]), columns(norm1_gain[0]), columns(norm2_gain[0]), hlb,
                                   columns(rwkv_mu[0]), *rw, *na, desc, np.full((P, 1), 64e-5, f32),
                                   rows(np.arange(SLOTS).astype(f32)), np.ones((P, N_EXP), f32)], 1)
    out["rows2"] = np.concatenate([rows(hgrn_gn_gain[0].reshape(-1)), rows(rwkv_ln_gain[0]), rows(rwkv_ln_bias[0])], 1)
    out["reset"] = rows((np.arange(T2) % P != 0).astype(f32))
    out["rw_up"] = np.stack([rwkv_w_up[0].reshape(P, 256), rwkv_a_up[0].reshape(P, 256), rwkv_g_up[0]], 1)
    cq, ck = np.meshgrid(np.arange(64), np.arange(64), indexing="ij")
    bias = na_rpb[0][:, :, np.clip(ck - cq + 15, 0, 30)].transpose(2, 0, 1, 3)
    out["na_table"] = np.concatenate([bias[:, :, 1:15], bias[:, :, 0:14]], 0).reshape(P, 8, 14 * 64)
    ws = np.clip(cq - 8, 0, 48)
    out["na_window"] = np.tile(np.where((ck >= ws) & (ck < ws + 16), 0.0, NEG).astype(f32), (2, 1))
    inv = (f32(10000.0) ** (-np.arange(16, dtype=f32) / f32(16))).astype(f32)
    pos = np.arange(S)
    ang = np.concatenate([(pos // 64).astype(f32)[:, None] * inv, (pos % 64).astype(f32)[:, None] * inv], -1)
    ang = np.tile(ang, (1, 4)).T
    out["cos2"], out["sin2"] = np.cos(ang).astype(f32), np.sin(ang).astype(f32)
    out["w_router"] = blocks(np.concatenate([w_router_group[0], w_router_expert[0]], 1))
    out["b_router"] = rows(np.concatenate([b_router_group[0], b_router_expert[0]]))
    out["w_gate"] = w_exp_gate[0].reshape(N_EXP, KD, P, D_EXP).transpose(0, 2, 1, 3)
    out["w_up"] = w_exp_up[0].reshape(N_EXP, KD, P, D_EXP).transpose(0, 2, 1, 3)
    out["w_down"] = w_exp_down[0].reshape(N_EXP, FT, P, D).transpose(0, 2, 1, 3)
    return out


def arrays_of(x, norm_w, w_in, conv_w, a_log, dt_bias, gdn_norm_w, w_up_a, w_up_b, w_out, final_norm_w, **r):
    w = w_in[0]
    G = 1536
    feat = [w[:, g * G:g * G + 1024] for g in range(3)] + [w[:, 4608:5120], w[:, 5120:6656], w[:, 6656:7168], w[:, 7184:9232]]
    out = constants()
    out["xT"] = blocks(np.ascontiguousarray(x[0].T))
    out["w1f"] = feature_tiles(np.concatenate(feat, 1))
    out["w1v"] = np.stack([blocks(w[:, g * G + 1024:(g + 1) * G]) for g in range(3)])
    out["w1ba"] = blocks(w[:, 7168:7184])
    out["upa"], out["upb"], out["wo1"] = feature_tiles(w_up_a[0]), feature_tiles(w_up_b[0]), feature_tiles(w_out[0])
    conv = conv_w[0].T.reshape(12, P, 4).transpose(1, 0, 2).reshape(P, 48)
    out["vecs"] = np.concatenate([columns(norm_w[0]), columns(final_norm_w), conv, rows(dt_bias[0]), rows(a_log[0]), np.full((P, 1), EPS, np.float32)], 1)
    out["gdn_gain"] = rows(np.tile(gdn_norm_w[0], 8))
    out.update(second_arrays(**{n[:-2]: v for n, v in r.items()}))
    return out


def kernel(**inputs):
    import concourse.bacc as bacc
    from concourse.bass_utils import run_bass_kernel_spmd

    nc = bacc.Bacc("TRN2", target_bir_lowering=False, num_devices=1)
    arrays = {n: np.ascontiguousarray(v) for n, v in arrays_of(**{k: np.asarray(v) for k, v in inputs.items()}).items()}
    a = {n: nc.dram_tensor("in_" + n, v.shape, mybir.dt.from_np(v.dtype), kind="ExternalInput").ap() for n, v in arrays.items()}
    out = nc.dram_tensor("out", (P, KD, S), F32, kind="ExternalOutput").ap()
    build(nc, a, out)
    r = run_bass_kernel_spmd(nc, [{"in_" + n: v for n, v in arrays.items()}], core_ids=[0])
    y = r.results[0]["out"]
    return np.ascontiguousarray(y.transpose(2, 1, 0)).reshape(1, S, D)
```
